# Optimizing a Trainium2 kernel written in Bass

```python
import jax, jax.numpy as jnp
from jax import lax
import numpy as np
import math

D_MODEL = 1024
BATCH = 1
SEQ = 512
DEPTH = 1

CONV_CH = D_MODEL // 2
CONV_WIDTH = 31
N_HEADS = 8
HEAD_DIM = 64
ATTN_WIDTH = N_HEADS * HEAD_DIM
D_FF = ((8 * D_MODEL // 3 + 255) // 256) * 256
Q_BLOCK = 128
EPS = 1e-6

COL_SIZES = (2 * CONV_CH,
             ATTN_WIDTH,
             ATTN_WIDTH,
             ATTN_WIDTH,
             N_HEADS,
             D_MODEL,
             D_MODEL)
IN_COLS = sum(COL_SIZES)
COL_SPLITS = tuple(int(s) for s in np.cumsum(COL_SIZES)[:-1])


def rmsnorm(x, g):
    xf = x.astype(jnp.float32)
    inv = lax.rsqrt(jnp.mean(xf * xf, axis=-1, keepdims=True) + EPS)
    return (xf * inv).astype(x.dtype) * g

def layernorm(x, g, b):
    xf = x.astype(jnp.float32)
    mu = jnp.mean(xf, axis=-1, keepdims=True)
    var = jnp.mean(jnp.square(xf - mu), axis=-1, keepdims=True)
    return ((xf - mu) * lax.rsqrt(var + EPS)).astype(x.dtype) * g + b

def causal_depthwise_conv(a, w, b):
    out = lax.conv_general_dilated(
        a, w[:, None, :], window_strides=(1,), padding=[(CONV_WIDTH - 1, 0)],
        dimension_numbers=("NWC", "WIO", "NWC"), feature_group_count=CONV_CH)
    return out + b

def conformer_conv_branch(a_in, w_dw, b_dw, g_ln, b_ln, w_out):
    a = a_in[..., :CONV_CH] * jax.nn.sigmoid(a_in[..., CONV_CH:])
    a = causal_depthwise_conv(a, w_dw, b_dw)
    a = jax.nn.silu(layernorm(a, g_ln, b_ln))
    return a @ w_out

def forgetting_attention(q, k, v, f_logit, b_forget, g_q, g_k):
    B, S, _ = q.shape
    nb = S // Q_BLOCK
    def heads(t, g):
        t = t.reshape(B, S, N_HEADS, HEAD_DIM)
        if g is not None:
            t = rmsnorm(t, g)
        return t.transpose(0, 2, 1, 3)
    qh, kh, vh = heads(q, g_q), heads(k, g_k), heads(v, None)
    log_f = jax.nn.log_sigmoid(f_logit.astype(jnp.float32) + b_forget.astype(jnp.float32))
    c = jnp.cumsum(log_f, axis=1).transpose(0, 2, 1)
    scale = HEAD_DIM ** -0.5
    q_blocks = qh.reshape(B, N_HEADS, nb, Q_BLOCK, HEAD_DIM).transpose(2, 0, 1, 3, 4)
    c_blocks = c.reshape(B, N_HEADS, nb, Q_BLOCK).transpose(2, 0, 1, 3)
    k_pos = jnp.arange(S)

    def one_block(args):
        qi, ci, i = args
        s = jnp.einsum("bhqd,bhkd->bhqk", qi, kh).astype(jnp.float32) * scale
        s = s + ci[..., :, None] - c[:, :, None, :]
        q_pos = i * Q_BLOCK + jnp.arange(Q_BLOCK)
        s = jnp.where(k_pos[None, :] <= q_pos[:, None], s, -jnp.inf)
        p = jax.nn.softmax(s, axis=-1).astype(vh.dtype)
        return jnp.einsum("bhqk,bhkd->bhqd", p, vh)

    out = lax.map(one_block, (q_blocks, c_blocks, jnp.arange(nb)))
    return out.transpose(1, 0, 3, 2, 4).reshape(B, S, ATTN_WIDTH)

def first_inputs(seed: int = 0) -> dict:
    key = jax.random.key(seed)
    ks = jax.random.split(key, 20)
    f32 = jnp.float32
    def nrm(k, shape, fan_in):
        return jax.random.normal(k, shape, f32) * fan_in ** -0.5
    def gain(k, shape):
        return 1.0 + 0.02 * jax.random.normal(k, shape, f32)
    return {
        "x": jax.random.normal(ks[0], (BATCH, SEQ, D_MODEL), f32),
        "g_mix": gain(ks[1], (DEPTH, D_MODEL)),
        "w_in": nrm(ks[2], (DEPTH, D_MODEL, IN_COLS), D_MODEL),
        "b_forget": jax.random.uniform(ks[3], (DEPTH, N_HEADS), f32, 2.0, 5.0),
        "w_dw": nrm(ks[4], (DEPTH, CONV_WIDTH, CONV_CH), CONV_WIDTH),
        "b_dw": 0.02 * jax.random.normal(ks[5], (DEPTH, CONV_CH), f32),
        "g_conv_ln": gain(ks[6], (DEPTH, CONV_CH)),
        "b_conv_ln": 0.02 * jax.random.normal(ks[7], (DEPTH, CONV_CH), f32),
        "w_conv_out": nrm(ks[8], (DEPTH, CONV_CH, D_MODEL), CONV_CH),
        "g_q": gain(ks[9], (DEPTH, HEAD_DIM)),
        "g_k": gain(ks[10], (DEPTH, HEAD_DIM)),
        "w_attn_out": nrm(ks[11], (DEPTH, ATTN_WIDTH, D_MODEL), ATTN_WIDTH),
        "w_out": nrm(ks[12], (DEPTH, D_MODEL, D_MODEL), D_MODEL),
        "g_ffn": gain(ks[13], (DEPTH, D_MODEL)),
        "w_ffn_in": nrm(ks[14], (DEPTH, D_MODEL, 2 * D_FF), D_MODEL),
        "w_ffn_out": nrm(ks[15], (DEPTH, D_FF, D_MODEL), D_FF),
    }

def first_block(x, g_mix, w_in, b_forget, w_dw, b_dw, g_conv_ln, b_conv_ln, w_conv_out,
              g_q, g_k, w_attn_out, w_out, g_ffn, w_ffn_in, w_ffn_out):
    for l in range(DEPTH):
        h = rmsnorm(x, g_mix[l])
        proj = h @ w_in[l]
        a_in, q, k, v, f_logit, gate_a, gate_b = jnp.split(proj, COL_SPLITS, axis=-1)
        y_conv = conformer_conv_branch(a_in, w_dw[l], b_dw[l], g_conv_ln[l],
                                       b_conv_ln[l], w_conv_out[l])
        y_attn = forgetting_attention(q, k, v, f_logit, b_forget[l], g_q[l], g_k[l]) @ w_attn_out[l]
        merged = jax.nn.sigmoid(gate_a) * y_conv + jax.nn.sigmoid(gate_b) * y_attn
        x = x + merged @ w_out[l]
        h2 = rmsnorm(x, g_ffn[l])
        gu = h2 @ w_ffn_in[l]
        x = x + (jax.nn.silu(gu[..., :D_FF]) * gu[..., D_FF:]) @ w_ffn_out[l]
    return x


CHUNK = 64
N_MEM = 256
MIX_WIDTH = D_MODEL
M_WIDTH = MIX_WIDTH // 2
M_HEADS = 4
M_HDIM = M_WIDTH // M_HEADS
M_CONV = 4
F_BIAS_LO = 3.0
F_BIAS_HI = 6.0
R_WIDTH = MIX_WIDTH - M_WIDTH
R_HDIM = 64
R_HEADS = R_WIDTH // R_HDIM
R_DECAY_LORA = 64
R_AAA_LORA = 64
R_GATE_LORA = 160
DECAY_SCALE = math.exp(-0.5)
X_HEADS = 4
X_HDIM = D_MODEL // X_HEADS
D_FF_2 = 2816
FFN_CONV = 3
NORM_EPS = 1e-6
GN_EPS = 64e-5
M_COLS = 4 * M_WIDTH + 2 * M_HEADS
R_COLS = 3 * R_WIDTH + R_DECAY_LORA + R_AAA_LORA + R_GATE_LORA
IN_COLS_2 = M_COLS + R_COLS


def rmsnorm_2(x, g, eps=NORM_EPS):
    xf = x.astype(jnp.float32)
    y = xf * lax.rsqrt(jnp.mean(xf * xf, -1, keepdims=True) + eps)
    return (y * g.astype(jnp.float32)).astype(x.dtype)

def standardize_heads(y, eps):
    yf = y.astype(jnp.float32)
    mu = jnp.mean(yf, -1, keepdims=True)
    var = jnp.mean(jnp.square(yf - mu), -1, keepdims=True)
    return (yf - mu) * lax.rsqrt(var + eps)

def causal_dwconv(x, w, b):
    width = w.shape[0]
    seq = x.shape[1]
    xp = jnp.pad(x, ((0, 0), (width - 1, 0), (0, 0)))
    y = b
    for j in range(width):
        y = y + xp[:, j:j + seq] * w[j]
    return y

def token_shift(p, mu):
    prev = jnp.pad(p, ((0, 0), (1, 0), (0, 0)))[:, :-1]
    return p + (prev - p) * mu

def mlstm_chunkwise(q, k, v, i_pre, f_pre):
    B, H, S, dh = q.shape
    nc = S // CHUNK
    f32 = jnp.float32
    q = q.astype(f32).reshape(B, H, nc, CHUNK, dh) * (dh ** -0.5)
    k = k.astype(f32).reshape(B, H, nc, CHUNK, dh)
    v = v.astype(f32).reshape(B, H, nc, CHUNK, dh)
    logi = i_pre.astype(f32).reshape(B, H, nc, CHUNK)
    logf = jax.nn.log_sigmoid(f_pre.astype(f32)).reshape(B, H, nc, CHUNK)
    b = jnp.cumsum(logf, -1)
    g = b[..., -1]
    a = g[..., None] - b + logi
    m_loc = jnp.max(a, -1)
    wa = jnp.exp(a - m_loc[..., None])
    c_loc = jnp.einsum('bhclv,bhclk->bhcvk', v * wa[..., None], k)
    n_loc = jnp.einsum('bhcl,bhclk->bhck', wa, k)

    def step(carry, inp):
        c, n, m = carry
        g_c, m_l, c_l, n_l = inp
        m_new = jnp.maximum(g_c + m, m_l)
        s_old = jnp.exp(g_c + m - m_new)
        s_loc = jnp.exp(m_l - m_new)
        c_new = s_old[..., None, None] * c + s_loc[..., None, None] * c_l
        n_new = s_old[..., None] * n + s_loc[..., None] * n_l
        return (c_new, n_new, m_new), (c, n, m)

    init = (jnp.zeros((B, H, dh, dh), f32), jnp.zeros((B, H, dh), f32), jnp.zeros((B, H), f32))
    xs = (jnp.moveaxis(g, 2, 0), jnp.moveaxis(m_loc, 2, 0),
          jnp.moveaxis(c_loc, 2, 0), jnp.moveaxis(n_loc, 2, 0))
    _, (c_prev, n_prev, m_prev) = lax.scan(step, init, xs)
    c_prev = jnp.moveaxis(c_prev, 0, 2)
    n_prev = jnp.moveaxis(n_prev, 0, 2)
    m_prev = jnp.moveaxis(m_prev, 0, 2)

    inter = b + m_prev[..., None]
    causal = jnp.tril(jnp.ones((CHUNK, CHUNK), dtype=bool))
    d = jnp.where(causal, b[..., :, None] - b[..., None, :] + logi[..., None, :], -jnp.inf)
    m_t = jnp.maximum(inter, jnp.max(d, -1))
    s_int = jnp.exp(inter - m_t)
    p = jnp.exp(d - m_t[..., None]) * jnp.einsum('bhctd,bhcsd->bhcts', q, k)
    num = (s_int[..., None] * jnp.einsum('bhcvk,bhctk->bhctv', c_prev, q)
           + jnp.einsum('bhcts,bhcsv->bhctv', p, v))
    den = s_int * jnp.einsum('bhck,bhctk->bhct', n_prev, q) + jnp.sum(p, -1)
    h = num / jnp.maximum(jnp.abs(den), jnp.exp(-m_t))[..., None]
    return h.reshape(B, H, S, dh)

def rwkv7_scan(r, w, k, v, kk, a):
    B, S, H, N = r.shape

    def step(state, inp):
        r_t, w_t, k_t, v_t, kk_t, a_t = inp
        sk = jnp.einsum('bhvk,bhk->bhv', state, kk_t)
        state = (state * w_t[:, :, None, :]
                 - sk[..., None] * (kk_t * a_t)[:, :, None, :]
                 + v_t[..., None] * k_t[:, :, None, :])
        y = jnp.einsum('bhvk,bhk->bhv', state, r_t)
        return state, y

    xs = (jnp.moveaxis(r, 1, 0), jnp.moveaxis(w, 1, 0), jnp.moveaxis(k, 1, 0),
          jnp.moveaxis(v, 1, 0), jnp.moveaxis(kk, 1, 0), jnp.moveaxis(a, 1, 0))
    _, y = lax.scan(step, jnp.zeros((B, H, N, N), jnp.float32), xs)
    return jnp.moveaxis(y, 0, 1)

def hybrid_token_mixer(h, w_in, m_conv_w, m_conv_b, m_gate_b, m_norm_g, r_mu, r_w0, r_w_up,
                       r_a0, r_a_up, r_g_up, r_kk, r_ka, r_rk, r_gn_g, r_gn_b, w_out):
    B, S, _ = h.shape
    f32 = jnp.float32
    p = h @ w_in
    pm, pr = p[..., :M_COLS], p[..., M_COLS:]

    qk = jax.nn.silu(causal_dwconv(pm[..., :2 * M_WIDTH], m_conv_w, m_conv_b))
    q, k = qk[..., :M_WIDTH], qk[..., M_WIDTH:]
    v = pm[..., 2 * M_WIDTH:3 * M_WIDTH]
    o = pm[..., 3 * M_WIDTH:4 * M_WIDTH]
    gates = pm[..., 4 * M_WIDTH:] + m_gate_b
    i_pre, f_pre = gates[..., :M_HEADS], gates[..., M_HEADS:]

    def to_heads(t):
        return t.reshape(B, S, M_HEADS, M_HDIM).transpose(0, 2, 1, 3)

    hm = mlstm_chunkwise(to_heads(q), to_heads(k), to_heads(v),
                         i_pre.transpose(0, 2, 1), f_pre.transpose(0, 2, 1))
    hm = standardize_heads(hm.transpose(0, 2, 1, 3), NORM_EPS).reshape(B, S, M_WIDTH)
    y_m = (jax.nn.sigmoid(o.astype(f32)) * hm * m_norm_g.astype(f32)).astype(h.dtype)

    pr = token_shift(pr, r_mu)
    rr = pr[..., :R_WIDTH]
    kr = pr[..., R_WIDTH:2 * R_WIDTH]
    vr = pr[..., 2 * R_WIDTH:3 * R_WIDTH]
    off = 3 * R_WIDTH
    wd = pr[..., off:off + R_DECAY_LORA]
    off = off + R_DECAY_LORA
    ad = pr[..., off:off + R_AAA_LORA]
    off = off + R_AAA_LORA
    gd = pr[..., off:off + R_GATE_LORA]
    w = jnp.exp(-DECAY_SCALE * jax.nn.sigmoid((r_w0 + jnp.tanh(wd) @ r_w_up).astype(f32)))
    a = jax.nn.sigmoid((r_a0 + ad @ r_a_up).astype(f32))
    g = jax.nn.sigmoid(gd) @ r_g_up

    def rh(t):
        return t.astype(f32).reshape(B, S, R_HEADS, R_HDIM)

    kk = rh(kr * r_kk)
    kk = kk / jnp.maximum(jnp.sqrt(jnp.sum(kk * kk, -1, keepdims=True)), 1e-12)
    kr = kr.astype(f32) * (1.0 + (a - 1.0) * r_ka.astype(f32))
    rr, kr, vr, w, a = rh(rr), rh(kr), rh(vr), rh(w), rh(a)
    yr = rwkv7_scan(rr, w, kr, vr, kk, a)
    yr = (standardize_heads(yr, GN_EPS) * r_gn_g.astype(f32).reshape(R_HEADS, R_HDIM)
          + r_gn_b.astype(f32).reshape(R_HEADS, R_HDIM))
    yr = yr + jnp.sum(rr * kr * r_rk.astype(f32), -1, keepdims=True) * vr
    y_r = (yr.reshape(B, S, R_WIDTH) * g.astype(f32)).astype(h.dtype)

    return jnp.concatenate([y_m, y_r], -1) @ w_out

def mem_cross_attn(h, memn, w_q, w_kv, w_o):
    B, S, _ = h.shape
    M = memn.shape[1]
    q = (h @ w_q).reshape(B, S, X_HEADS, X_HDIM)
    kv = memn @ w_kv
    k = kv[..., :D_MODEL].reshape(B, M, X_HEADS, X_HDIM)
    v = kv[..., D_MODEL:].reshape(B, M, X_HEADS, X_HDIM)
    s = jnp.einsum('bshd,bmhd->bhsm', q, k).astype(jnp.float32) * (X_HDIM ** -0.5)
    pr = jax.nn.softmax(s, -1).astype(v.dtype)
    o = jnp.einsum('bhsm,bmhd->bshd', pr, v).reshape(B, S, D_MODEL)
    return o @ w_o

def conv_glu_ffn(h, w_up, conv_w, conv_b, w_down):
    u = h @ w_up
    gate, val = u[..., :D_FF_2], u[..., D_FF_2:]
    gate = causal_dwconv(gate, conv_w, conv_b)
    return (jax.nn.silu(gate) * val) @ w_down

def second_inputs(seed: int = 0) -> dict:
    key = jax.random.key(seed)
    ks = iter(jax.random.split(key, 48))
    L = DEPTH

    def nrm(shape, scale):
        return jax.random.normal(next(ks), shape, jnp.float32) * scale

    def gain(shape):
        return 1.0 + nrm(shape, 0.02)

    def unif(shape, lo, hi):
        return jax.random.uniform(next(ks), shape, jnp.float32, minval=lo, maxval=hi)

    x = nrm((BATCH, SEQ, D_MODEL), 1.0)
    mem = nrm((BATCH, N_MEM, D_MODEL), 1.0)
    f_bias = jnp.linspace(F_BIAS_LO, F_BIAS_HI, M_HEADS, dtype=jnp.float32)
    m_gate_b = jnp.concatenate([nrm((L, M_HEADS), 0.1), f_bias + nrm((L, M_HEADS), 0.1)], -1)
    return {
        'x': x,
        'mem': mem,
        'norm_mix': gain((L, D_MODEL)),
        'w_in': nrm((L, D_MODEL, IN_COLS_2), D_MODEL ** -0.5),
        'm_conv_w': nrm((L, M_CONV, 2 * M_WIDTH), M_CONV ** -0.5),
        'm_conv_b': nrm((L, 2 * M_WIDTH), 0.02),
        'm_gate_b': m_gate_b,
        'm_norm_g': gain((L, M_WIDTH)),
        'r_mu': unif((L, R_COLS), 0.0, 1.0),
        'r_w0': unif((L, R_WIDTH), -2.0, 2.0),
        'r_w_up': nrm((L, R_DECAY_LORA, R_WIDTH), R_DECAY_LORA ** -0.5),
        'r_a0': nrm((L, R_WIDTH), 0.1),
        'r_a_up': nrm((L, R_AAA_LORA, R_WIDTH), R_AAA_LORA ** -0.5),
        'r_g_up': nrm((L, R_GATE_LORA, R_WIDTH), R_GATE_LORA ** -0.5),
        'r_kk': 0.85 + nrm((L, R_WIDTH), 0.05),
        'r_ka': 1.0 + nrm((L, R_WIDTH), 0.05),
        'r_rk': nrm((L, R_HEADS, R_HDIM), 0.1),
        'r_gn_g': gain((L, R_WIDTH)),
        'r_gn_b': nrm((L, R_WIDTH), 0.02),
        'w_out': nrm((L, MIX_WIDTH, D_MODEL), MIX_WIDTH ** -0.5),
        'norm_x': gain((L, D_MODEL)),
        'norm_mem': gain((L, D_MODEL)),
        'x_wq': nrm((L, D_MODEL, D_MODEL), D_MODEL ** -0.5),
        'x_wkv': nrm((L, D_MODEL, 2 * D_MODEL), D_MODEL ** -0.5),
        'x_wo': nrm((L, D_MODEL, D_MODEL), D_MODEL ** -0.5),
        'norm_ffn': gain((L, D_MODEL)),
        'f_up': nrm((L, D_MODEL, 2 * D_FF_2), D_MODEL ** -0.5),
        'f_conv_w': nrm((L, FFN_CONV, D_FF_2), FFN_CONV ** -0.5),
        'f_conv_b': nrm((L, D_FF_2), 0.02),
        'f_down': nrm((L, D_FF_2, D_MODEL), D_FF_2 ** -0.5),
        'norm_final': gain((D_MODEL,)),
    }

def second_block(x, mem, norm_mix, w_in, m_conv_w, m_conv_b, m_gate_b, m_norm_g, r_mu, r_w0,
              r_w_up, r_a0, r_a_up, r_g_up, r_kk, r_ka, r_rk, r_gn_g, r_gn_b, w_out,
              norm_x, norm_mem, x_wq, x_wkv, x_wo, norm_ffn, f_up, f_conv_w, f_conv_b,
              f_down, norm_final):
    for l in range(DEPTH):
        h = rmsnorm_2(x, norm_mix[l])
        x = x + hybrid_token_mixer(h, w_in[l], m_conv_w[l], m_conv_b[l], m_gate_b[l],
                                   m_norm_g[l], r_mu[l], r_w0[l], r_w_up[l], r_a0[l],
                                   r_a_up[l], r_g_up[l], r_kk[l], r_ka[l], r_rk[l],
                                   r_gn_g[l], r_gn_b[l], w_out[l])
        h = rmsnorm_2(x, norm_x[l])
        memn = rmsnorm_2(mem, norm_mem[l])
        x = x + mem_cross_attn(h, memn, x_wq[l], x_wkv[l], x_wo[l])
        h = rmsnorm_2(x, norm_ffn[l])
        x = x + conv_glu_ffn(h, f_up[l], f_conv_w[l], f_conv_b[l], f_down[l])
    return rmsnorm_2(x, norm_final)


def setup_inputs(seed=0):
    out = dict(first_inputs(seed))
    for name, value in second_inputs(seed + 1).items():
        if name != "x":
            out[name + "_2"] = value
    return out


def reference(
    x, g_mix, w_in, b_forget, w_dw, b_dw, g_conv_ln, b_conv_ln, w_conv_out, g_q, g_k,
    w_attn_out, w_out, g_ffn, w_ffn_in, w_ffn_out, mem_2, norm_mix_2, w_in_2, m_conv_w_2,
    m_conv_b_2, m_gate_b_2, m_norm_g_2, r_mu_2, r_w0_2, r_w_up_2, r_a0_2, r_a_up_2, r_g_up_2,
    r_kk_2, r_ka_2, r_rk_2, r_gn_g_2, r_gn_b_2, w_out_2, norm_x_2, norm_mem_2, x_wq_2, x_wkv_2,
    x_wo_2, norm_ffn_2, f_up_2, f_conv_w_2, f_conv_b_2, f_down_2, norm_final_2,
):
    x = first_block(
        x, g_mix, w_in, b_forget, w_dw, b_dw, g_conv_ln, b_conv_ln, w_conv_out, g_q, g_k,
        w_attn_out, w_out, g_ffn, w_ffn_in, w_ffn_out,
    )
    return second_block(
        x, mem_2, norm_mix_2, w_in_2, m_conv_w_2, m_conv_b_2, m_gate_b_2, m_norm_g_2, r_mu_2,
        r_w0_2, r_w_up_2, r_a0_2, r_a_up_2, r_g_up_2, r_kk_2, r_ka_2, r_rk_2, r_gn_g_2,
        r_gn_b_2, w_out_2, norm_x_2, norm_mem_2, x_wq_2, x_wkv_2, x_wo_2, norm_ffn_2, f_up_2,
        f_conv_w_2, f_conv_b_2, f_down_2, norm_final_2,
    )


_drawn_inputs = setup_inputs


def setup_inputs(seed=0):
    import zlib

    import numpy as np

    out = dict(_drawn_inputs(seed))
    spreads = {}
    factors = {'g_mix': 4.263,
     'g_conv_ln': 4.723,
     'b_conv_ln': 5.06,
     'g_q': 8.0,
     'g_k': 8.0,
     'g_ffn': 3.035,
     'norm_mix_2': 3.423,
     'm_conv_b_2': 23.921,
     'm_norm_g_2': 8.0,
     'r_a0_2': 3.574,
     'r_kk_2': 22.079,
     'r_ka_2': 2.732,
     'r_gn_g_2': 8.0,
     'r_gn_b_2': 8.0,
     'norm_x_2': 8.0,
     'norm_mem_2': 8.0,
     'norm_ffn_2': 12.408,
     'f_conv_b_2': 33.767,
     'norm_final_2': 22.146}
    for name, (base, spread) in spreads.items():
        noise = np.random.default_rng([zlib.crc32(name.encode()), seed]).standard_normal(out[name].shape)
        drawn = base * np.exp(spread * noise) if base else spread * noise
        out[name] = __import__('jax').numpy.asarray(drawn.astype(out[name].dtype))
    for name, factor in factors.items():
        out[name] = (out[name] * factor).astype(out[name].dtype)
    return out
```

```python
from contextlib import ExitStack
import math

import concourse.bass as bass
from concourse import mybir

F32 = mybir.dt.float32
F32R = mybir.dt.float32r
ALU = mybir.AluOpType
ACT = mybir.ActivationFunctionType
AX = mybir.AxisListType

P = 128
D = 1024
T = 512
KT = D // P
TB = T // P
EPS = 1e-6
CONV_CH, CONV_W = 512, 31
HEADS, HD = 8, 64
FF = 2816
FT = FF // P
RING = 4
UK, UN = 4, 256
PAD = CONV_W - 1
MASKED = -1.0e30

MH = 4
M_COLS = 4 * 512 + 2 * MH
R_COLS = 3 * 512 + 64 + 64 + 160
DECAY = math.exp(-0.5)
GN_EPS = 64e-5
CH = 64
NC = T // CH
M_TOK = 256
XH, XHD = 4, 256

TABLE_A = [("g_mix", 8), ("b_dw", 4), ("g_conv_ln", 4), ("b_conv_ln", 4), ("g_ffn", 8), ("norm_mix_2", 8),
           ("m_conv_b_2", 8), ("m_norm_g_2", 4), ("r_mu_2", 14), ("r_mu_tail", 1), ("r_w0_2", 4), ("r_a0_2", 4), ("r_kk_2", 4),
           ("r_ka_2", 4), ("r_rk_2", 4), ("r_gn_g_2", 4), ("r_gn_b_2", 4), ("norm_x_2", 8), ("norm_mem_2", 8),
           ("norm_ffn_2", 8), ("norm_final_2", 8), ("g_q", 1), ("g_k", 1)]
TABLE_B = [("w_dw", 124)]
TABLE_C = [("m_conv_w_2", 32), ("f_conv_w_2", 66), ("f_conv_b_2", 22)]


class Steps:

    def __init__(self, eng, sem):
        self.eng, self.sem, self.n = eng, sem, 0

    def __call__(self, ins):
        ins.then_inc(self.sem, 1)
        self.n = self.n + 1
        self.eng.wait_ge(self.sem, self.n)

    def enter(self, i, per):
        self.start, self.per = self.n, per
        self.n = i * per + self.start

    def leave(self, times):
        self.n = self.start + times * self.per


def build(nc, d, out, stop=None):
    ctx = ExitStack()
    with ctx:
        def sb(name, shape, dt=F32, where=ctx):
            return where.enter_context(nc.sbuf_tensor(name, shape, dt))

        def sem(name):
            return ctx.enter_context(nc.semaphore(name))

        w_raw = sb("w_raw", [P, RING, UK, UN])
        w_hi = sb("w_hi", [P, RING, UK, UN], F32R)
        w_lo = sb("w_lo", [P, RING, UK, UN], F32R)
        xT = sb("xT", [P, KT, T])
        ident = sb("ident", [P, P])
        ones = sb("ones", [P, P])
        halves = sb("halves", [P, P])
        upto = sb("upto", [P, P])
        before = sb("before", [P, P])
        later_key = sb("later_key", [P, P])
        tab = sb("tab", [P, 3, P])
        rms_inv = sb("rms_inv", [P, T])
        q_gain = sb("q_gain", [P, 1])
        eps_col = sb("eps_col", [P, 2])
        f_bias = sb("f_bias", [P, 2, 8])

        with ExitStack() as ph:
            raw_rows = sb("raw_rows", [P, 3, P], where=ph)
            x_rows = sb("x_rows", [P, TB, D], where=ph)
        act_hi = sb("act_hi", [P, KT, T], F32R)
        act_lo = sb("act_lo", [P, KT, T], F32R)
        tmp = sb("tmp", [P, 2, T])
        with ExitStack() as ph:
            glu = sb("glu", [P, 4, T + PAD], where=ph)
            conv = sb("conv", [P, 4, T], where=ph)
            qkv = sb("qkv", [P, 12, T], where=ph)
            v_tok = sb("v_tok", [P, TB, 512], where=ph)
            sig = sb("sig", [P, 16, T], where=ph)
            br_hi = sb("br_hi", [P, 4, T], F32R, where=ph)
            br_lo = sb("br_lo", [P, 4, T], F32R, where=ph)
            wf_raw = sb("wf_raw", [P, KT, 8], where=ph)
            wf_hi = sb("wf_hi", [P, KT, 8], F32R, where=ph)
            wf_lo = sb("wf_lo", [P, KT, 8], F32R, where=ph)
            lf = sb("lf", [P, 4, TB, 8], where=ph)
            csum = sb("csum", [P, TB, 8], where=ph)
            neg_lf_wide = sb("neg_lf_wide", [P, TB, P], where=ph)
            stat = sb("stat", [P, 3, 4], where=ph)
            diag = sb("diag", [P, 2, P], where=ph)
        probsT = glu
        scores_sb = conv
        with ExitStack() as ph:
            hid_hi = sb("hid_hi", [P, FT, T], F32R, where=ph)
            hid_lo = sb("hid_lo", [P, FT, T], F32R, where=ph)
            ffn_tmp = sb("ffn_tmp", [P, 4, T], where=ph)
        with ExitStack() as ph:
            mix = sb("mix", [P, 25632], where=ph)
            wg_hi = sb("wg_hi", [P, KT, 8], F32R, where=ph)
            wg_lo = sb("wg_lo", [P, KT, 8], F32R, where=ph)

        def part(at, *dims, rows=slice(0, P)):
            size = math.prod(dims)
            names = "abcde"[:len(dims)]
            flat = mix[rows, at:at + size]
            if len(dims) == 1:
                return flat
            return flat.rearrange(f"p ({' '.join(names)}) -> p {' '.join(names)}", **dict(zip(names, dims)))

        rkv = part(0, 12, T)
        lora = part(6144, 3, T)
        sw = part(7680, 4, T)
        rate = part(9728, 4, T)
        ptT = part(7680, 4, T)
        decay_e = part(9728, 2, T)
        rows = part(10752, 2, T, rows=slice(0, MH))
        m_qk = part(11776, 8, T)
        m_v = part(15872, 4, T)
        m_h = part(15872, 4, T)
        m_vtok = part(17920, TB, 512)
        m_o = part(19968, 4, T)
        pad = part(22016, 2, T + 4)
        up_w = part(23048, 512)
        wg_raw = part(23560, KT, 8)
        mg = part(23624, 5, TB, 8)
        RK = part(11776, 2, NC, 2, CH)
        BKt = part(13824, 2, NC, P)
        BK = part(15872, 2, NC, 2, CH)
        UV = part(17920, NC, 4, CH)
        G = part(19968, 2, 2, NC, P)
        work = part(19968, 8, T)
        half64 = slice(0, CH)
        X = [part(15872 + 1024 * p, 16, CH, rows=half64) for p in range(2)]
        XT = [part(17920 + 1024 * p, 16, CH, rows=half64) for p in range(2)]
        y_sb = part(11776, 2, T)
        end_decay = part(24064, NC, 4)
        g_mask = part(24096, P)
        level = part(24224, 6, CH, rows=half64)
        up_g = part(24608, 2, 512)
        state = part(6144, 2, 4, CH)

        with ExitStack() as ph:
            q_x = sb("q_x", [P, KT, T], where=ph)
            mem_rows = sb("mem_rows", [P, 2, D], where=ph)
            memT = sb("memT", [P, KT, M_TOK], where=ph)
            mem_hi = sb("mem_hi", [P, KT, M_TOK], F32R, where=ph)
            mem_lo = sb("mem_lo", [P, KT, M_TOK], F32R, where=ph)
            kv_x = sb("kv_x", [P, 16, M_TOK], where=ph)
            v_xtok = sb("v_xtok", [P, 2, D], where=ph)
            x_s = sb("x_s", [P, 2, M_TOK], where=ph)
            x_pT = sb("x_pT", [P, 2, 2, T], where=ph)
            x_stat = sb("x_stat", [P, 3, 4], where=ph)
            x_diag = sb("x_diag", [P, 2, P], where=ph)
        with ExitStack() as ph:
            hid2_hi = sb("hid2_hi", [P, FT, T], F32R, where=ph)
            hid2_lo = sb("hid2_lo", [P, FT, T], F32R, where=ph)
            gpad = sb("gpad", [P, 2, T + 2], where=ph)
            gconv = sb("gconv", [P, 2, T], where=ph)
        with ExitStack() as ph:
            out_rows = sb("out_rows", [P, TB, D], where=ph)
            y_fin = sb("y_fin", [P, KT, T], where=ph)

        lin = ctx.enter_context(nc.psum_tensor("lin", [P, 4, T], F32))
        aux = ctx.enter_context(nc.psum_tensor("aux", [P, 4, T], F32))

        class Layer:
            units, slabs = 0, 0

            def __init__(self, weight, kt, bodies, column, slabs=2, skip=None):
                self.skip = skip
                self.w = weight.rearrange("o (k p) n -> p (o k) n", p=P)
                self.bodies, self.column, self.slabs = bodies, column, slabs
                self.parts = [(k, min(UK, kt - k)) for k in range(0, kt, UK)]
                self.kt, self.per = kt, slabs * len(self.parts)
                self.u0, self.s0 = Layer.units, Layer.slabs
                Layer.units += bodies * self.per
                Layer.slabs += bodies * slabs
                assert self.per % RING == 0

            def unit(self, k):
                return (k // len(self.parts), *self.parts[k % len(self.parts)])

        Layer.slabs = 0
        whole = lambda i, s: i * 2 * UN + s * UN
        glu_l = Layer(d["w_in"], KT, 2, lambda i, s: i * UN + s * CONV_CH)
        qkv_l = Layer(d["w_in"], KT, 3, lambda i, s: 2 * CONV_CH + whole(i, s))
        gate_l = Layer(d["w_in"], KT, 4, lambda i, s: 2 * CONV_CH + 3 * HEADS * HD + HEADS + whole(i, s))
        conv_out_l = Layer(d["w_conv_out"], 4, 1, lambda i, s: s * UN, slabs=4)
        attn_out_l = Layer(d["w_attn_out"], 4, 1, lambda i, s: s * UN, slabs=4)
        out_l = Layer(d["w_out"], KT, 2, whole)
        ffn_in_l = Layer(d["w_ffn_in"], KT, 11, lambda i, s: i * UN + s * FF)
        ffn_out_l = Layer(d["w_ffn_out"], FT, 2, whole)
        layers = [glu_l, qkv_l, gate_l, conv_out_l, attn_out_l, out_l, ffn_in_l, ffn_out_l]
        if stop != "ffn":
            m_qk_l = Layer(d["w_in_2"], KT, 2, whole)
            m_vo_l = Layer(d["w_in_2"], KT, 2, lambda i, s: 1024 + whole(i, s))
            rkv_l = Layer(d["w_in_2"], KT, 3, lambda i, s: M_COLS + whole(i, s))
            lora_l = Layer(d["w_in_2"], KT, 1, lambda i, s: M_COLS + 3 * 512 + 32 * s, skip=(1, 0))
            mix_out_l = Layer(d["w_out_2"], KT, 2, whole)
            layers += [m_qk_l, m_vo_l, rkv_l, lora_l, mix_out_l]
        if stop not in ("ffn", "mix2"):
            xkv_l = Layer(d["x_wkv_2"], KT, 4, whole)
            xq_l = Layer(d["x_wq_2"], KT, 2, whole)
            xo_l = Layer(d["x_wo_2"], KT, 2, whole)
            up_l = Layer(d["f_up_2"], KT, 11, lambda i, s: i * UN + s * FF)
            down_l = Layer(d["f_down_2"], FT, 2, whole)
            layers += [xkv_l, xq_l, xo_l, up_l, down_l]

        w_arrived = [sem(f"w_arrived{s}") for s in range(RING)]
        w_high = sem("w_high")
        w_low = sem("w_low")
        w_used = sem("w_used")
        bank_free = [sem("bank_free0"), sem("bank_free1")]
        consts = sem("consts")
        rows_zero = sem("rows_zero")
        rows_in = sem("rows_in")
        x_in = sem("x_in")
        small_in = sem("small_in")
        tab_turned = sem("tab_turned")
        tab_ready = sem("tab_ready")
        x_turned = sem("x_turned")
        x_done = sem("x_done")
        n_square, n_added, n_summed, n_root, n_scaled, n_high, act_ready = (
            sem(n) for n in ("n_square", "n_added", "n_summed", "n_root", "n_scaled", "n_high", "act_ready"))
        dve_step, act_step, pool_step = (sem(n) for n in ("dve_step", "act_step", "pool_step"))

        conv_step = sem("conv_step")
        f_split, f_low, f_logits, f_biased, f_ln, f_ready, f_sum, c_ready = (
            sem(n) for n in ("f_split", "f_low", "f_logits", "f_biased", "f_ln", "f_ready", "f_sum", "c_ready"))
        ln_mean, ln_centered, ln_square, ln_var, ln_root, ln_scaled, ln_silu, br_ready = (
            sem(n) for n in ("ln_mean", "ln_centered", "ln_square", "ln_var", "ln_root", "ln_scaled", "ln_silu",
                             "br_ready"))
        qk_square, qk_summed, qk_root, qk_done = (sem(n) for n in ("qk_square", "qk_summed", "qk_root", "qk_done"))
        v_turned, v_done = sem("v_turned"), sem("v_done")
        lf_wide, cb_ready, cb_copied = sem("lf_wide"), sem("cb_ready"), sem("cb_copied")
        s_ready, s_taken, s_max, s_exp, s_diag, p_turned, p_copied, o_ready, o_high, o_done = (
            sem(n) for n in ("s_ready", "s_taken", "s_max", "s_exp", "s_diag", "p_turned", "p_copied", "o_ready",
                             "o_high", "o_done"))
        m_ready, hid_ready = sem("m_ready"), sem("hid_ready")
        stored = sem("stored")

        place, row = {}, 0
        for t, table in enumerate((TABLE_A, TABLE_B, TABLE_C)):
            row = 0
            for name, n in table:
                place[name] = (t, row, n)
                row += n
            assert row <= P

        def col(name, j):
            t, r, _ = place[name]
            return tab[:, t, r + j:r + j + 1]

        def stream(eng, layer):
            with eng.Fori(0, layer.bodies) as i:
                at = [eng.snap(layer.column(i, s)) for s in range(layer.slabs)]
                for k in range(layer.per):
                    s, r, n = layer.unit(k)
                    eng.wait_ge(w_low, i * layer.per + (layer.u0 + k + 1))
                    eng.dma_start(w_raw[:, k % RING, 0:n, :], layer.w[:, r:r + n, bass.ds(at[s], UN)])\
                       .then_inc(w_arrived[k % RING], 16)

        def round_unit(layer, i, k):
            if k >= layer.per:
                follow = layers.index(layer) + 1
                last = layer.bodies - 1
                if type(i) is int and i == last:
                    if follow == len(layers):
                        return
                    layer, i, k = layers[follow], 0, k - layer.per
                else:
                    i, k = i + 1, k - layer.per
            n = layer.unit(k)[2]
            s = k % RING
            nc.scalar.wait_ge(w_arrived[s], i * (16 * (layer.per // RING)) + 16 * (layer.u0 // RING + k // RING + 1))
            nc.scalar.wait_ge(w_used, i * layer.per + (layer.u0 + k + 1))
            nc.scalar.activation(w_hi[:, s, 0:n, :], w_raw[:, s, 0:n, :], ACT.Copy).then_inc(w_high, 1)

        AHEAD = 2

        def act_linear(layer, take=None, unroll=False):
            def body(i):
                for k in range(layer.per):
                    round_unit(layer, i, k + AHEAD)
                    if (k + 1) % len(layer.parts) == 0 and take:
                        take(i, k // len(layer.parts))
            if unroll:
                for i in range(layer.bodies - 1):
                    body(i)
            elif layer.bodies > 1:
                with nc.scalar.Fori(0, layer.bodies - 1) as i:
                    body(i)
            body(layer.bodies - 1)

        def slab_ready(eng, layer, i, s):
            eng.wait_ge(w_used, i * layer.per + (RING + layer.u0 + (s + 1) * len(layer.parts)))

        def tile_taken(eng, layer, i, s, t):
            eng.wait_ge(bank_free[s % 2], i * layer.slabs + (layer.s0 + 2 * (s // 2) + 3 + t))

        def every_tile_taken(eng, layer):
            for s in (layer.slabs - 2, layer.slabs - 1):
                tile_taken(eng, layer, layer.bodies - 1, s, 1)

        def pool_linear(layer):
            with nc.gpsimd.Fori(0, layer.bodies) as i:
                for k in range(layer.per):
                    n, s = layer.unit(k)[2], k % RING
                    nc.gpsimd.wait_ge(w_high, i * layer.per + (layer.u0 + k + 1))
                    nc.gpsimd.tensor_tensor(w_lo[:, s, 0:n, :], w_raw[:, s, 0:n, :], w_hi[:, s, 0:n, :].bitcast(F32),
                                            ALU.subtract).then_inc(w_low, 1)

        def pe_linear(layer, hi, lo):
            with nc.tensor.Fori(0, layer.bodies) as i:
                for k in range(layer.per):
                    s, r, n = layer.unit(k)
                    if r == 0:
                        nc.tensor.wait_ge(bank_free[s % 2], i * layer.slabs + (layer.s0 + 2 * (s // 2) + 2))
                    nc.tensor.wait_ge(w_low, i * layer.per + (RING + layer.u0 + k + 1))
                    for t in range(2):
                        if (s, t) == layer.skip:
                            continue
                        bank = lin[:, 2 * (s % 2) + t, 0:hi.shape[2]]
                        for j in range(n):
                            c = slice(t * P, t * P + P)
                            high, low = w_hi[:, k % RING, j, c], w_lo[:, k % RING, j, c]
                            nc.tensor.matmul(bank, high, hi[:, r + j, :], start=(r + j == 0), stop=False)
                            nc.tensor.matmul(bank, high, lo[:, r + j, :], start=False, stop=False)
                            last = nc.tensor.matmul(bank, low, hi[:, r + j, :], start=False,
                                                    stop=(r + j == layer.kt - 1))
                    last.then_inc(w_used, 1)

        def add_to_residual(layer):
            for i in range(2):
                for s in range(2):
                    slab_ready(nc.vector, layer, i, s)
                    for t in range(2):
                        x = xT[:, 4 * i + 2 * s + t, :]
                        nc.vector.tensor_tensor(x, lin[:, 2 * s + t, :], x, ALU.add)\
                          .then_inc(bank_free[s], 1)

        def act_norm_square(m, after):
            for k in range(KT):
                if after is None:
                    nc.scalar.wait_ge(x_done, k + 1)
                else:
                    tile_taken(nc.scalar, after, k // 4, k // 2 % 2, k % 2)
                if k >= 2:
                    nc.scalar.wait_ge(n_added, KT * m + k - 1)
                nc.scalar.activation(tmp[:, k % 2, :], xT[:, k, :], ACT.Square).then_inc(n_square, 1)

        def act_norm_root(m):
            nc.scalar.wait_ge(n_summed, m + 1)
            nc.scalar.activation(tmp[:, 0, :], aux[:, 0, :], ACT.Sqrt, scale=1.0 / D, bias=eps_col[:, 0:1])\
              .then_inc(n_root, 1)

        def act_norm_high(m):
            for k in range(KT):
                nc.scalar.wait_ge(n_scaled, KT * m + k + 1)
                nc.scalar.activation(act_hi[:, k, :], tmp[:, k % 2, :], ACT.Copy).then_inc(n_high, 1)

        def act_norm(m, after):
            act_norm_square(m, after)
            act_norm_root(m)
            act_norm_high(m)

        def pe_norm(m):
            nc.tensor.wait_ge(n_added, KT * (m + 1))
            nc.tensor.matmul(aux[:, 0, :], ones[:, :], rms_inv[:, :], start=True, stop=True).then_inc(n_summed, 1)

        def dve_norm(m, gain, step, to=None):
            v = nc.vector
            for k in range(KT):
                v.wait_ge(n_square, KT * m + k + 1)
                if k == 0:
                    v.tensor_copy(rms_inv[:, :], tmp[:, 0, :]).then_inc(n_added, 1)
                else:
                    v.wait_ge(n_added, KT * m + k)
                    v.tensor_tensor(rms_inv[:, :], rms_inv[:, :], tmp[:, k % 2, :], ALU.add).then_inc(n_added, 1)
            v.wait_ge(n_root, m + 1)
            step(v.reciprocal(rms_inv[:, :], tmp[:, 0, :]))

            if to is not None:
                for k in range(KT):
                    v.scalar_tensor_tensor(to[:, k, :], xT[:, k, :], col(gain, k), rms_inv[:, :], ALU.mult, ALU.mult)\
                     .then_inc(y_ready, 1)
                return

            def low(k):
                v.wait_ge(n_high, KT * m + k + 1)
                v.tensor_tensor(act_lo[:, k, :], tmp[:, k % 2, :], act_hi[:, k, :].bitcast(F32), ALU.subtract)\
                 .then_inc(act_ready, 1)
            for k in range(KT):
                if k >= 2:
                    low(k - 2)
                    v.wait_ge(act_ready, KT * m + k - 1)
                v.scalar_tensor_tensor(tmp[:, k % 2, :], xT[:, k, :], col(gain, k), rms_inv[:, :], ALU.mult, ALU.mult)\
                 .then_inc(n_scaled, 1)
            low(KT - 2)
            low(KT - 1)

        (m_conv, m_silu, r_shift, u_ready, u_turned, rows_ready, m_e, m_s, m_exp, m_p, m_pv, m_den, m_head) = (sem(n) for n in (
            "m_conv", "m_silu", "r_shift", "u_ready",
            "u_turned", "rows_ready", "m_e", "m_s", "m_exp", "m_p", "m_pv", "m_den", "m_head"))
        (gn_mean, gn_centered, gn_square, gn_var, gn_root, gn_done) = (sem(n) for n in (
            "gn_mean", "gn_centered", "gn_square", "gn_var", "gn_root", "gn_done"))
        (two_in, masks_ready, r_act, r_pre, r_sig, kk_square, kk_sum, kk_floor, kk_root, z_cum, z_exp, packed, bonus_in,
         bonus_sum, bonus_done) = (sem(n) for n in (
            "two_in", "masks_ready", "r_act", "r_pre", "r_sig", "kk_square", "kk_sum", "kk_floor", "kk_root", "z_cum",
            "z_exp", "packed", "bonus_in", "bonus_sum", "bonus_done"))
        (bt_turned, bt_done, g_built, g_masked, xt_first, x_first, x_copied, iv_y, iv_t, iv_x, iv_xd, iv_xt, iv_xtd, uv_zero,
         uv_turned, uv_done) = (sem(n) for n in (
            "bt_turned", "bt_done", "g_built", "g_masked", "xt_first", "x_first", "x_copied", "iv_y", "iv_t", "iv_x",
            "iv_xd", "iv_xt", "iv_xtd", "uv_zero", "uv_turned", "uv_done"))
        (w_sum, w_taken, u_sum, u_taken, s_sum, s_new, y_sum, y_copied, y_mean, y_centered, y_square, y_var, y_root,
         y_gate, mix_ready) = (sem(n) for n in (
            "w_sum", "w_taken", "u_sum", "u_taken", "s_sum", "s_new", "y_sum", "y_copied", "y_mean", "y_centered",
            "y_square", "y_var", "y_root", "y_gate", "mix_ready"))

        def act_mix(act, step):
            act_norm_square(2, ffn_out_l)
            act.dma_start(wg_raw, m_qk_l.w[:, :, 4 * 512:M_COLS]).then_inc(two_in, 16)
            act.dma_start(up_w[0:64, :], d["r_w_up_2"][0]).then_inc(two_in, 16)
            act.dma_start(up_w[64:128, :], d["r_a_up_2"][0]).then_inc(two_in, 16)
            act.dma_start(up_g[:, 0, :], d["r_g_up_2"][0, 0:P, :]).then_inc(two_in, 16)
            act.wait_ge(masks_ready, 1)
            act.dma_start(up_g[96:128, 1, :], d["r_g_up_2"][0, P:160, :]).then_inc(two_in, 16)
            act_norm_root(2)
            act_norm_high(2)
            act.wait_ge(two_in, 80)
            step(act.activation(pad[:, :, 0:3], ident[:, 0:6].rearrange("p (a b) -> p a b", a=2), ACT.Copy, scale=0.0))

            def silu(q):
                act.wait_ge(m_conv, q + 1)
                act.activation(m_qk[:, q, :], m_qk[:, q, :], ACT.Silu).then_inc(m_silu, 1)

            def take_qk(i, s):
                slab_ready(act, m_qk_l, i, s)
                for t in range(2):
                    q = 4 * i + 2 * s + t
                    if q >= 2:
                        act.wait_ge(m_conv, q - 1)
                    act.activation(pad[:, t, 3:3 + T], lin[:, 2 * s + t, :], ACT.Copy).then_inc(bank_free[s], 1)
                    if q >= 2:
                        silu(q - 2)

            def take_vo(i, s):
                slab_ready(act, m_vo_l, i, s)
                for t in range(2):
                    q = 2 * s + t
                    if i == 0:
                        act.activation(m_v[:, q, :], lin[:, q, :], ACT.Copy).then_inc(bank_free[s], 1)
                    else:
                        act.activation(m_o[:, q, :], lin[:, q, :], ACT.Sigmoid).then_inc(bank_free[s], 1)

            def take_shift(layer, i, s, t, q):
                if q >= 2:
                    act.wait_ge(r_shift, q - 1)
                act.activation(pad[:, q % 2, 3:3 + T], lin[:, 2 * s + t, :], ACT.Copy).then_inc(bank_free[s], 1)

            def take_rkv(i, s):
                slab_ready(act, rkv_l, i, s)
                for t in range(2):
                    take_shift(rkv_l, i, s, t, 4 * i + 2 * s + t)

            def take_lora(i, s):
                slab_ready(act, lora_l, i, s)
                if s == 1:
                    act.sem_inc(bank_free[1], 1)
                for t in range(s, 2):
                    take_shift(lora_l, i, s, t, 12 + s + t)

            act_linear(m_qk_l, take_qk, unroll=True)
            silu(6)
            silu(7)
            act.activation(wg_hi[:, :, :], wg_raw, ACT.Copy).then_inc(f_split, 1)
            act_linear(m_vo_l, take_vo, unroll=True)
            act_linear(rkv_l, take_rkv, unroll=True)
            act_linear(lora_l, take_lora, unroll=True)

            act.wait_ge(f_biased, 2)
            step(act.activation(mg[:, 1, :, :], mg[:, 0, :, :], ACT.Abs))
            step(act.activation(mg[:, 2, :, :], mg[:, 1, :, :], ACT.Exp, scale=-1.0))
            act.activation(mg[:, 1, :, :], mg[:, 2, :, :], ACT.Ln, bias=ones[:, 0:1]).then_inc(f_ln, 1)
            for b in range(TB):
                act.wait_ge(v_turned, TB + b + 1)
                act.activation(m_vtok[:, b, :], aux[:, 2 + b % 2, :], ACT.Copy).then_inc(v_done, 1)
            for h in range(MH):
                for j in range(TB):
                    n, w = TB * h + j, T - j * P
                    act.wait_ge(m_e, 5 * h + j + 1)
                    if n >= 2:
                        act.wait_ge(m_p, n - 1)
                    act.activation(decay_e[:, n % 2, 0:w], aux[:, 2 + (5 * h + j) % 2, 0:w], ACT.Exp,
                                   bias=mg[:, 4, j, h:h + 1]).then_inc(m_exp, 1)
                act.wait_ge(m_e, 5 * h + 5)
                if h:
                    act.wait_ge(m_head, h)
                act.activation(tmp[:, 0, :], aux[:, 2 + (5 * h + 4) % 2, :], ACT.Exp).then_inc(m_exp, 1)
                act.wait_ge(m_pv, TB * h + TB)
                act.activation(tmp[:, 1, :], lin[:, 2 * (h % 2) + 1, :], ACT.Abs).then_inc(m_den, 1)
            for h in range(MH):
                act.wait_ge(gn_centered, h + 1)
                if h:
                    act.wait_ge(gn_done, h)
                act.activation(tmp[:, 0, :], m_h[:, h, :], ACT.Square).then_inc(gn_square, 1)
                act.wait_ge(gn_var, h + 1)
                act.activation(tmp[:, 1, :], aux[:, 2 + h % 2, :], ACT.Sqrt, scale=1.0 / P, bias=eps_col[:, 0:1])\
                   .then_inc(gn_root, 1)

            act.activation(lora[0:64, 0, :], lora[0:64, 0, :], ACT.Tanh).then_inc(r_act, 1)
            act.activation(lora[:, 1:3, :], lora[:, 1:3, :], ACT.Sigmoid).then_inc(r_act, 1)
            for q in range(8):
                act.wait_ge(r_pre, q + 1)
                act.activation((sw, rate)[q % 2][:, q // 2, :], aux[:, q % 4, :], ACT.Sigmoid,
                               bias=col(("r_w0_2", "r_a0_2")[q % 2], q // 2)).then_inc(r_sig, 1)
            for half in range(2):
                for pl in range(2):
                    p = 2 * half + pl
                    if p:
                        act.wait_ge(packed, p)
                    if p == 2:
                        act.wait_ge(mix_ready, 6)
                    act.activation(tmp[:, 0, :], rkv[:, 4 + p, :], ACT.Square, scale=col("r_kk_2", p))\
                       .then_inc(kk_square, 1)
                    act.wait_ge(kk_floor, p + 1)
                    act.activation(tmp[:, 0, :], tmp[:, 0, :], ACT.Sqrt).then_inc(kk_root, 1)
                    act.wait_ge(z_cum, p + 1)
                    act.activation(work[:, 2, :], work[:, 0, :], ACT.Exp, scale=-DECAY).then_inc(z_exp, 1)
                    act.activation(work[:, 3, :], work[:, 0, :], ACT.Exp, scale=DECAY).then_inc(z_exp, 1)
                    act.activation(work[:, 1, :], work[:, 1, :], ACT.Exp, scale=-DECAY).then_inc(z_exp, 1)
                for pl in range(2):
                    for b in range(2):
                        act.wait_ge(bt_turned, 4 * half + 2 * pl + b + 1)
                        act.activation(BKt[:, pl, 4 * b:4 * b + 4, :],
                                       aux[:, 2 * (pl % 2) + b, :].rearrange("p (c n) -> p c n", n=P), ACT.Copy)\
                           .then_inc(bt_done, 1)
                for pl in range(2):
                    act.wait_ge(x_first, 2 * half + pl + 1)
                    act.activation(X[pl], (aux, lin)[pl][half64, 2:4, :].rearrange("p a (u n) -> p (a u) n", n=CH),
                                   ACT.Copy).then_inc(x_copied, 1)
                for pl in range(2):
                    for b in range(2):
                        n = 4 * half + 2 * pl + b
                        act.wait_ge(uv_turned, n + 1)
                        act.activation(UV[64:128, 4 * b:4 * b + 4, 2 * pl:2 * pl + 2, :],
                                       aux[64:128, 2 * pl + b, :].rearrange("p (c g n) -> p c g n", c=4, g=2), ACT.Copy)\
                           .then_inc(uv_done, 1)
                for c in range(NC):
                    n = NC * half + c
                    act.wait_ge(u_sum, n + 1)
                    act.activation(UV[0:64, c, :, :], aux[0:64, 1, 0:256].rearrange("p (g n) -> p g n", n=CH), ACT.Copy)\
                       .then_inc(u_taken, 1)
                for pl in range(2):
                    p = 2 * half + pl
                    act.wait_ge(y_sum, NC * (half + 1))
                    act.activation(y_sb[:, pl, :], lin[:, pl, :], ACT.Copy).then_inc(y_copied, 1)
                for pl in range(2):
                    p = 2 * half + pl
                    act.wait_ge(y_centered, p + 1)
                    act.activation(tmp[:, pl, :], y_sb[:, pl, :], ACT.Square).then_inc(y_square, 1)
                    act.wait_ge(y_var, p + 1)
                    act.activation(tmp[:, pl, :], aux[:, 1, :], ACT.Sqrt, scale=1.0 / CH, bias=eps_col[:, 1:2])\
                       .then_inc(y_root, 1)
            if stop:
                act_linear(mix_out_l)
                return
            act_mem_load(act)

            def root(i, s):
                if (i, s) == (0, 1):
                    act.wait_ge(mem_summed, 1)
                    act.activation(tmp[:, 1, 0:M_TOK], aux[:, 2, 0:M_TOK], ACT.Sqrt, scale=1.0 / D, bias=eps_col[:, 0:1])\
                       .then_inc(mem_root, 1)
            act_linear(mix_out_l, root, unroll=True)

        def pe_mix(pe):
            pe_norm(2)
            pe.wait_ge(act_ready, 3 * KT)
            pe_linear(m_qk_l, act_hi, act_lo)
            pe_linear(m_vo_l, act_hi, act_lo)
            pe_linear(rkv_l, act_hi, act_lo)
            pe_linear(lora_l, act_hi, act_lo)
            pe.wait_ge(f_low, 2)
            for b in range(TB):
                blk, to = slice(b * P, (b + 1) * P), aux[:, 1, 8 * b:8 * b + 8]
                for k in range(KT):
                    pe.matmul(to, act_hi[:, k, blk], wg_hi[:, k, :], start=(k == 0), stop=False)
                    pe.matmul(to, act_hi[:, k, blk], wg_lo[:, k, :], start=False, stop=False)
                    last = pe.matmul(to, act_lo[:, k, blk], wg_hi[:, k, :], start=False, stop=(k == KT - 1))
            last.then_inc(f_logits, 1)
            for b in range(TB):
                if b >= 2:
                    pe.wait_ge(v_done, TB + b - 1)
                for t in range(4):
                    last = pe.transpose(aux[:, 2 + b % 2, t * P:(t + 1) * P], m_v[:, t, b * P:(b + 1) * P], ident[:, :])
                last.then_inc(v_turned, 1)
            pe.wait_ge(f_ready, 2)
            for b in range(TB):
                for a in range(b + 1):
                    last = pe.matmul(aux[:, 0, 8 * b:8 * b + 8], upto[:, :] if a == b else ones[:, :], mg[:, 3, a, :],
                                     start=(a == 0), stop=(a == b))
            last.then_inc(f_sum, 1)
            pe.wait_ge(v_done, TB + TB)
            pe.wait_ge(u_ready, 2)
            for kind in range(2):
                for b in range(TB):
                    last = pe.transpose(aux[0:MH, 2 + kind, b * P:(b + 1) * P], mg[:, 4, b, MH * kind:MH * kind + MH],
                                        ident[:, :])
            last.then_inc(u_turned, 1)
            pe.wait_ge(rows_ready, 1)
            pe.wait_ge(m_silu, 8)
            every_tile_taken(pe, lora_l)

            def spread(e, row, w):
                if e >= 2:
                    pe.wait_ge(m_exp, e - 1)
                return pe.matmul(aux[:, 2 + e % 2, 0:w], ident[0:MH, e // 5:e // 5 + 1].broadcast_to([MH, P]), rows[:, row, T - w:T], start=True,
                                 stop=(row == 0))

            def weigh(n):
                h, j = n // TB, n % TB
                pe.wait_ge(m_p, n + 1)
                if j == 0 and h >= 2:
                    pe.wait_ge(m_head, h - 1)
                to = lin[:, 2 * (h % 2), j * P:T]
                pe.matmul(to, m_vtok[:, j, h * P:(h + 1) * P], ptT[:, n % 4, 0:T - j * P], start=(j == 0),
                          stop=(j == TB - 1))
                to = lin[:, 2 * (h % 2) + 1, j * P:T]
                pe.matmul(to, ones[:, :], ptT[:, n % 4, 0:T - j * P], start=(j == 0), stop=(j == TB - 1))\
                  .then_inc(m_pv, 1)

            for n in range(MH * TB):
                h, j = n // TB, n % TB
                w = T - j * P
                spread(5 * h + j, 1, w)
                pe.matmul(aux[:, 2 + (5 * h + j) % 2, 0:P], later_key[:, :], ident[:, :], start=False, stop=True)\
                  .then_inc(m_e, 1)
                if n >= 2:
                    pe.wait_ge(m_p, n - 1)
                pe.matmul(aux[:, n % 2, 0:w], m_qk[:, 4 + h, j * P:(j + 1) * P], m_qk[:, h, j * P:T], start=True,
                          stop=True).then_inc(m_s, 1)
                if n:
                    weigh(n - 1)
                if j == TB - 1:
                    spread(5 * h + 4, 0, T).then_inc(m_e, 1)
            weigh(MH * TB - 1)
            for h in range(MH):
                pe.wait_ge(m_head, MH)
                if h >= 2:
                    pe.wait_ge(gn_centered, h - 1)
                pe.matmul(aux[:, h % 2, :], ones[:, :], m_h[:, h, :], start=True, stop=True).then_inc(gn_mean, 1)
            for h in range(MH):
                pe.wait_ge(gn_square, h + 1)
                pe.matmul(aux[:, 2 + h % 2, :], ones[:, :], tmp[:, 0, :], start=True, stop=True).then_inc(gn_var, 1)

            pe.wait_ge(gn_root, MH)
            pe.wait_ge(r_act, 2)
            for q in range(8):
                rws = slice(64 * (q % 2), 64 * (q % 2) + 64)
                if q >= 4:
                    pe.wait_ge(r_sig, q - 3)
                pe.matmul(aux[:, q % 4, :], up_w[rws, q // 2 * P:(q // 2 + 1) * P], lora[rws, 0, :], start=True,
                          stop=True).then_inc(r_pre, 1)
            pe.wait_ge(r_sig, 8)
            for half in range(2):
                for pl in range(2):
                    p = 2 * half + pl
                    pe.wait_ge(kk_square, p + 1)
                    pe.matmul(aux[:, 0, :], halves[:, :], tmp[:, 0, :], start=True, stop=True).then_inc(kk_sum, 1)
                    pe.wait_ge(bonus_in, p + 1)
                    pe.matmul(aux[:, 1, :], halves[:, :], tmp[:, 1, :], start=True, stop=True).then_inc(bonus_sum, 1)
                for pl in range(2):
                    pe.wait_ge(bonus_done, 2 * half + 2)
                    for b in range(2):
                        for c in range(4):
                            last = pe.transpose(aux[:, 2 * pl + b, c * P:(c + 1) * P],
                                                BK[:, pl, 4 * b + c, :, :].rearrange("p a b -> p (a b)"), ident[:, :])
                        last.then_inc(bt_turned, 1)
                for pl in range(2):
                    if pl:
                        pe.wait_ge(g_masked, 4 * (2 * half + 1))
                    for hh in range(2):
                        rws = slice(64 * hh, 64 * hh + 64)
                        for b in range(2):
                            for c in range(4):
                                last = pe.matmul(lin[:, 2 * hh + b, c * P:(c + 1) * P],
                                                 BK[rws, pl, 4 * b + c, :, :].rearrange("p a b -> p (a b)"),
                                                 RK[rws, pl, 4 * b + c, :, :].rearrange("p a b -> p (a b)"),
                                                 start=True, stop=True)
                            last.then_inc(g_built, 1)
                bank = (aux, lin)
                pe.wait_ge(bt_done, 4 * (half + 1))

                def units(pl, first, lhs, rhs):
                    for u in range(16):
                        last = pe.matmul(bank[pl][half64, first + u // 8, u % 8 * CH:(u % 8 + 1) * CH], lhs(u), rhs(u),
                                         start=True, stop=True)
                    return last

                for pl in range(2):
                    pe.wait_ge(xt_first, 2 * half + pl + 1)
                    units(pl, 2, lambda u: XT[pl][:, u, :], lambda u: ident[half64, 0:CH]).then_inc(x_first, 1)
                for m in range(5):
                    for pl in range(2):
                        n = (5 * half + m) * 2 + pl
                        if m == 0:
                            pe.wait_ge(x_copied, 2 * half + pl + 1)
                        else:
                            pe.wait_ge(iv_xd, (4 * half + m - 1) * 2 + pl + 1)
                            pe.wait_ge(iv_xtd, n - 1)
                        units(pl, 0, lambda u: G[half64, pl, u // NC, u % NC, CH:2 * CH], lambda u: X[pl][:, u, :])\
                            .then_inc(iv_y, 1)
                    for pl in range(2):
                        n = (5 * half + m) * 2 + pl
                        pe.wait_ge(iv_t, n + 1)
                        if m < 4:
                            units(pl, 2, lambda u: XT[pl][:, u, :], lambda u: T1(half, pl)[:, u, :]).then_inc(iv_x, 1)
                        units(pl, 0, lambda u: T1(half, pl)[:, u, :], lambda u: XT[pl][:, u, :]).then_inc(iv_xt, 1)
                pe.wait_ge(iv_xtd, 10 * (half + 1))
                for pl in range(2):
                    for b in range(2):
                        for c in range(4):
                            at = (8 + 2 * half + pl) * T + (4 * b + c) * CH - CH
                            last = pe.transpose(aux[:, 2 * pl + b, c * P:(c + 1) * P], mix[:, at:at + P], ident[:, :])
                        last.then_inc(uv_turned, 1)
                pe.wait_ge(uv_zero, half + 1)
                pe.wait_ge(uv_done, 4 * (half + 1))
                for c in range(NC):
                    n = NC * half + c
                    s_now = state[:, c % 2, :, :]
                    if c:
                        pe.wait_ge(s_new, (NC + 1) * half + c + 1)
                    else:
                        pe.wait_ge(s_new, (NC + 1) * half + 1)
                    for g in range(4):
                        pl, hh = g // 2, g % 2
                        to = aux[half64, 0, g * CH:(g + 1) * CH]
                        pe.matmul(to, RK[:, pl, c, 1, :], s_now[:, g, :], start=True, stop=False)
                        last = pe.matmul(to, G[:, pl, hh, c, CH:2 * CH], UV[:, c, g, :], start=False, stop=True)
                    last.then_inc(w_sum, 1)
                    pe.wait_ge(w_taken, n + 1)
                    for g in range(4):
                        pl, hh = g // 2, g % 2
                        last = pe.matmul(aux[half64, 1, g * CH:(g + 1) * CH], G[half64, pl, hh, c, CH:2 * CH],
                                         w_sb(half)[:, g, :], start=True, stop=True)
                    last.then_inc(u_sum, 1)
                    pe.wait_ge(u_taken, n + 1)
                    for g in range(4):
                        last = pe.matmul(aux[:, 2, g * CH:(g + 1) * CH], BKt[:, g // 2, c, :], UV[:, c, g, :],
                                         start=True, stop=True)
                    last.then_inc(s_sum, 1)
                    for g in range(4):
                        pl, hh = g // 2, g % 2
                        to = lin[64 * hh:64 * hh + 64, pl, c * CH:(c + 1) * CH]
                        pe.matmul(to, s_now[:, g, :], RK[:, pl, c, 0, :], start=True, stop=False)
                        last = pe.matmul(to, UV[:, c, g, :], G[:, pl, hh, c, 0:CH], start=False, stop=True)
                    last.then_inc(y_sum, 1)
                pe.wait_ge(s_new, (NC + 1) * (half + 1))
                for pl in range(2):
                    p = 2 * half + pl
                    pe.wait_ge(y_copied, p + 1)
                    if pl:
                        pe.wait_ge(y_centered, p)
                    pe.matmul(aux[:, 0, :], halves[:, :], y_sb[:, pl, :], start=True, stop=True).then_inc(y_mean, 1)
                for pl in range(2):
                    p = 2 * half + pl
                    pe.wait_ge(y_square, p + 1)
                    if pl:
                        pe.wait_ge(y_root, p)
                    pe.matmul(aux[:, 1, :], halves[:, :], tmp[:, pl, :], start=True, stop=True).then_inc(y_var, 1)
                    pe.matmul(aux[:, 2 + pl, :], up_g[:, 0, p * P:(p + 1) * P], lora[:, 1, :], start=True, stop=False)
                    pe.matmul(aux[:, 2 + pl, :], up_g[:, 1, p * P:(p + 1) * P], lora[:, 2, :], start=False, stop=True)\
                      .then_inc(y_gate, 1)
            pe.wait_ge(mix_ready, KT)
            if not stop:
                pe_mem(pe)
            pe_linear(mix_out_l, act_hi, act_lo)

        def pool_masks(pool, step):
            every_tile_taken(pool, ffn_out_l)
            step(pool.memset(up_g[:, 1, :], 0.0))
            pool.memset(eps_col[:, 1:2], GN_EPS)
            for r in (0, 64):
                rws = slice(r, r + 64)
                pool.tensor_copy(g_mask[rws, 0:CH], upto[rws, r:r + CH])
                step(pool.tensor_copy(g_mask[rws, CH:2 * CH], before[rws, r:r + CH]))
            for m in range(6):
                b = 1 << m
                lev = level[:, m, :]
                step(pool.memset(lev, 0.0))
                v = lev.rearrange("p (g w) -> p g w", w=2 * b)
                cols = v[:, :, b:2 * b] if m == 0 else v[:, :, 0:b]
                step(pool.memset(cols, 1.0))
                first = 0 if m == 0 else b
                n = CH // (2 * b)
                step(pool.affine_select(out=cols, in_=cols, compare_op=ALU.is_ge, fill=0.0, base=-first,
                                        pattern=[[-2 * b, n], [0, b]], channel_multiplier=1))
                ins = pool.affine_select(out=cols, in_=cols, compare_op=ALU.is_ge, fill=0.0, base=first + b - 1,
                                         pattern=[[2 * b, n], [0, b]], channel_multiplier=-1)
                step(ins)
            pool.nop().then_inc(masks_ready, 1)

        def T1(half, pl):
            return part((7680, 9728)[pl] + 1024 * half, 16, CH, rows=half64)

        def w_sb(half):
            return part(7680 + 1024 * half, 4, CH, rows=half64)

        def dve_mix(dve, step):
            dve_norm(2, "norm_mix_2", step)
            for q in range(8):
                slab_ready(dve, m_qk_l, q // 4, q // 2 % 2)
                tile_taken(dve, m_qk_l, q // 4, q // 2 % 2, q % 2)
                for j in range(4):
                    tap = tab[:, 2, 8 * j + q:8 * j + q + 1]
                    if j == 0:
                        step(dve.tensor_scalar(m_qk[:, q, :], pad[:, q % 2, 0:T], tap, col("m_conv_b_2", q), ALU.mult,
                                               ALU.add))
                    else:
                        ins = dve.scalar_tensor_tensor(m_qk[:, q, :], pad[:, q % 2, j:j + T], tap, m_qk[:, q, :],
                                                       ALU.mult, ALU.add)
                        if j < 3:
                            step(ins)
                ins.then_inc(m_conv, 1)
            for q in range(15):
                layer, i, s, t = (rkv_l, q // 4, q // 2 % 2, q % 2) if q < 12 else (lora_l, 0, (q - 12) // 2,
                                                                                   (q - 12 + 1) // 2)
                slab_ready(dve, layer, i, s)
                tile_taken(dve, layer, i, s, t)
                to = rkv[:, q, :] if q < 12 else lora[:, q - 12, :]
                mu = col("r_mu_2", q) if q < 14 else col("r_mu_tail", 0)
                step(dve.tensor_tensor(tmp[:, q % 2, :], pad[:, q % 2, 2:2 + T], pad[:, q % 2, 3:3 + T], ALU.subtract))
                dve.scalar_tensor_tensor(to, tmp[:, q % 2, :], mu, pad[:, q % 2, 3:3 + T], ALU.mult, ALU.add)\
                   .then_inc(r_shift, 1)
                if q == 0:
                    dve.wait_ge(f_split, 2)
                    dve.tensor_tensor(wg_lo[:, :, :], wg_raw, wg_hi[:, :, :].bitcast(F32), ALU.subtract)\
                       .then_inc(f_low, 1)
            dve.wait_ge(f_logits, 2)
            dve.tensor_tensor(mg[:, 0, :, :], aux[:, 1, 0:32].rearrange("p (b h) -> p b h", h=8),
                              f_bias[:, 1:2, :].broadcast_to([P, TB, 8]), ALU.add).then_inc(f_biased, 1)
            dve.wait_ge(f_ln, 2)
            dve.scalar_tensor_tensor(mg[:, 3, :, :], mg[:, 0, :, :], 0.0, mg[:, 1, :, :], ALU.min, ALU.subtract)\
               .then_inc(f_ready, 1)
            dve.wait_ge(f_sum, 2)
            b_sum = aux[:, 0, 0:32].rearrange("p (b h) -> p b h", h=8)[:, :, MH:2 * MH]
            dve.tensor_tensor(mg[:, 4, :, 0:MH], mg[:, 0, :, 0:MH], b_sum, ALU.subtract).then_inc(u_ready, 1)
            dve.tensor_copy(mg[:, 4, :, MH:2 * MH], b_sum).then_inc(u_ready, 1)
            dve.wait_ge(u_turned, 1)
            step(dve.tensor_copy(rows[:, 0, :], aux[0:MH, 2, :]))
            step(dve.tensor_tensor_scan(rows[:, 1, :], rows[:, 0, :], rows[:, 0, :], -3.0e38, ALU.max, ALU.max))
            step(dve.scalar_tensor_tensor(rows[:, 0, :], aux[0:MH, 3, :], -1.0, rows[:, 1, :], ALU.mult, ALU.subtract))
            dve.tensor_scalar(rows[:, 1, :], rows[:, 1, :], -1.0, None, ALU.mult).then_inc(rows_ready, 1)
            for h in range(MH):
                for j in range(TB):
                    n, w = TB * h + j, T - j * P
                    dve.wait_ge(m_s, n + 1)
                    dve.wait_ge(m_exp, 5 * h + j + 1)
                    if n >= 4:
                        dve.wait_ge(m_pv, n - 3)
                    dve.scalar_tensor_tensor(ptT[:, n % 4, 0:w], aux[:, n % 2, 0:w], float(P) ** -0.5,
                                             decay_e[:, n % 2, 0:w], ALU.mult, ALU.mult).then_inc(m_p, 1)
                dve.wait_ge(m_den, h + 1)
                step(dve.tensor_tensor(tmp[:, 0, :], tmp[:, 0, :], tmp[:, 1, :], ALU.max))
                step(dve.reciprocal(tmp[:, 0, :], tmp[:, 0, :]))
                dve.tensor_tensor(m_h[:, h, :], lin[:, 2 * (h % 2), :], tmp[:, 0, :], ALU.mult).then_inc(m_head, 1)
            for h in range(MH):
                dve.wait_ge(gn_mean, h + 1)
                dve.scalar_tensor_tensor(m_h[:, h, :], aux[:, h % 2, :], -1.0 / P, m_h[:, h, :], ALU.mult, ALU.add)\
                   .then_inc(gn_centered, 1)
            for h in range(MH):
                dve.wait_ge(gn_root, h + 1)
                step(dve.reciprocal(tmp[:, 1, :], tmp[:, 1, :]))
                step(dve.scalar_tensor_tensor(m_h[:, h, :], m_h[:, h, :], col("m_norm_g_2", h), tmp[:, 1, :], ALU.mult,
                                              ALU.mult))
                step(dve.tensor_tensor(act_hi[:, h, :], m_h[:, h, :], m_o[:, h, :], ALU.mult))
                step(dve.tensor_tensor(m_h[:, h, :], m_h[:, h, :], m_o[:, h, :], ALU.mult))
                step(dve.tensor_tensor(act_lo[:, h, :], m_h[:, h, :], act_hi[:, h, :].bitcast(F32), ALU.subtract))
                dve.nop().then_inc(gn_done, 1)
                dve.nop().then_inc(mix_ready, 1)

            dve.wait_ge(r_sig, 8)
            dve.wait_ge(masks_ready, 1)
            for half in range(2):
                step(dve.memset(end_decay, 0.0))
                for pl in range(2):
                    p = 2 * half + pl
                    r, k, v = rkv[:, p, :], rkv[:, 4 + p, :], rkv[:, 8 + p, :]
                    chunks = lambda ap: ap.rearrange("p (c n) -> p c n", n=CH)
                    if p:
                        dve.wait_ge(z_exp, 3 * p)
                    for c in range(NC):
                        cs = slice(c * CH, (c + 1) * CH)
                        ins = dve.tensor_tensor_scan(work[:, 0, cs], ones[:, 0:CH], sw[:, p, cs], 0.0, ALU.mult, ALU.add)
                    step(ins)
                    dve.tensor_tensor(work[:, 1, :], work[:, 0, :], sw[:, p, :], ALU.subtract).then_inc(z_cum, 1)
                    dve.wait_ge(kk_sum, p + 1)
                    dve.tensor_scalar(tmp[:, 0, :], aux[:, 0, :], 1e-24, None, ALU.max).then_inc(kk_floor, 1)
                    dve.wait_ge(kk_root, p + 1)
                    step(dve.reciprocal(work[:, 4, :], tmp[:, 0, :]))
                    step(dve.scalar_tensor_tensor(work[:, 4, :], k, col("r_kk_2", p), work[:, 4, :], ALU.mult, ALU.mult))
                    step(dve.tensor_scalar(work[:, 5, :], rate[:, p, :], -1.0, col("r_ka_2", p), ALU.add, ALU.mult))
                    step(dve.scalar_tensor_tensor(k, work[:, 5, :], 1.0, k, ALU.add, ALU.mult))
                    dve.scalar_tensor_tensor(tmp[:, 1, :], r, col("r_rk_2", p), k, ALU.mult, ALU.mult)\
                       .then_inc(bonus_in, 1)
                    step(dve.tensor_tensor(work[:, 5, :], work[:, 4, :], rate[:, p, :], ALU.mult))
                    dve.wait_ge(z_exp, 3 * p + 3)
                    dve.tensor_tensor(RK[:, pl, :, 0, :], chunks(r), chunks(work[:, 2, :]), ALU.mult)
                    dve.tensor_tensor(RK[:, pl, :, 1, :], chunks(work[:, 4, :]), chunks(work[:, 1, :]), ALU.mult)
                    dve.tensor_tensor(BK[:, pl, :, 0, :], chunks(work[:, 5, :]), chunks(work[:, 3, :]), ALU.mult)
                    dve.tensor_tensor(BK[:, pl, :, 1, :], chunks(k), chunks(work[:, 3, :]), ALU.mult)
                    for hh in range(2):
                        rws = slice(64 * hh, 64 * hh + 64)
                        ins = dve.tensor_copy(end_decay[rws, :, 2 * pl + hh], chunks(work[rws, 2, :])[:, :, CH - 1])
                    ins.then_inc(packed, 1)
                    dve.wait_ge(packed, p + 1)
                    dve.wait_ge(bonus_sum, p + 1)
                    dve.tensor_tensor(r, aux[:, 1, :], v, ALU.mult).then_inc(bonus_done, 1)
                for pl in range(2):
                    for hh in range(2):
                        for b in range(2):
                            dve.wait_ge(g_built, 4 * (2 * half + pl) + 2 * hh + b + 1)
                            dve.tensor_tensor(G[:, pl, hh, 4 * b:4 * b + 4, :],
                                              lin[:, 2 * hh + b, :].rearrange("p (c n) -> p c n", n=P),
                                              g_mask.unsqueeze(1).broadcast_to([P, 4, P]), ALU.mult)\
                               .then_inc(g_masked, 1)
                dve.wait_ge(g_masked, 8 * (half + 1))
                wide = lambda ap: ap.unsqueeze(1).broadcast_to([CH, 16, CH])
                for pl in range(2):
                    lbt = G[half64, pl, :, :, CH:2 * CH].rearrange("p a c n -> p (a c) n")
                    step(dve.tensor_tensor(XT[pl], lbt, wide(level[:, 0, :]), ALU.mult))
                    dve.tensor_tensor(XT[pl], wide(ident[half64, 0:CH]), XT[pl], ALU.subtract).then_inc(xt_first, 1)
                bank = (aux, lin)
                banks = lambda pl, a: bank[pl][half64, a:a + 2, :].rearrange("p a (u n) -> p (a u) n", n=CH)
                for m in range(5):
                    for pl in range(2):
                        n = (5 * half + m) * 2 + pl
                        dve.wait_ge(iv_y, n + 1)
                        dve.tensor_tensor(T1(half, pl), banks(pl, 0), wide(level[:, m + 1, :]), ALU.mult)\
                           .then_inc(iv_t, 1)
                    for pl in range(2):
                        n = (5 * half + m) * 2 + pl
                        if m < 4:
                            dve.wait_ge(iv_x, (4 * half + m) * 2 + pl + 1)
                            dve.tensor_tensor(X[pl], X[pl], banks(pl, 2), ALU.subtract).then_inc(iv_xd, 1)
                        dve.wait_ge(iv_xt, n + 1)
                        if m < 4:
                            dve.tensor_tensor(XT[pl], XT[pl], banks(pl, 0), ALU.subtract).then_inc(iv_xtd, 1)
                        else:
                            lbt = G[half64, pl, :, :, CH:2 * CH].rearrange("p a c n -> p (a c) n")
                            dve.tensor_tensor(lbt, banks(pl, 0), XT[pl], ALU.subtract).then_inc(iv_xtd, 1)
                dve.wait_ge(iv_xtd, 10 * (half + 1))
                dve.memset(UV[0:64, :, :, :], 0.0).then_inc(uv_zero, 1)
                dve.memset(state[:, 0, :, :], 0.0).then_inc(s_new, 1)
                for c in range(NC):
                    n = NC * half + c
                    dve.wait_ge(w_sum, n + 1)
                    dve.tensor_copy(w_sb(half), aux[half64, 0, 0:256].rearrange("p (g n) -> p g n", n=CH))\
                       .then_inc(w_taken, 1)
                    dve.wait_ge(s_sum, n + 1)
                    if c:
                        dve.wait_ge(y_sum, n)
                    nxt = state[:, (c + 1) % 2, :, :]
                    step(dve.tensor_tensor(nxt, state[:, c % 2, :, :],
                                           aux[:, 2, 0:256].rearrange("p (g n) -> p g n", n=CH), ALU.add))
                    dve.tensor_tensor(nxt, nxt, end_decay[:, c, :].unsqueeze(2).broadcast_to([P, 4, CH]), ALU.mult)\
                       .then_inc(s_new, 1)
                    dve.wait_ge(s_new, (NC + 1) * half + c + 2)
                for pl in range(2):
                    p = 2 * half + pl
                    dve.wait_ge(y_mean, p + 1)
                    dve.scalar_tensor_tensor(y_sb[:, pl, :], aux[:, 0, :], -1.0 / CH, y_sb[:, pl, :], ALU.mult, ALU.add)\
                       .then_inc(y_centered, 1)
                for pl in range(2):
                    p = 2 * half + pl
                    y = y_sb[:, pl, :]
                    dve.wait_ge(y_root, p + 1)
                    step(dve.reciprocal(tmp[:, pl, :], tmp[:, pl, :]))
                    step(dve.scalar_tensor_tensor(y, y, col("r_gn_g_2", p), tmp[:, pl, :], ALU.mult, ALU.mult))
                    step(dve.scalar_tensor_tensor(y, y, col("r_gn_b_2", p), rkv[:, p, :], ALU.add, ALU.add))
                    dve.wait_ge(y_gate, p + 1)
                    step(dve.tensor_tensor(act_hi[:, 4 + p, :], aux[:, 2 + pl, :], y, ALU.mult))
                    step(dve.tensor_tensor(y, aux[:, 2 + pl, :], y, ALU.mult))
                    dve.tensor_tensor(act_lo[:, 4 + p, :], y, act_hi[:, 4 + p, :].bitcast(F32), ALU.subtract)\
                       .then_inc(mix_ready, 1)

        (mem_in, mem_turned, mem_done, mem_added, mem_summed, mem_root, mem_ready) = (sem(n) for n in (
            "mem_in", "mem_turned", "mem_done", "mem_added", "mem_summed", "mem_root", "mem_ready"))
        f_conv, f_silu, y_ready, y_turned, rows_act, rows_dve = (sem(n) for n in (
            "f_conv", "f_silu", "y_ready", "y_turned", "rows_act", "rows_dve"))
        XSTEPS = XH * TB
        XB = HEADS * TB

        def act_mem_load(act):
            act.wait_ge(mix_ready, KT)
            act.dma_start(mem_rows[:, :, :], d["mem_2"].rearrange("o (b p) c -> p (o b) c", p=P)).then_inc(mem_in, 16)

        def act_rest(act, step):
            act_norm_square(3, mix_out_l)

            def take_kv(i, s):
                slab_ready(act, xkv_l, i, s)
                for t in range(2):
                    act.activation(kv_x[:, 4 * i + 2 * s + t, :], lin[:, 2 * s + t, 0:M_TOK], ACT.Copy)\
                       .then_inc(bank_free[s], 1)

            def take_q(i, s):
                slab_ready(act, xq_l, i, s)
                for t in range(2):
                    act.activation(q_x[:, 4 * i + 2 * s + t, :], lin[:, 2 * s + t, :], ACT.Copy)\
                       .then_inc(bank_free[s], 1)

            act_linear(xkv_l, take_kv, unroll=True)
            act_norm_root(3)
            act_norm_high(3)
            act_linear(xq_l, take_q, unroll=True)
            for g in range(4):
                act.wait_ge(v_turned, 2 * TB + g + 1)
                act.activation(v_xtok[:, g // 2, g % 2 * 512:(g % 2 + 1) * 512], aux[:, g, :], ACT.Copy)\
                   .then_inc(v_done, 1)

            def turned(n):
                h, i = n // TB, n % TB
                act.wait_ge(p_turned, XB + n + 1)
                if h >= 2:
                    act.wait_ge(o_ready, HEADS + 2 * (h - 1))
                act.activation(x_pT[:, h % 2, :, i * P:(i + 1) * P],
                               aux[:, 2 + n % 2, 0:2 * P].rearrange("p (m q) -> p m q", m=2), ACT.Copy)\
                   .then_inc(p_copied, 1)

            for n in range(XSTEPS):
                act.wait_ge(s_max, XB + n + 1)
                if n >= 2:
                    act.wait_ge(p_turned, XB + n - 1)
                step(act.activation(x_s[:, n % 2, :], aux[:, n % 2, 0:M_TOK], ACT.Exp, bias=x_stat[:, 1, n % 4:n % 4 + 1],
                                    scale=XHD ** -0.5, accum_out=x_stat[:, 2, n % 4:n % 4 + 1]))
                act.nop().then_inc(s_exp, 1)
                if n:
                    turned(n - 1)
            turned(XSTEPS - 1)
            act_linear(xo_l)
            act_norm(4, xo_l)
            step(act.activation(gpad[:, :, 0:2], ident[:, 0:4].rearrange("p (a b) -> p a b", a=2), ACT.Copy, scale=0.0))

            def take_up(i, s):
                if s == 0:
                    slab_ready(act, up_l, i, 0)
                    for t in range(2):
                        tile_taken(act, up_l, i - 1, 1, t)
                        act.activation(gpad[:, t, 2:2 + T], lin[:, t, :], ACT.Copy).then_inc(bank_free[0], 1)
                else:
                    for t in range(2):
                        act.wait_ge(f_conv, 2 * i + t + 1)
                        act.activation(gconv[:, t, :], gconv[:, t, :], ACT.Silu).then_inc(f_silu, 1)

            act_linear(up_l, take_up)
            act_linear(down_l)
            act_norm_square(5, down_l)
            act_norm_root(5)
            for n in range(0, 8, 2):
                act.wait_ge(y_turned, n + 1)
                act.activation(out_rows[:, n % 4, n // 4 * 512:(n // 4 + 1) * 512], (aux, lin)[n // 4][:, n % 4, :],
                               ACT.Copy).then_inc(rows_act, 1)

        def pe_mem(pe):
            pe.wait_ge(mem_in, 16)
            for k in range(0, KT, 2):
                if k >= 4:
                    pe.wait_ge(mem_done, k // 2 - 1)
                for j in range(4):
                    last = pe.transpose(aux[:, k // 2 % 2, j * P:(j + 1) * P],
                                        mem_rows[:, j % 2, (k + j // 2) * P:(k + j // 2 + 1) * P], ident[:, :])
                last.then_inc(mem_turned, 1)
            pe.wait_ge(mem_added, KT)
            pe.matmul(aux[:, 2, 0:M_TOK], ones[:, :], rms_inv[:, 0:M_TOK], start=True, stop=True).then_inc(mem_summed, 1)

        def pe_rest(pe):
            pe.wait_ge(mem_ready, KT)
            pe_linear(xkv_l, mem_hi, mem_lo)
            pe_norm(3)
            pe.wait_ge(act_ready, 4 * KT)
            pe_linear(xq_l, act_hi, act_lo)
            every_tile_taken(pe, xkv_l)
            for g in range(4):
                for j in range(4):
                    last = pe.transpose(aux[:, g, j * P:(j + 1) * P],
                                        kv_x[:, 8 + g % 2 * 4 + j, g // 2 * P:(g // 2 + 1) * P], ident[:, :])
                last.then_inc(v_turned, 1)
            every_tile_taken(pe, xq_l)

            def turn(n):
                h, i = n // TB, n % TB
                pe.wait_ge(s_diag, XB + n + 1)
                if n >= 2:
                    pe.wait_ge(p_copied, XB + n - 1)
                for m in range(2):
                    last = pe.matmul(aux[:, 2 + n % 2, m * P:(m + 1) * P], x_s[:, n % 2, m * P:(m + 1) * P],
                                     x_diag[:, n % 2, :], start=True, stop=True)
                last.then_inc(p_turned, 1)
                if i == TB - 1:
                    pe.wait_ge(p_copied, XB + n + 1)
                    if h >= 2:
                        pe.wait_ge(o_done, HEADS + 2 * (h - 1))
                    for dt in range(2):
                        at = h * XHD + dt * P
                        for m in range(2):
                            last = pe.matmul(lin[:, 2 * (h % 2) + dt, :], v_xtok[:, m, at:at + P], x_pT[:, h % 2, m, :],
                                             start=(m == 0), stop=(m == 1))
                        last.then_inc(o_ready, 1)

            for n in range(XSTEPS):
                h, i = n // TB, n % TB
                if n >= 2:
                    pe.wait_ge(s_exp, XB + n - 1)
                else:
                    pe.wait_ge(v_done, 2 * TB + n + 1)
                for dt in range(2):
                    last = pe.matmul(aux[:, n % 2, 0:M_TOK], q_x[:, 2 * h + dt, i * P:(i + 1) * P], kv_x[:, 2 * h + dt, :],
                                     start=(dt == 0), stop=(dt == 1))
                last.then_inc(s_ready, 1)
                if n == 1:
                    pe.wait_ge(v_done, 2 * TB + 4)
                if n:
                    turn(n - 1)
            turn(XSTEPS - 1)
            pe.wait_ge(o_done, HEADS + KT)
            pe_linear(xo_l, act_hi, act_lo)
            pe_norm(4)
            pe.wait_ge(act_ready, 5 * KT)
            pe_linear(up_l, act_hi, act_lo)
            pe.wait_ge(hid_ready, FT + FT)
            pe_linear(down_l, hid2_hi, hid2_lo)
            pe_norm(5)
            every_tile_taken(pe, down_l)
            for n in range(8):
                k0, b = 4 * (n // 4), n % 4
                pe.wait_ge(y_ready, k0 + 4)
                for j in range(4):
                    last = pe.transpose((aux, lin)[n // 4][:, b, j * P:(j + 1) * P], y_fin[:, k0 + j, b * P:(b + 1) * P],
                                        ident[:, :])
                last.then_inc(y_turned, 1)

        def dve_mem(dve, step):
            for g in range(KT // 2):
                dve.wait_ge(mem_turned, g + 1)
                dve.tensor_copy(memT[:, 2 * g:2 * g + 2, :], aux[:, g % 2, :].rearrange("p (k m) -> p k m", k=2))\
                   .then_inc(mem_done, 1)
                dve.wait_ge(mem_done, g + 1)
                for k in (2 * g, 2 * g + 1):
                    if k == 0:
                        dve.tensor_tensor(rms_inv[:, 0:M_TOK], memT[:, k, :], memT[:, k, :], ALU.mult)\
                           .then_inc(mem_added, 1)
                    else:
                        step(dve.tensor_tensor(tmp[:, 0, 0:M_TOK], memT[:, k, :], memT[:, k, :], ALU.mult))
                        dve.tensor_tensor(rms_inv[:, 0:M_TOK], rms_inv[:, 0:M_TOK], tmp[:, 0, 0:M_TOK], ALU.add)\
                           .then_inc(mem_added, 1)
                    dve.wait_ge(mem_added, k + 1)
            dve.wait_ge(mem_root, 1)
            step(dve.reciprocal(rms_inv[:, 0:M_TOK], tmp[:, 1, 0:M_TOK]))
            for k in range(KT):
                step(dve.scalar_tensor_tensor(memT[:, k, :], memT[:, k, :], col("norm_mem_2", k), rms_inv[:, 0:M_TOK],
                                              ALU.mult, ALU.mult))
                step(dve.tensor_copy(mem_hi[:, k, :], memT[:, k, :]))
                dve.tensor_tensor(mem_lo[:, k, :], memT[:, k, :], mem_hi[:, k, :].bitcast(F32), ALU.subtract)\
                   .then_inc(mem_ready, 1)

        def dve_rest(dve, step):
            dve_norm(3, "norm_x_2", step)

            def divide(n):
                dve.wait_ge(s_exp, XB + n + 1)
                step(dve.reciprocal(x_stat[:, 0, n % 4:n % 4 + 1], x_stat[:, 2, n % 4:n % 4 + 1]))
                dve.tensor_scalar(x_diag[:, n % 2, :], ident[:, :], x_stat[:, 0, n % 4:n % 4 + 1], None, ALU.mult)\
                   .then_inc(s_diag, 1)

            def head_out(h):
                for dt in range(2):
                    k, bank = 2 * h + dt, lin[:, 2 * (h % 2) + dt, :]
                    dve.wait_ge(o_ready, HEADS + k + 1)
                    step(dve.tensor_copy(act_hi[:, k, :], bank))
                    dve.tensor_tensor(act_lo[:, k, :], bank, act_hi[:, k, :].bitcast(F32), ALU.subtract)\
                       .then_inc(o_done, 1)

            for n in range(XSTEPS):
                dve.wait_ge(s_ready, XB + n + 1)
                if n >= 2:
                    dve.wait_ge(p_turned, XB + n - 1)
                step(dve.tensor_reduce(x_stat[:, 0, n % 4:n % 4 + 1], aux[:, n % 2, 0:M_TOK], AX.X, ALU.max))
                dve.tensor_scalar(x_stat[:, 1, n % 4:n % 4 + 1], x_stat[:, 0, n % 4:n % 4 + 1], -XHD ** -0.5, None,
                                  ALU.mult).then_inc(s_max, 1)
                if n:
                    divide(n - 1)
                if n % TB == 2 and n // TB:
                    head_out(n // TB - 1)
            divide(XSTEPS - 1)
            head_out(XH - 1)
            add_to_residual(xo_l)
            dve_norm(4, "norm_ffn_2", step)
            with dve.Fori(0, up_l.bodies) as i:
                step.enter(i, 6)
                for t in range(2):
                    tile_taken(dve, up_l, i, 0, t)
                    tap = lambda j: tab[:, 2, bass.ds(2 * i + (32 + FT * j + t), 1)]
                    step(dve.tensor_scalar(gconv[:, t, :], gpad[:, t, 0:T], tap(0), tap(3), ALU.mult, ALU.add))
                    step(dve.scalar_tensor_tensor(gconv[:, t, :], gpad[:, t, 1:1 + T], tap(1), gconv[:, t, :], ALU.mult,
                                                  ALU.add))
                    dve.scalar_tensor_tensor(gconv[:, t, :], gpad[:, t, 2:2 + T], tap(2), gconv[:, t, :], ALU.mult,
                                             ALU.add).then_inc(f_conv, 1)
                for t in range(2):
                    slab_ready(dve, up_l, i, 1)
                    dve.wait_ge(f_silu, 2 * i + t + 1)
                    at = 2 * i + t
                    step(dve.tensor_tensor(hid2_hi[:, bass.ds(at, 1), :], lin[:, 2 + t:3 + t, :], gconv[:, t:t + 1, :],
                                           ALU.mult))
                    dve.tensor_tensor(gconv[:, t, :], lin[:, 2 + t, :], gconv[:, t, :], ALU.mult).then_inc(bank_free[1], 1)
                    tile_taken(dve, up_l, i, 1, t)
                    dve.tensor_tensor(hid2_lo[:, bass.ds(at, 1), :], gconv[:, t:t + 1, :],
                                      hid2_hi[:, bass.ds(at, 1), :].bitcast(F32), ALU.subtract).then_inc(hid_ready, 1)
                    dve.wait_ge(hid_ready, FT + at + 1)
            step.leave(up_l.bodies)
            add_to_residual(down_l)
            dve_norm(5, "norm_final_2", step, to=y_fin)
            for n in range(1, 8, 2):
                dve.wait_ge(y_turned, n + 1)
                dve.tensor_copy(out_rows[:, n % 4, n // 4 * 512:(n // 4 + 1) * 512], (aux, lin)[n // 4][:, n % 4, :])\
                   .then_inc(rows_dve, 1)

        block = ctx.enter_context(nc.Block())

        @block.sync
        def _(sp):
            for t in range(2):
                sp.dma_start(x_rows[:, 2 * t:2 * t + 2, :],
                             d["x"].rearrange("o (b p) c -> p (o b) c", p=P)[:, 2 * t:2 * t + 2, :]).then_inc(x_in, 16)
            for layer in layers:
                stream(sp, layer)
            if stop:
                every_tile_taken(sp, layers[-1])
                sp.dma_start(out, xT[:, :, :]).then_inc(stored, 16)
                sp.wait_ge(stored, 16)
                return
            for n in range(8):
                sp.wait_ge((rows_act, rows_dve)[n % 2], n // 2 + 1)
                c = slice(n // 4 * 512, (n // 4 + 1) * 512)
                sp.dma_start(out.rearrange("o (b p) c -> p (o b) c", p=P)[:, n % 4, c], out_rows[:, n % 4, c])\
                   .then_inc(stored, 16)
            sp.wait_ge(stored, 16 * 8)

        @block.gpsimd
        def _(pool):
            step = Steps(pool, pool_step)
            pool.memset(raw_rows[:, :, :], 0.0).then_inc(rows_zero, 1)
            pool.memset(ident[:, :], 0.0)
            pool.memset(ones[:, :], 1.0)
            pool.memset(upto[:, :], 1.0)
            pool.memset(before[:, :], 1.0)
            pool.memset(later_key[:, :], 0.0)
            pool.memset(eps_col[:, :], EPS)
            step(pool.memset(halves[:, :], 0.0))
            pool.sem_inc(w_low, RING)
            pool.memset(halves[0:64, 0:64], 1.0)
            step(pool.memset(halves[64:128, 64:128], 1.0))
            pool.affine_select(out=ident[:, :], in_=ident[:, :], compare_op=ALU.not_equal, fill=1.0, base=0,
                               pattern=[[-1, P]], channel_multiplier=1)
            pool.affine_select(out=upto[:, :], in_=upto[:, :], compare_op=ALU.is_ge, fill=0.0, base=0,
                               pattern=[[1, P]], channel_multiplier=-1)
            pool.affine_select(out=before[:, :], in_=before[:, :], compare_op=ALU.is_ge, fill=0.0, base=-1,
                               pattern=[[1, P]], channel_multiplier=-1)
            pool.affine_select(out=later_key[:, :], in_=later_key[:, :], compare_op=ALU.is_ge, fill=MASKED, base=0,
                               pattern=[[-1, P]], channel_multiplier=1).then_inc(consts, 1)
            for layer in layers[:8]:
                pool_linear(layer)
            if stop != "ffn":
                pool_masks(pool, step)
                for layer in layers[8:]:
                    pool_linear(layer)


        @block.scalar
        def _(act):
            step = Steps(act, act_step)
            act.wait_ge(rows_zero, 1)
            for name, (t, r, n) in place.items():
                if name == "r_mu_tail":
                    act.dma_start(raw_rows[r:r + 1, t, :], d["r_mu_2"][:, R_COLS - P:R_COLS]).then_inc(rows_in, 16)
                    continue
                src = d[name]
                if name in ("g_q", "g_k"):
                    for half in (0, 64):
                        act.dma_start(raw_rows[r:r + 1, t, half:half + 64], src).then_inc(rows_in, 16)
                    continue
                size = 1
                for m in src.shape:
                    size *= m
                flat = src.rearrange({1: "a -> a", 2: "a b -> (a b)", 3: "a b c -> (a b c)"}[len(src.shape)])
                full = n
                act.dma_start(raw_rows[r:r + full, t, :], flat[0:full * P].rearrange("(r c) -> r c", c=P))\
                   .then_inc(rows_in, 16)
            act.dma_start(f_bias[:, 0, :], d["b_forget"].broadcast_to([P, 8])).then_inc(small_in, 16)
            act.dma_start(f_bias[:, 1, :], d["m_gate_b_2"].broadcast_to([P, 8])).then_inc(small_in, 16)
            act.dma_start(wf_raw[:, :, :], glu_l.w[:, :, 2 * CONV_CH + 3 * HEADS * HD:2 * CONV_CH + 3 * HEADS * HD + 8])\
               .then_inc(small_in, 16)
            act.sem_inc(w_used, RING)
            act.sem_inc(bank_free[0], 2)
            act.sem_inc(bank_free[1], 2)
            act.wait_ge(tab_turned, 3)
            act.activation(tab[:, :, :], aux[:, 2, 0:3 * P], ACT.Copy).then_inc(tab_ready, 1)
            round_unit(layers[0], 0, 0)
            round_unit(layers[0], 0, 1)
            act_norm(0, None)

            def take_glu(i, s):
                if s == 1:
                    for t in range(2):
                        slab_ready(act, glu_l, i, s)
                        if i:
                            tile_taken(act, glu_l, i - 1, 0, t)
                        act.activation(tmp[:, t, :], lin[:, 2 + t, :], ACT.Sigmoid).then_inc(bank_free[1], 1)

            def take_qkv(i, s):
                slab_ready(act, qkv_l, i, s)
                for t in range(2):
                    act.activation(qkv[:, 4 * i + 2 * s + t, :], lin[:, 2 * (s % 2) + t, :], ACT.Copy)\
                       .then_inc(bank_free[s % 2], 1)

            def take_gate(i, s):
                slab_ready(act, gate_l, i, s)
                for t in range(2):
                    act.activation(sig[:, 4 * i + 2 * s + t, :], lin[:, 2 * (s % 2) + t, :], ACT.Sigmoid)\
                       .then_inc(bank_free[s % 2], 1)

            act_linear(glu_l, take_glu, unroll=True)
            act_linear(qkv_l, take_qkv, unroll=True)
            act.wait_ge(small_in, 48)
            act.activation(wf_hi[:, :, :], wf_raw[:, :, :], ACT.Copy).then_inc(f_split, 1)
            act_linear(gate_l, take_gate, unroll=True)

            act.wait_ge(f_biased, 1)
            step(act.activation(lf[:, 1, :, :], lf[:, 0, :, :], ACT.Abs))
            step(act.activation(lf[:, 2, :, :], lf[:, 1, :, :], ACT.Exp, scale=-1.0))
            act.activation(lf[:, 1, :, :], lf[:, 2, :, :], ACT.Ln, bias=ones[:, 0:1]).then_inc(f_ln, 1)
            for b in range(TB):
                act.wait_ge(v_turned, b + 1)
                act.activation(v_tok[:, b, :], aux[:, 2 + b % 2, :], ACT.Copy).then_inc(v_done, 1)

            for t in range(4):
                act.wait_ge(ln_centered, t + 1)
                if t >= 2:
                    act.wait_ge(ln_var, t - 1)
                act.activation(tmp[:, t % 2, :], conv[:, t, :], ACT.Square).then_inc(ln_square, 1)
            act.wait_ge(ln_var, 4)
            act.activation(tmp[:, 0, :], aux[:, 1, :], ACT.Sqrt, scale=1.0 / CONV_CH, bias=eps_col[:, 0:1])\
               .then_inc(ln_root, 1)
            for t in range(4):
                act.wait_ge(ln_scaled, t + 1)
                act.activation(conv[:, t, :], conv[:, t, :], ACT.Silu, bias=col("b_conv_ln", t)).then_inc(ln_silu, 1)
            act_linear(conv_out_l)

            act.wait_ge(br_ready, 4)
            for t in range(10):
                if t < 8:
                    if t >= 2:
                        act.wait_ge(qk_done, t - 1)
                    act.activation(tmp[:, t % 2, :], qkv[:, t, :], ACT.Square).then_inc(qk_square, 1)
                if 1 <= t < 9:
                    act.wait_ge(qk_summed, t)
                    act.activation(tmp[:, (t - 1) % 2, :], aux[:, 2 + (t - 1) % 2, :], ACT.Sqrt, scale=1.0 / HD,
                                   bias=eps_col[:, 0:1]).then_inc(qk_root, 1)

            def turned(n):
                h, i = n // TB, n % TB
                act.wait_ge(p_turned, n + 1)
                if h:
                    act.wait_ge(o_ready, h)
                act.activation(glu[:, 0:i + 1, i * P:(i + 1) * P],
                               aux[:, 2 + n % 2, 0:(i + 1) * P].rearrange("p (j q) -> p j q", q=P), ACT.Copy)\
                   .then_inc(p_copied, 1)
                if i == TB - 1:
                    act.wait_ge(o_ready, h + 1)
                    r = slice(64 * (h % 2), 64 * (h % 2) + 64)
                    act.activation(br_hi[r, h // 2, :], lin[r, 2 + h % 2, :], ACT.Copy).then_inc(o_high, 1)

            for n in range(HEADS * TB):
                h, i = n // TB, n % TB
                if i == 0:
                    act.wait_ge(cb_ready, h + 1)
                    if h >= 2:
                        act.wait_ge(s_taken, TB * (h - 1))
                    act.activation(conv[:, 2 + h % 2, :], lin[:, h % 2, :], ACT.Copy).then_inc(cb_copied, 1)
                act.wait_ge(s_max, n + 1)
                step(act.activation(conv[:, n % 2, 0:(i + 1) * P], conv[:, n % 2, 0:(i + 1) * P], ACT.Exp,
                                    bias=stat[:, 1, n % 4:n % 4 + 1], accum_out=stat[:, 2, n % 4:n % 4 + 1]))
                act.nop().then_inc(s_exp, 1)
                if n:
                    turned(n - 1)
            turned(HEADS * TB - 1)
            act_linear(attn_out_l)
            act_linear(out_l)
            act_norm(1, out_l)

            def take_ff(i, s):
                if s == 0:
                    slab_ready(act, ffn_in_l, i, s)
                    for t in range(2):
                        tile_taken(act, ffn_in_l, i - 1, 1, t)
                        act.activation(ffn_tmp[:, t, :], lin[:, t, :], ACT.Silu).then_inc(bank_free[0], 1)
            act_linear(ffn_in_l, take_ff)
            act_linear(ffn_out_l)
            if stop != "ffn":
                act_mix(act, step)
            if not stop:
                act_rest(act, step)

        @block.tensor
        def _(pe):
            pe.wait_ge(consts, 1)
            pe.wait_ge(rows_in, 16 * (len(place) + 2))
            for t in range(3):
                pe.transpose(aux[:, 2, t * P:(t + 1) * P], raw_rows[:, t, :], ident[:, :]).then_inc(tab_turned, 1)
            pe.wait_ge(x_in, 32)
            for k in range(KT):
                if k >= 2:
                    pe.wait_ge(x_done, k - 1)
                for b in range(TB):
                    last = pe.transpose(aux[:, k % 2, b * P:(b + 1) * P], x_rows[:, b, k * P:(k + 1) * P], ident[:, :])
                last.then_inc(x_turned, 1)
            pe.wait_ge(x_done, KT)
            pe_norm(0)
            pe.wait_ge(act_ready, KT)
            pe_linear(glu_l, act_hi, act_lo)
            pe_linear(qkv_l, act_hi, act_lo)
            pe_linear(gate_l, act_hi, act_lo)

            pe.wait_ge(f_low, 1)
            for b in range(TB):
                blk = slice(b * P, (b + 1) * P)
                for k in range(KT):
                    pe.matmul(aux[:, 1, 8 * b:8 * b + 8], act_hi[:, k, blk], wf_hi[:, k, :], start=(k == 0), stop=False)
                    pe.matmul(aux[:, 1, 8 * b:8 * b + 8], act_hi[:, k, blk], wf_lo[:, k, :], start=False, stop=False)
                    last = pe.matmul(aux[:, 1, 8 * b:8 * b + 8], act_lo[:, k, blk], wf_hi[:, k, :], start=False,
                                     stop=(k == KT - 1))
            last.then_inc(f_logits, 1)
            every_tile_taken(pe, qkv_l)
            for b in range(TB):
                if b >= 2:
                    pe.wait_ge(v_done, b - 1)
                for t in range(4):
                    last = pe.transpose(aux[:, 2 + b % 2, t * P:(t + 1) * P], qkv[:, 8 + t, b * P:(b + 1) * P],
                                        ident[:, :])
                last.then_inc(v_turned, 1)
            pe.wait_ge(f_ready, 1)
            for b in range(TB):
                for a in range(b + 1):
                    last = pe.matmul(aux[:, 0, 8 * b:8 * b + 8], upto[:, :] if a == b else ones[:, :], lf[:, 3, a, :],
                                     start=(a == 0), stop=(a == b))
            last.then_inc(f_sum, 1)

            pe.wait_ge(c_ready, 1)
            pe.wait_ge(conv_step, 4 * CONV_W)
            for t in range(4):
                last = pe.matmul(aux[:, 0, :], ones[:, :], conv[:, t, :], start=(t == 0), stop=(t == 3))
            last.then_inc(ln_mean, 1)
            for t in range(4):
                pe.wait_ge(ln_square, t + 1)
                pe.matmul(aux[:, 1, :], ones[:, :], tmp[:, t % 2, :], start=(t == 0), stop=(t == 3)).then_inc(ln_var, 1)
            pe.wait_ge(br_ready, 4)
            pe_linear(conv_out_l, br_hi, br_lo)

            pe.wait_ge(v_done, TB)
            for t in range(8):
                pe.wait_ge(qk_square, t + 1)
                if t >= 2:
                    pe.wait_ge(qk_root, t - 1)
                pe.matmul(aux[:, 2 + t % 2, :], halves[:, :], tmp[:, t % 2, :], start=True, stop=True)\
                  .then_inc(qk_summed, 1)
            pe.wait_ge(qk_done, 8)
            every_tile_taken(pe, conv_out_l)

            def scores(n):
                h, i = n // TB, n % TB
                r = slice(64 * (h % 2), 64 * (h % 2) + 64)
                if n >= 2:
                    pe.wait_ge(s_taken, n - 1)
                pe.matmul(aux[:, n % 2, 0:(i + 1) * P], qkv[r, h // 2, i * P:(i + 1) * P],
                          qkv[r, 4 + h // 2, 0:(i + 1) * P], start=True, stop=False)
                pe.matmul(aux[:, n % 2, i * P:(i + 1) * P], ident[:, :], later_key[:, :], start=False, stop=True)\
                  .then_inc(s_ready, 1)

            def key_bias(h):
                pe.wait_ge(lf_wide, h + 1)
                if h >= 2:
                    pe.wait_ge(cb_copied, h - 1)
                for b in range(TB):
                    for a in range(b + 1):
                        last = pe.matmul(lin[:, h % 2, b * P:(b + 1) * P], neg_lf_wide[:, a, :],
                                         upto[:, :] if a == b else ones[:, :], start=(a == 0), stop=(a == b))
                last.then_inc(cb_ready, 1)

            def turn(n):
                h, i = n // TB, n % TB
                pe.wait_ge(s_diag, n + 1)
                if n >= 2:
                    pe.wait_ge(p_copied, n - 1)
                for j in range(i + 1):
                    last = pe.matmul(aux[:, 2 + n % 2, j * P:(j + 1) * P], conv[:, n % 2, j * P:(j + 1) * P],
                                     diag[:, n % 2, :], start=True, stop=True)
                last.then_inc(p_turned, 1)
                if i == TB - 1:
                    pe.wait_ge(p_copied, n + 1)
                    if h >= 2:
                        pe.wait_ge(o_done, h - 1)
                    for j in range(TB):
                        last = pe.matmul(lin[64 * (h % 2):64 * (h % 2) + 64, 2 + h % 2, j * P:T],
                                         v_tok[:, j, h * HD:(h + 1) * HD], glu[:, j, j * P:T],
                                         start=(j == 0), stop=(j == TB - 1))
                    last.then_inc(o_ready, 1)

            key_bias(0)
            for n in range(HEADS * TB):
                scores(n)
                if n % TB == 2 and n // TB + 1 < HEADS:
                    key_bias(n // TB + 1)
                if n:
                    turn(n - 1)
            turn(HEADS * TB - 1)
            pe.wait_ge(o_done, HEADS)
            pe_linear(attn_out_l, br_hi, br_lo)
            pe.wait_ge(m_ready, KT)
            pe_linear(out_l, act_hi, act_lo)
            pe_norm(1)
            pe.wait_ge(act_ready, 2 * KT)
            pe_linear(ffn_in_l, act_hi, act_lo)
            pe.wait_ge(hid_ready, FT)
            pe_linear(ffn_out_l, hid_hi, hid_lo)
            if stop != "ffn":
                pe_mix(pe)
            if not stop:
                pe_rest(pe)

        @block.vector
        def _(dve):
            step = Steps(dve, dve_step)
            for k in range(KT):
                dve.wait_ge(x_turned, k + 1)
                dve.tensor_copy(xT[:, k, :], aux[:, k % 2, :]).then_inc(x_done, 1)
            dve.wait_ge(tab_ready, 1)
            dve_norm(0, "g_mix", step)
            step(dve.tensor_scalar(q_gain[:, :], col("g_q", 0), HD ** -0.5, None, ALU.mult))
            step(dve.memset(glu[:, :, 0:PAD], 0.0))
            for i in range(2):
                for t in range(2):
                    slab_ready(dve, glu_l, i, 0)
                    tile_taken(dve, glu_l, i, 1, t)
                    dve.tensor_tensor(glu[:, 2 * i + t, PAD:PAD + T], lin[:, t, :], tmp[:, t, :], ALU.mult)\
                       .then_inc(bank_free[0], 1)
            tile_taken(dve, glu_l, 1, 0, 1)
            for j in range(CONV_W):
                for t in range(4):
                    tap = tab[:, 1, 4 * j + t:4 * j + t + 1]
                    if j == 0:
                        dve.tensor_scalar(conv[:, t, :], glu[:, t, 0:T], tap, col("b_dw", t), ALU.mult, ALU.add)\
                           .then_inc(conv_step, 1)
                    else:
                        dve.wait_ge(conv_step, 4 * (j - 1) + t + 1)
                        dve.scalar_tensor_tensor(conv[:, t, :], glu[:, t, j:j + T], tap, conv[:, t, :], ALU.mult,
                                                 ALU.add).then_inc(conv_step, 1)
            dve.wait_ge(f_split, 1)
            dve.tensor_tensor(wf_lo[:, :, :], wf_raw[:, :, :], wf_hi[:, :, :].bitcast(F32), ALU.subtract)\
               .then_inc(f_low, 1)
            dve.wait_ge(f_logits, 1)
            dve.wait_ge(small_in, 48)
            dve.tensor_tensor(lf[:, 0, :, :], aux[:, 1, 0:32].rearrange("p (b h) -> p b h", h=8),
                                   f_bias[:, 0:1, :].broadcast_to([P, TB, 8]), ALU.add).then_inc(f_biased, 1)
            dve.wait_ge(f_ln, 1)
            dve.scalar_tensor_tensor(lf[:, 3, :, :], lf[:, 0, :, :], 0.0, lf[:, 1, :, :], ALU.min, ALU.subtract)\
               .then_inc(f_ready, 1)
            dve.wait_ge(f_sum, 1)
            dve.tensor_copy(csum[:, :, :], aux[:, 0, 0:32].rearrange("p (b h) -> p b h", h=8)).then_inc(c_ready, 1)

            dve.wait_ge(ln_mean, 1)
            for t in range(4):
                dve.scalar_tensor_tensor(conv[:, t, :], aux[:, 0, :], -1.0 / CONV_CH, conv[:, t, :], ALU.mult, ALU.add)\
                   .then_inc(ln_centered, 1)
            dve.wait_ge(ln_root, 1)
            step(dve.reciprocal(rms_inv[:, :], tmp[:, 0, :]))
            for t in range(4):
                dve.scalar_tensor_tensor(conv[:, t, :], conv[:, t, :], col("g_conv_ln", t), rms_inv[:, :], ALU.mult,
                                         ALU.mult).then_inc(ln_scaled, 1)
            for t in range(4):
                dve.wait_ge(ln_silu, t + 1)
                step(dve.tensor_copy(br_hi[:, t, :], conv[:, t, :]))
                dve.tensor_tensor(br_lo[:, t, :], conv[:, t, :], br_hi[:, t, :].bitcast(F32), ALU.subtract)\
                   .then_inc(br_ready, 1)
            for s in range(4):
                slab_ready(dve, conv_out_l, 0, s)
                for t in range(2):
                    g = sig[:, 2 * s + t, :]
                    dve.tensor_tensor(g, lin[:, 2 * (s % 2) + t, :], g, ALU.mult).then_inc(bank_free[s % 2], 1)

            for t in range(8):
                dve.wait_ge(qk_root, t + 1)
                step(dve.reciprocal(tmp[:, t % 2, :], tmp[:, t % 2, :]))
                dve.scalar_tensor_tensor(qkv[:, t, :], qkv[:, t, :], q_gain[:, :] if t < 4 else col("g_k", 0),
                                         tmp[:, t % 2, :], ALU.mult, ALU.mult).then_inc(qk_done, 1)

            def widen(h):
                if h:
                    dve.wait_ge(cb_ready, h)
                dve.tensor_scalar(neg_lf_wide[:, :, :], lf[:, 3, :, h:h + 1].broadcast_to([P, TB, P]), -1.0, None,
                                  ALU.mult).then_inc(lf_wide, 1)

            def divide(n):
                dve.wait_ge(s_exp, n + 1)
                step(dve.reciprocal(stat[:, 0, n % 4:n % 4 + 1], stat[:, 2, n % 4:n % 4 + 1]))
                dve.tensor_scalar(diag[:, n % 2, :], ident[:, :], stat[:, 0, n % 4:n % 4 + 1], None, ALU.mult)\
                   .then_inc(s_diag, 1)

            def head_out(h):
                r = slice(64 * (h % 2), 64 * (h % 2) + 64)
                dve.wait_ge(o_high, h + 1)
                dve.tensor_tensor(br_lo[r, h // 2, :], lin[r, 2 + h % 2, :], br_hi[r, h // 2, :].bitcast(F32),
                                  ALU.subtract).then_inc(o_done, 1)

            widen(0)
            for n in range(HEADS * TB):
                h, i = n // TB, n % TB
                m = (i + 1) * P
                dve.wait_ge(s_ready, n + 1)
                dve.wait_ge(cb_copied, h + 1)
                if n >= 2:
                    dve.wait_ge(p_turned, n - 1)
                dve.scalar_tensor_tensor(conv[:, n % 2, 0:m], aux[:, n % 2, 0:m], csum[:, i, h:h + 1],
                                         conv[:, 2 + h % 2, 0:m], ALU.add, ALU.add).then_inc(s_taken, 1)
                dve.wait_ge(s_taken, n + 1)
                step(dve.tensor_reduce(stat[:, 0, n % 4:n % 4 + 1], conv[:, n % 2, 0:m], AX.X, ALU.max))
                dve.tensor_scalar(stat[:, 1, n % 4:n % 4 + 1], stat[:, 0, n % 4:n % 4 + 1], -1.0, None, ALU.mult)\
                   .then_inc(s_max, 1)
                if i == 1 and h + 1 < HEADS:
                    widen(h + 1)
                if n:
                    divide(n - 1)
                if i == 2 and h:
                    head_out(h - 1)
            divide(HEADS * TB - 1)
            head_out(HEADS - 1)

            for s in range(4):
                slab_ready(dve, attn_out_l, 0, s)
                for t in range(2):
                    k = 2 * s + t
                    dve.tensor_tensor(tmp[:, t, :], lin[:, 2 * (s % 2) + t, :], sig[:, KT + k, :], ALU.mult)\
                       .then_inc(bank_free[s % 2], 1)
                    tile_taken(dve, attn_out_l, 0, s, t)
                    step(dve.tensor_tensor(act_hi[:, k, :], tmp[:, t, :], sig[:, k, :], ALU.add))
                    step(dve.tensor_tensor(tmp[:, t, :], tmp[:, t, :], sig[:, k, :], ALU.add))
                    dve.tensor_tensor(act_lo[:, k, :], tmp[:, t, :], act_hi[:, k, :].bitcast(F32), ALU.subtract)\
                       .then_inc(m_ready, 1)
                    dve.wait_ge(m_ready, k + 1)

            add_to_residual(out_l)
            dve_norm(1, "g_ffn", step)
            with dve.Fori(0, ffn_in_l.bodies) as i:
                step.enter(i, 2)
                for t in range(2):
                    slab_ready(dve, ffn_in_l, i, 1)
                    tile_taken(dve, ffn_in_l, i, 0, t)
                    at = 2 * i + t
                    step(dve.tensor_tensor(hid_hi[:, bass.ds(at, 1), :], lin[:, 2 + t:3 + t, :], ffn_tmp[:, t:t + 1, :],
                                           ALU.mult))
                    dve.tensor_tensor(ffn_tmp[:, 2 + t, :], lin[:, 2 + t, :], ffn_tmp[:, t, :], ALU.mult)\
                       .then_inc(bank_free[1], 1)
                    tile_taken(dve, ffn_in_l, i, 1, t)
                    dve.tensor_tensor(hid_lo[:, bass.ds(at, 1), :], ffn_tmp[:, 2 + t:3 + t, :],
                                      hid_hi[:, bass.ds(at, 1), :].bitcast(F32), ALU.subtract).then_inc(hid_ready, 1)
                    dve.wait_ge(hid_ready, at + 1)
            step.leave(ffn_in_l.bodies)
            add_to_residual(ffn_out_l)
            if stop != "ffn":
                dve_mix(dve, step)
                if not stop:
                    dve_mem(dve, step)
                add_to_residual(mix_out_l)
            if not stop:
                dve_rest(dve, step)


def kernel(**inputs):
    import numpy as np
    import concourse.bacc as bacc
    from concourse.bass_utils import run_bass_kernel_spmd

    nc = bacc.Bacc("TRN2", target_bir_lowering=False, num_devices=1)
    arrays, d = {}, {}
    for name, value in inputs.items():
        a = np.ascontiguousarray(value)
        arrays[f"in_{name}_dram"] = a
        d[name] = nc.dram_tensor(f"in_{name}_dram", a.shape, mybir.dt.from_np(a.dtype), kind="ExternalInput").ap()
    out = nc.dram_tensor("out_0_dram", (1, T, D), F32, kind="ExternalOutput").ap()
    build(nc, d, out)
    return run_bass_kernel_spmd(nc, [arrays], core_ids=[0]).results[0]["out_0_dram"]
```

```python
from contextlib import ExitStack
import math

import concourse.bass as bass
from concourse import mybir

F32 = mybir.dt.float32
F32R = mybir.dt.float32r
ALU = mybir.AluOpType
ACT = mybir.ActivationFunctionType
AX = mybir.AxisListType

P = 128
D = 1024
T = 512
KT = D // P
TB = T // P
EPS = 1e-6
CONV_CH, CONV_W = 512, 31
HEADS, HD = 8, 64
FF = 2816
FT = FF // P
RING = 4
UK, UN = 4, 256
PAD = CONV_W - 1
LAG = 3
MASKED = -1.0e30

MH = 4
M_COLS = 4 * 512 + 2 * MH
R_COLS = 3 * 512 + 64 + 64 + 160
DECAY = math.exp(-0.5)
GN_EPS = 64e-5
CH = 64
NC = T // CH
M_TOK = 256
XH, XHD = 4, 256

TABLE_A = [("g_mix", 8), ("b_dw", 4), ("g_conv_ln", 4), ("b_conv_ln", 4), ("g_ffn", 8), ("norm_mix_2", 8),
           ("m_conv_b_2", 8), ("m_norm_g_2", 4), ("r_mu_2", 14), ("r_mu_tail", 1), ("r_w0_2", 4), ("r_a0_2", 4), ("r_kk_2", 4),
           ("r_ka_2", 4), ("r_rk_2", 4), ("r_gn_g_2", 4), ("r_gn_b_2", 4), ("norm_x_2", 8), ("norm_mem_2", 8),
           ("norm_ffn_2", 8), ("norm_final_2", 8), ("g_q", 1), ("g_k", 1)]
TABLE_B = [("w_dw", 124)]
TABLE_C = [("m_conv_w_2", 32), ("f_conv_w_2", 66), ("f_conv_b_2", 22)]

INVERSES = ["norm 0", "qk", "ln", "norm 1", "norm 2", "m", "gn", "kk", "y 0", "y 1", "mem", "norm 3", "norm 4", "norm 5"]
SPREADS = [("norm 0", 1), ("ln", 1), ("qk", 8), ("norm 1", 1), ("norm 2", 1), ("m", MH), ("gn", MH), ("kk 0", 2), ("y 0", 2),
           ("kk 1", 2), ("y 1", 2), ("mem", 1), ("norm 3", 1), ("norm 4", 1), ("norm 5", 1)]


def inverse_of(name):
    return INVERSES.index(name) + 1


def spread_of(name, k=0):
    at = [n for n, _ in SPREADS].index(name)
    return sum(n for _, n in SPREADS[:at]) + k + 1


def pairs_of(name, k=0):
    of_pairs = [(n, c) for n, c in SPREADS if n.split()[0] in ("qk", "kk", "y")]
    at = [n for n, _ in of_pairs].index(name)
    return sum(c for _, c in of_pairs[:at]) + k + 1


class Steps:

    def __init__(self, eng, sem):
        self.eng, self.sem, self.n = eng, sem, 0

    def __call__(self, ins):
        ins.then_inc(self.sem, 1)
        self.n = self.n + 1
        self.eng.wait_ge(self.sem, self.n)

    def enter(self, i, per):
        self.start, self.per = self.n, per
        self.n = i * per + self.start

    def leave(self, times):
        self.n = self.start + times * self.per


def build(nc, d, out, stop=None):
    ctx = ExitStack()
    with ctx:
        def sb(name, shape, dt=F32, where=ctx):
            return where.enter_context(nc.sbuf_tensor(name, shape, dt))

        def sem(name):
            return ctx.enter_context(nc.semaphore(name))

        w_raw = sb("w_raw", [P, RING, UK, UN])
        w_hi = sb("w_hi", [P, RING, UK, UN], F32R)
        w_lo = sb("w_lo", [P, RING, UK, UN], F32R)
        xT = sb("xT", [P, KT, T])
        ident = sb("ident", [P, P])
        ones = sb("ones", [P, P])
        halves = sb("halves", [P, P])
        upto = sb("upto", [P, P])
        before = sb("before", [P, P])
        later_key = sb("later_key", [P, P])
        tab = sb("tab", [P, 3, P])
        rms_inv = sb("rms_inv", [P, T])
        eps_col = sb("eps_col", [P, 3])
        q_gain = eps_col[:, 2:3]
        root = sb("root", [P, 76])
        inv = sb("inv", [P, 76])
        f_bias = sb("f_bias", [P, 2, 8])

        with ExitStack() as ph:
            raw_rows = sb("raw_rows", [P, 3, P], where=ph)
            x_rows = sb("x_rows", [P, TB, D], where=ph)
        act_hi = sb("act_hi", [P, KT, T], F32R)
        act_lo = sb("act_lo", [P, KT, T], F32R)
        tmp = sb("tmp", [P, 2, T])
        with ExitStack() as ph:
            glu = sb("glu", [P, 4, T + PAD], where=ph)
            conv = sb("conv", [P, 4, T], where=ph)
            qkv = sb("qkv", [P, 12, T], where=ph)
            v_tok = sb("v_tok", [P, TB, 512], where=ph)
            sig = sb("sig", [P, 16, T], where=ph)
            br_hi = sb("br_hi", [P, 4, T], F32R, where=ph)
            br_lo = sb("br_lo", [P, 4, T], F32R, where=ph)
            lf = sb("lf", [P, 4, TB, 8], where=ph)
            csum = sb("csum", [P, TB, 8], where=ph)
            neg_c = sb("neg_c", [HEADS, T], where=ph)
            stat = sb("stat", [P, 3, 4], where=ph)

        diag = rms_inv[:, 0:2 * P].rearrange("p (a b) -> p a b", a=2)

        def score(n):
            return (conv, tmp)[n % 4 // 2][:, n % 2, :]
        with ExitStack() as ph:
            hid_hi = sb("hid_hi", [P, FT, T], F32R, where=ph)
            hid_lo = sb("hid_lo", [P, FT, T], F32R, where=ph)
            ffn_tmp = sb("ffn_tmp", [P, 4, T], where=ph)
        with ExitStack() as ph:
            mix = sb("mix", [P, 25632], where=ph)

        def part(at, *dims, rows=slice(0, P)):
            size = math.prod(dims)
            names = "abcde"[:len(dims)]
            flat = mix[rows, at:at + size]
            if len(dims) == 1:
                return flat
            return flat.rearrange(f"p ({' '.join(names)}) -> p {' '.join(names)}", **dict(zip(names, dims)))

        rkv = part(0, 12, T)
        lora = part(6144, 3, T)
        sw = part(7680, 4, T)
        rate = part(9728, 4, T)
        ptT = part(7680, 4, T)
        decay_e = part(9728, 2, T)
        rows = part(10752, 2, T, rows=slice(0, MH))
        m_qk = part(11776, 8, T)
        m_v = part(15872, 4, T)
        m_h = part(15872, 4, T)
        m_vtok = part(17920, TB, 512)
        m_o = part(19968, 4, T)
        pad = part(22016, 2, T + 4)
        up_w = part(23048, 512)
        mg = part(23560, 5, TB, 8)
        RK = part(11776, 2, NC, 2, CH)
        BKt = part(13824, 2, NC, P)
        BK = part(15872, 2, NC, 2, CH)
        UV = part(17920, NC, 4, CH)
        G = part(19968, 2, 2, NC, P)
        work = part(19968, 8, T)
        half64 = slice(0, CH)
        X = [part(15872 + 1024 * p, 16, CH, rows=half64) for p in range(2)]
        XT = [part(17920 + 1024 * p, 16, CH, rows=half64) for p in range(2)]
        y_sb = part(11776, 2, T)
        end_decay = part(24064, NC, 4)
        g_mask = part(24096, P)
        level = part(24224, 6, CH, rows=half64)
        up_g = part(24608, 2, 512)
        state = part(6144, 2, 4, CH)

        with ExitStack() as ph:
            q_x = sb("q_x", [P, KT, T], where=ph)
            mem_rows = sb("mem_rows", [P, 2, D], where=ph)
            memT = sb("memT", [P, KT, M_TOK], where=ph)
            mem_hi = sb("mem_hi", [P, KT, M_TOK], F32R, where=ph)
            mem_lo = sb("mem_lo", [P, KT, M_TOK], F32R, where=ph)
            kv_x = sb("kv_x", [P, 16, M_TOK], where=ph)
            v_xtok = sb("v_xtok", [P, 2, D], where=ph)
            x_s = sb("x_s", [P, 4, M_TOK], where=ph)
            x_pT = sb("x_pT", [P, 2, 2, T], where=ph)
            x_stat = sb("x_stat", [P, 3, 4], where=ph)
            x_diag = sb("x_diag", [P, 2, P], where=ph)
        with ExitStack() as ph:
            hid2_hi = sb("hid2_hi", [P, FT, T], F32R, where=ph)
            hid2_lo = sb("hid2_lo", [P, FT, T], F32R, where=ph)
            gpad = sb("gpad", [P, 2, T + 2], where=ph)
            gconv = sb("gconv", [P, 2, T], where=ph)
        with ExitStack() as ph:
            out_rows = sb("out_rows", [P, TB, D], where=ph)
            y_fin = sb("y_fin", [P, KT, T], where=ph)

        lin = ctx.enter_context(nc.psum_tensor("lin", [P, 4, T], F32))
        aux = ctx.enter_context(nc.psum_tensor("aux", [P, 4, T], F32))

        class Layer:
            units, slabs = 0, 0

            def __init__(self, weight, kt, bodies, column, slabs=2, skip=(), uk=UK, made=None):
                self.skip = skip
                made = made or slabs
                self.w = weight.rearrange("o (k p) n -> p (o k) n", p=P)
                self.bodies, self.column, self.slabs = bodies, column, slabs
                self.parts = [(k, min(uk, kt - k)) for k in range(0, kt, uk)]
                self.kt, self.per = kt, made * len(self.parts)
                self.u0, self.s0 = Layer.units, Layer.slabs
                Layer.units += bodies * self.per
                Layer.slabs += bodies * slabs
                assert self.per % RING == 0

            def unit(self, k):
                return (k // len(self.parts), *self.parts[k % len(self.parts)])

        Layer.slabs = 0
        whole = lambda i, s: i * 2 * UN + s * UN
        glu_l = Layer(d["w_in"], KT, 2, lambda i, s: i * UN + s * CONV_CH)
        qkv_l = Layer(d["w_in"], KT, 3, lambda i, s: 2 * CONV_CH + whole(i, s))
        eight = dict(skip=[(0, 1), (1, 0), (1, 1)], uk=2, made=1)
        forget_l = Layer(d["w_in"], KT, 1, lambda i, s: 2 * CONV_CH + 3 * HEADS * HD, **eight)
        gate_l = Layer(d["w_in"], KT, 4, lambda i, s: 2 * CONV_CH + 3 * HEADS * HD + HEADS + whole(i, s))
        conv_out_l = Layer(d["w_conv_out"], 4, 1, lambda i, s: s * UN, slabs=4)
        attn_out_l = Layer(d["w_attn_out"], 4, 1, lambda i, s: s * UN, slabs=4)
        out_l = Layer(d["w_out"], KT, 2, whole)
        ffn_in_l = Layer(d["w_ffn_in"], KT, 11, lambda i, s: i * UN + s * FF)
        ffn_out_l = Layer(d["w_ffn_out"], FT, 2, whole)
        layers = [glu_l, qkv_l, forget_l, gate_l, conv_out_l, attn_out_l, out_l, ffn_in_l, ffn_out_l]
        if stop != "ffn":
            m_qk_l = Layer(d["w_in_2"], KT, 2, whole)
            m_vo_l = Layer(d["w_in_2"], KT, 2, lambda i, s: 1024 + whole(i, s))
            rkv_l = Layer(d["w_in_2"], KT, 3, lambda i, s: M_COLS + whole(i, s))
            lora_l = Layer(d["w_in_2"], KT, 1, lambda i, s: M_COLS + 3 * 512 + 32 * s, skip=[(1, 0)])
            m_gate_l = Layer(d["w_in_2"], KT, 1, lambda i, s: 4 * 512, **eight)
            mix_out_l = Layer(d["w_out_2"], KT, 2, whole)
            layers += [m_qk_l, m_vo_l, rkv_l, lora_l, m_gate_l, mix_out_l]
        if stop not in ("ffn", "mix2"):
            xkv_l = Layer(d["x_wkv_2"], KT, 4, whole)
            xq_l = Layer(d["x_wq_2"], KT, 2, whole)
            xo_l = Layer(d["x_wo_2"], KT, 2, whole)
            up_l = Layer(d["f_up_2"], KT, 11, lambda i, s: i * UN + s * FF)
            down_l = Layer(d["f_down_2"], FT, 2, whole)
            layers += [xkv_l, xq_l, xo_l, up_l, down_l]

        w_arrived = [sem(f"w_arrived{s}") for s in range(RING)]
        w_high = sem("w_high")
        w_low = sem("w_low")
        w_used = sem("w_used")
        bank_free = [sem("bank_free0"), sem("bank_free1")]
        consts = sem("consts")
        rows_zero = sem("rows_zero")
        rows_in = sem("rows_in")
        x_in = sem("x_in")
        small_in = sem("small_in")
        tab_turned = sem("tab_turned")
        tab_ready = sem("tab_ready")
        x_turned = sem("x_turned")
        x_done = sem("x_done")
        n_square, n_added, n_summed, n_root, n_scaled, n_high, act_ready = (
            sem(n) for n in ("n_square", "n_added", "n_summed", "n_root", "n_scaled", "n_high", "act_ready"))
        inv_ready, wide_ready, pairs_ready = sem("inv_ready"), sem("wide_ready"), sem("pairs_ready")
        dve_step, act_step, pool_step = (sem(n) for n in ("dve_step", "act_step", "pool_step"))

        conv_step = sem("conv_step")
        f_rows, f_logits, f_biased, f_ln, f_ready, f_sum, c_ready = (
            sem(n) for n in ("f_rows", "f_logits", "f_biased", "f_ln", "f_ready", "f_sum", "c_ready"))
        ln_mean, ln_centered, ln_square, ln_var, ln_root, ln_scaled, ln_silu, br_ready = (
            sem(n) for n in ("ln_mean", "ln_centered", "ln_square", "ln_var", "ln_root", "ln_scaled", "ln_silu",
                             "br_ready"))
        qk_square, qk_summed, qk_root, qk_done = (sem(n) for n in ("qk_square", "qk_summed", "qk_root", "qk_done"))
        v_turned, v_done = sem("v_turned"), sem("v_done")
        c_turned, c_rows, cb_ready, cb_copied = sem("c_turned"), sem("c_rows"), sem("cb_ready"), sem("cb_copied")
        s_ready, s_taken, s_max, s_exp, s_diag, p_turned, p_copied, o_ready, o_high, o_done = (
            sem(n) for n in ("s_ready", "s_taken", "s_max", "s_exp", "s_diag", "p_turned", "p_copied", "o_ready",
                             "o_high", "o_done"))
        m_ready, hid_ready = sem("m_ready"), sem("hid_ready")
        stored = sem("stored")

        place, row = {}, 0
        for t, table in enumerate((TABLE_A, TABLE_B, TABLE_C)):
            row = 0
            for name, n in table:
                place[name] = (t, row, n)
                row += n
            assert row <= P

        def col(name, j):
            t, r, _ = place[name]
            return tab[:, t, r + j:r + j + 1]

        def stream(eng, layer):
            with eng.Fori(0, layer.bodies) as i:
                at = [eng.snap(layer.column(i, s)) for s in range(layer.slabs)]
                for k in range(layer.per):
                    s, r, n = layer.unit(k)
                    eng.wait_ge(w_low, i * layer.per + (layer.u0 + k + 1))
                    eng.dma_start(w_raw[:, k % RING, 0:n, :], layer.w[:, r:r + n, bass.ds(at[s], UN)])\
                       .then_inc(w_arrived[k % RING], 16)

        def round_unit(layer, i, k):
            if k >= layer.per:
                follow = layers.index(layer) + 1
                last = layer.bodies - 1
                if type(i) is int and i == last:
                    if follow == len(layers):
                        return
                    layer, i, k = layers[follow], 0, k - layer.per
                else:
                    i, k = i + 1, k - layer.per
            n = layer.unit(k)[2]
            s = k % RING
            nc.scalar.wait_ge(w_arrived[s], i * (16 * (layer.per // RING)) + 16 * (layer.u0 // RING + k // RING + 1))
            nc.scalar.wait_ge(w_used, i * layer.per + (layer.u0 + k + 1))
            nc.scalar.activation(w_hi[:, s, 0:n, :], w_raw[:, s, 0:n, :], ACT.Copy).then_inc(w_high, 1)

        AHEAD = 2

        def act_linear(layer, take=None, unroll=False):
            def body(i):
                for k in range(layer.per):
                    round_unit(layer, i, k + AHEAD)
                    if (k + 1) % len(layer.parts) == 0 and take:
                        take(i, k // len(layer.parts))
            if unroll:
                for i in range(layer.bodies - 1):
                    body(i)
            elif layer.bodies > 1:
                with nc.scalar.Fori(0, layer.bodies - 1) as i:
                    body(i)
            body(layer.bodies - 1)

        def slab_ready(eng, layer, i, s):
            eng.wait_ge(w_used, i * layer.per + (RING + layer.u0 + (s + 1) * len(layer.parts)))

        def tile_taken(eng, layer, i, s, t):
            eng.wait_ge(bank_free[s % 2], i * layer.slabs + (layer.s0 + 2 * (s // 2) + 3 + t))

        def every_tile_taken(eng, layer):
            for s in (layer.slabs - 2, layer.slabs - 1):
                tile_taken(eng, layer, layer.bodies - 1, s, 1)

        def pool_linear(layer):
            with nc.gpsimd.Fori(0, layer.bodies) as i:
                for k in range(layer.per):
                    n, s = layer.unit(k)[2], k % RING
                    nc.gpsimd.wait_ge(w_high, i * layer.per + (layer.u0 + k + 1))
                    nc.gpsimd.tensor_tensor(w_lo[:, s, 0:n, :], w_raw[:, s, 0:n, :], w_hi[:, s, 0:n, :].bitcast(F32),
                                            ALU.subtract).then_inc(w_low, 1)

        def pe_linear(layer, hi, lo, ready=None):
            def body(i, first):
                for k in range(layer.per):
                    s, r, n = layer.unit(k)
                    if r == 0:
                        nc.tensor.wait_ge(bank_free[s % 2], i * layer.slabs + (layer.s0 + 2 * (s // 2) + 2))
                    nc.tensor.wait_ge(w_low, i * layer.per + (RING + layer.u0 + k + 1))
                    tiles = [t for t in range(2) if (s, t) not in layer.skip]
                    if first and s == 0:
                        order = [(j, t) for j in range(n) for t in tiles]
                    else:
                        order = [(j, t) for t in tiles for j in range(n)]
                    for j, t in order:
                        if first and s == 0 and t == 0:
                            nc.tensor.wait_ge(ready[0], ready[1] + r + j + 1)
                        bank = lin[:, 2 * (s % 2) + t, 0:hi.shape[2]]
                        c = slice(t * P, t * P + P)
                        high, low = w_hi[:, k % RING, j, c], w_lo[:, k % RING, j, c]
                        nc.tensor.matmul(bank, high, hi[:, r + j, :], start=(r + j == 0), stop=False)
                        nc.tensor.matmul(bank, high, lo[:, r + j, :], start=False, stop=False)
                        last = nc.tensor.matmul(bank, low, hi[:, r + j, :], start=False,
                                                stop=(r + j == layer.kt - 1))
                    last.then_inc(w_used, 1)
            if ready:
                body(0, True)
            if layer.bodies > bool(ready):
                with nc.tensor.Fori(int(bool(ready)), layer.bodies) as i:
                    body(i, False)

        def take_eight(layer):
            def take(i, s):
                slab_ready(nc.scalar, layer, 0, 0)
                nc.scalar.activation(rms_inv[0:8, :], lin[0:8, 0, :], ACT.Copy).then_inc(f_rows, 1)
                nc.scalar.wait_ge(f_rows, 1 if layer is forget_l else 2)
                nc.scalar.sem_inc(bank_free[0], 2)
                nc.scalar.sem_inc(bank_free[1], 2)
            return take

        def turn_eight(n):
            nc.tensor.wait_ge(f_rows, n)
            for b in range(TB):
                last = nc.tensor.transpose(aux[:, 1, 8 * b:8 * b + 8], rms_inv[0:8, b * P:(b + 1) * P], ident[0:8, 0:8])
            last.then_inc(f_logits, 1)

        def add_to_residual(layer):
            for i in range(2):
                for s in range(2):
                    slab_ready(nc.vector, layer, i, s)
                    for t in range(2):
                        x = xT[:, 4 * i + 2 * s + t, :]
                        nc.vector.tensor_tensor(x, lin[:, 2 * s + t, :], x, ALU.add)\
                          .then_inc(bank_free[s], 1)

        def act_norm_square(m, after):
            for k in range(KT):
                if after is None:
                    nc.scalar.wait_ge(x_done, k + 1)
                else:
                    tile_taken(nc.scalar, after, k // 4, k // 2 % 2, k % 2)
                if k >= 2:
                    nc.scalar.wait_ge(n_added, KT * m + k - 1)
                nc.scalar.activation(tmp[:, k % 2, :], xT[:, k, :], ACT.Square).then_inc(n_square, 1)

        def act_norm_root(m):
            nc.scalar.wait_ge(n_summed, m + 1)
            nc.scalar.activation(root[:, 0:TB], aux[:, 0, 0:TB], ACT.Sqrt, scale=1.0 / D, bias=eps_col[:, 0:1])\
              .then_inc(n_root, 1)

        def act_norm_high(m):
            for k in range(KT):
                nc.scalar.wait_ge(n_scaled, KT * m + k + 1)
                nc.scalar.activation(act_hi[:, k, :], tmp[:, k % 2, :], ACT.Copy).then_inc(n_high, 1)

        def act_norm(m, after):
            act_norm_square(m, after)
            act_norm_root(m)
            act_norm_high(m)

        def token_sums(to, squares, groups=1):
            for b in range(squares.shape[1] // P):
                last = nc.tensor.matmul(to[:, groups * b:groups * (b + 1)], squares[:, b * P:(b + 1) * P],
                                        ones[:, 0:1] if groups == 1 else halves[:, 0:P:CH], start=True, stop=True)
            return last

        def spread_tokens(to, at, blocks=TB):
            for b in range(blocks):
                last = nc.tensor.matmul(to[:, b * P:(b + 1) * P], inv[:, at + b:at + b + 1].broadcast_to([P, P]),
                                        ident[:, :], start=True, stop=True)
            last.then_inc(wide_ready, 1)

        def repeat_pair(to, at):
            nc.scalar.activation(to.rearrange("p (b g c) -> p b g c", b=TB, g=2),
                                 inv[:, at:at + 2 * TB].rearrange("p (b g) -> p b g", g=2).unsqueeze(3)
                                 .broadcast_to([P, TB, 2, CH]), ACT.Copy).then_inc(pairs_ready, 1)

        def spread_pair(to, repeated):
            for b in range(TB):
                last = nc.tensor.matmul(to[:, b * P:(b + 1) * P], repeated[:, b * P:(b + 1) * P], ident[:, :], start=True,
                                        stop=True)
            last.then_inc(wide_ready, 1)

        def pe_norm(m):
            nc.tensor.wait_ge(n_added, KT * (m + 1))
            token_sums(aux[:, 0, :], rms_inv).then_inc(n_summed, 1)
            nc.tensor.wait_ge(inv_ready, inverse_of(f"norm {m}"))
            spread_tokens(aux[:, 1, :], 0)

        def dve_norm(m, gain, step, to=None):
            v = nc.vector
            for k in range(KT):
                v.wait_ge(n_square, KT * m + k + 1)
                if k == 0:
                    v.tensor_copy(rms_inv[:, :], tmp[:, 0, :]).then_inc(n_added, 1)
                else:
                    v.wait_ge(n_added, KT * m + k)
                    v.tensor_tensor(rms_inv[:, :], rms_inv[:, :], tmp[:, k % 2, :], ALU.add).then_inc(n_added, 1)
            v.wait_ge(n_root, m + 1)
            v.reciprocal(inv[:, 0:TB], root[:, 0:TB]).then_inc(inv_ready, 1)
            v.wait_ge(wide_ready, spread_of(f"norm {m}"))

            if to is not None:
                for k in range(KT):
                    v.scalar_tensor_tensor(to[:, k, :], xT[:, k, :], col(gain, k), aux[:, 1, :], ALU.mult, ALU.mult)\
                     .then_inc(y_ready, 1)
                return

            def low(k):
                v.wait_ge(n_high, KT * m + k + 1)
                v.tensor_tensor(act_lo[:, k, :], tmp[:, k % 2, :], act_hi[:, k, :].bitcast(F32), ALU.subtract)\
                 .then_inc(act_ready, 1)
            for k in range(KT):
                if k >= 2:
                    low(k - 2)
                    v.wait_ge(act_ready, KT * m + k - 1)
                v.scalar_tensor_tensor(tmp[:, k % 2, :], xT[:, k, :], col(gain, k), aux[:, 1, :], ALU.mult, ALU.mult)\
                 .then_inc(n_scaled, 1)
            low(KT - 2)
            low(KT - 1)

        (m_conv, m_silu, r_shift, u_ready, u_turned, rows_ready, em_turned, m_e, m_s, m_exp, m_p, m_pv, m_den,
         m_head, m_normed) = (sem(n) for n in (
            "m_conv", "m_silu", "r_shift", "u_ready",
            "u_turned", "rows_ready", "em_turned", "m_e", "m_s", "m_exp", "m_p", "m_pv", "m_den",
            "m_head", "m_normed"))
        (gn_mean, gn_centered, gn_square, gn_var, gn_root, gn_done) = (sem(n) for n in (
            "gn_mean", "gn_centered", "gn_square", "gn_var", "gn_root", "gn_done"))
        (two_in, masks_ready, r_act, r_pre, r_sig, kk_square, kk_sum, kk_floor, kk_root, z_cum, z_exp, packed, bonus_in,
         bonus_sum, bonus_done) = (sem(n) for n in (
            "two_in", "masks_ready", "r_act", "r_pre", "r_sig", "kk_square", "kk_sum", "kk_floor", "kk_root", "z_cum",
            "z_exp", "packed", "bonus_in", "bonus_sum", "bonus_done"))
        (bt_turned, bt_done, g_built, g_masked, xt_first, x_first, x_copied, iv_y, iv_t, iv_x, iv_xd, iv_xt, iv_xtd, uv_zero,
         uv_turned, uv_done) = (sem(n) for n in (
            "bt_turned", "bt_done", "g_built", "g_masked", "xt_first", "x_first", "x_copied", "iv_y", "iv_t", "iv_x",
            "iv_xd", "iv_xt", "iv_xtd", "uv_zero", "uv_turned", "uv_done"))
        (w_sum, w_taken, u_sum, u_taken, s_sum, s_new, y_sum, y_copied, y_mean, y_centered, y_square, y_var, y_root,
         y_gate, mix_ready) = (sem(n) for n in (
            "w_sum", "w_taken", "u_sum", "u_taken", "s_sum", "s_new", "y_sum", "y_copied", "y_mean", "y_centered",
            "y_square", "y_var", "y_root", "y_gate", "mix_ready"))

        def act_mix(act, step):
            act_norm_square(2, ffn_out_l)
            act.dma_start(up_w[0:64, :], d["r_w_up_2"][0]).then_inc(two_in, 16)
            act.dma_start(up_w[64:128, :], d["r_a_up_2"][0]).then_inc(two_in, 16)
            act.dma_start(up_g[:, 0, :], d["r_g_up_2"][0, 0:P, :]).then_inc(two_in, 16)
            act.wait_ge(masks_ready, 1)
            act.dma_start(up_g[96:128, 1, :], d["r_g_up_2"][0, P:160, :]).then_inc(two_in, 16)
            act_norm_root(2)
            act_norm_high(2)
            act.wait_ge(two_in, 64)
            step(act.activation(pad[:, :, 0:3], ident[:, 0:6].rearrange("p (a b) -> p a b", a=2), ACT.Copy, scale=0.0))

            def silu(q):
                act.wait_ge(m_conv, q + 1)
                act.activation(m_qk[:, q, :], m_qk[:, q, :], ACT.Silu).then_inc(m_silu, 1)

            def take_qk(i, s):
                slab_ready(act, m_qk_l, i, s)
                for t in range(2):
                    q = 4 * i + 2 * s + t
                    if q >= 2:
                        act.wait_ge(m_conv, q - 1)
                    act.activation(pad[:, t, 3:3 + T], lin[:, 2 * s + t, :], ACT.Copy).then_inc(bank_free[s], 1)
                    if q >= 2:
                        silu(q - 2)

            def take_vo(i, s):
                slab_ready(act, m_vo_l, i, s)
                for t in range(2):
                    q = 2 * s + t
                    if i == 0:
                        act.activation(m_v[:, q, :], lin[:, q, :], ACT.Copy).then_inc(bank_free[s], 1)
                    else:
                        act.activation(m_o[:, q, :], lin[:, q, :], ACT.Sigmoid).then_inc(bank_free[s], 1)

            def take_shift(layer, i, s, t, q):
                if q >= 2:
                    act.wait_ge(r_shift, q - 1)
                act.activation(pad[:, q % 2, 3:3 + T], lin[:, 2 * s + t, :], ACT.Copy).then_inc(bank_free[s], 1)

            def take_rkv(i, s):
                slab_ready(act, rkv_l, i, s)
                for t in range(2):
                    take_shift(rkv_l, i, s, t, 4 * i + 2 * s + t)

            def take_lora(i, s):
                slab_ready(act, lora_l, i, s)
                if s == 1:
                    act.sem_inc(bank_free[1], 1)
                for t in range(s, 2):
                    take_shift(lora_l, i, s, t, 12 + s + t)

            act_linear(m_qk_l, take_qk, unroll=True)
            silu(6)
            silu(7)
            act_linear(m_vo_l, take_vo, unroll=True)
            act_linear(rkv_l, take_rkv, unroll=True)
            act_linear(lora_l, take_lora, unroll=True)
            act_linear(m_gate_l, take_eight(m_gate_l), unroll=True)

            act.wait_ge(f_biased, 2)
            step(act.activation(mg[:, 1, :, :], mg[:, 0, :, :], ACT.Abs))
            step(act.activation(mg[:, 2, :, :], mg[:, 1, :, :], ACT.Exp, scale=-1.0))
            act.activation(mg[:, 1, :, :], mg[:, 2, :, :], ACT.Ln, bias=ones[:, 0:1]).then_inc(f_ln, 1)
            for b in range(TB):
                act.wait_ge(v_turned, TB + b + 1)
                act.activation(m_vtok[:, b, :], aux[:, 2 + b % 2, :], ACT.Copy).then_inc(v_done, 1)
            act.wait_ge(em_turned, 1)
            step(act.activation(root[:, 28:44], lin[:, 3, 0:16], ACT.Exp))

            def copy_head(h):
                act.wait_ge(m_pv, TB * h + TB)
                act.activation(m_h[:, h, :], lin[:, 2 * (h % 2), :], ACT.Copy).then_inc(m_head, 1)

            for n in range(MH * TB):
                h, j = n // TB, n % TB
                w = T - j * P
                act.wait_ge(m_e, n + 1)
                if n >= 2:
                    act.wait_ge(m_p, n - 1)
                act.activation(decay_e[:, n % 2, 0:w], aux[:, 2 + n % 2, 0:w], ACT.Exp,
                               bias=mg[:, 4, j, h:h + 1]).then_inc(m_exp, 1)
                if h and j == 2:
                    copy_head(h - 1)
            copy_head(MH - 1)
            act.activation(root[:, 12:28], lin[:, 1, 0:16], ACT.Abs).then_inc(m_den, 1)
            for h in range(MH):
                act.wait_ge(gn_centered, h + 1)
                if h >= 2:
                    act.wait_ge(gn_var, h - 1)
                act.activation(tmp[:, h % 2, :], m_h[:, h, :], ACT.Square).then_inc(gn_square, 1)
            act.wait_ge(gn_var, MH)
            act.activation(root[:, 44:60], lin[:, 3, 0:16], ACT.Sqrt, scale=1.0 / P, bias=eps_col[:, 0:1])\
               .then_inc(gn_root, 1)

            act.activation(lora[0:64, 0, :], lora[0:64, 0, :], ACT.Tanh).then_inc(r_act, 1)
            act.activation(lora[:, 1:3, :], lora[:, 1:3, :], ACT.Sigmoid).then_inc(r_act, 1)
            for q in range(8):
                act.wait_ge(r_pre, q + 1)
                act.activation((sw, rate)[q % 2][:, q // 2, :], aux[:, q % 4, :], ACT.Sigmoid,
                               bias=col(("r_w0_2", "r_a0_2")[q % 2], q // 2)).then_inc(r_sig, 1)
            for p in range(4):
                if p >= 2:
                    act.wait_ge(kk_sum, p - 1)
                act.activation(tmp[:, p % 2, :], rkv[:, 4 + p, :], ACT.Square, scale=col("r_kk_2", p))\
                   .then_inc(kk_square, 1)
            act.wait_ge(kk_floor, 1)
            act.activation(root[:, 12:44], root[:, 12:44], ACT.Sqrt).then_inc(kk_root, 1)
            for half in range(2):
                for pl in range(2):
                    p = 2 * half + pl
                    if p == 0:
                        act.wait_ge(inv_ready, inverse_of("kk"))
                    if pl:
                        act.wait_ge(wide_ready, spread_of(f"kk {half}", 0))
                    if p == 2:
                        act.wait_ge(wide_ready, spread_of("y 0", 1))
                    repeat_pair(tmp[:, 0, :], 12 + 8 * p)
                    if p:
                        act.wait_ge(packed, p)
                    act.wait_ge(z_cum, p + 1)
                    act.activation(work[:, 2, :], work[:, 0, :], ACT.Exp, scale=-DECAY).then_inc(z_exp, 1)
                    act.activation(work[:, 3, :], work[:, 0, :], ACT.Exp, scale=DECAY).then_inc(z_exp, 1)
                    act.activation(work[:, 1, :], work[:, 1, :], ACT.Exp, scale=-DECAY).then_inc(z_exp, 1)
                for pl in range(2):
                    for b in range(2):
                        act.wait_ge(bt_turned, 4 * half + 2 * pl + b + 1)
                        act.activation(BKt[:, pl, 4 * b:4 * b + 4, :],
                                       aux[:, 2 * (pl % 2) + b, :].rearrange("p (c n) -> p c n", n=P), ACT.Copy)\
                           .then_inc(bt_done, 1)
                for pl in range(2):
                    act.wait_ge(x_first, 2 * half + pl + 1)
                    act.activation(X[pl], (aux, lin)[pl][half64, 2:4, :].rearrange("p a (u n) -> p (a u) n", n=CH),
                                   ACT.Copy).then_inc(x_copied, 1)
                for pl in range(2):
                    for b in range(2):
                        n = 4 * half + 2 * pl + b
                        act.wait_ge(uv_turned, n + 1)
                        act.activation(UV[64:128, 4 * b:4 * b + 4, 2 * pl:2 * pl + 2, :],
                                       aux[64:128, 2 * pl + b, :].rearrange("p (c g n) -> p c g n", c=4, g=2), ACT.Copy)\
                           .then_inc(uv_done, 1)
                for c in range(NC):
                    n = NC * half + c
                    act.wait_ge(u_sum, n + 1)
                    act.activation(UV[0:64, c, :, :], aux[0:64, 1, 0:256].rearrange("p (g n) -> p g n", n=CH), ACT.Copy)\
                       .then_inc(u_taken, 1)
                for pl in range(2):
                    p = 2 * half + pl
                    act.wait_ge(y_sum, NC * (half + 1))
                    act.activation(y_sb[:, pl, :], lin[:, pl, :], ACT.Copy).then_inc(y_copied, 1)
                for pl in range(2):
                    p = 2 * half + pl
                    act.wait_ge(y_centered, p + 1)
                    act.activation(tmp[:, pl, :], y_sb[:, pl, :], ACT.Square).then_inc(y_square, 1)
                act.wait_ge(y_var, 2 * half + 2)
                act.activation(root[:, 44:60], aux[:, 1, 0:16], ACT.Sqrt, scale=1.0 / CH, bias=eps_col[:, 1:2])\
                   .then_inc(y_root, 1)
                act.wait_ge(inv_ready, inverse_of(f"y {half}"))
                for pl in range(2):
                    repeat_pair(tmp[:, pl, :], 44 + 8 * pl)
            if stop:
                act_linear(mix_out_l)
                return
            act_mem_load(act)

            act.wait_ge(mem_summed, 1)
            act.activation(root[:, 8:10], aux[:, 2, 0:2], ACT.Sqrt, scale=1.0 / D, bias=eps_col[:, 0:1])\
               .then_inc(mem_root, 1)
            act_linear(mix_out_l, unroll=True)

        def pe_mix(pe):
            pe_norm(2)
            pe_linear(m_qk_l, act_hi, act_lo, (act_ready, 2 * KT))
            pe_linear(m_vo_l, act_hi, act_lo)
            pe_linear(rkv_l, act_hi, act_lo)
            pe_linear(lora_l, act_hi, act_lo)
            pe_linear(m_gate_l, act_hi, act_lo)
            turn_eight(2)
            for b in range(TB):
                if b >= 2:
                    pe.wait_ge(v_done, TB + b - 1)
                for t in range(4):
                    last = pe.transpose(aux[:, 2 + b % 2, t * P:(t + 1) * P], m_v[:, t, b * P:(b + 1) * P], ident[:, :])
                last.then_inc(v_turned, 1)
            pe.wait_ge(f_ready, 2)
            for b in range(TB):
                for a in range(b + 1):
                    last = pe.matmul(aux[:, 0, 8 * b:8 * b + 8], upto[:, :] if a == b else ones[:, :], mg[:, 3, a, :],
                                     start=(a == 0), stop=(a == b))
            last.then_inc(f_sum, 1)
            pe.wait_ge(v_done, TB + TB)
            pe.wait_ge(u_ready, 2)
            for kind in range(2):
                for b in range(TB):
                    last = pe.transpose(aux[0:MH, 2 + kind, b * P:(b + 1) * P], mg[:, 4, b, MH * kind:MH * kind + MH],
                                        ident[:, :])
            last.then_inc(u_turned, 1)
            pe.wait_ge(rows_ready, 1)
            pe.wait_ge(m_silu, 8)
            every_tile_taken(pe, m_gate_l)
            for b in range(TB):
                last = pe.transpose(lin[:, 3, MH * b:MH * b + MH], rows[:, 0, b * P:(b + 1) * P], ident[0:MH, 0:MH])
            last.then_inc(em_turned, 1)

            def weigh(n):
                h, j = n // TB, n % TB
                pe.wait_ge(m_p, n + 1)
                if j == 0 and h >= 2:
                    pe.wait_ge(m_head, h - 1)
                to = lin[:, 2 * (h % 2), j * P:T]
                last = pe.matmul(to, m_vtok[:, j, h * P:(h + 1) * P], ptT[:, n % 4, 0:T - j * P], start=(j == 0),
                                 stop=(j == TB - 1))
                if j == TB - 1:
                    for b in range(TB):
                        for a in range(b + 1):
                            last = pe.matmul(lin[:, 1, TB * h + b:TB * h + b + 1], ptT[:, a, (b - a) * P:(b - a + 1) * P],
                                             ones[:, 0:1], start=(a == 0), stop=(a == b))
                last.then_inc(m_pv, 1)

            for n in range(MH * TB):
                h, j = n // TB, n % TB
                w = T - j * P
                if n >= 2:
                    pe.wait_ge(m_exp, n - 1)
                pe.matmul(aux[:, 2 + n % 2, 0:w], ident[0:MH, h:h + 1].broadcast_to([MH, P]), rows[:, 1, T - w:T],
                          start=True, stop=False)
                pe.matmul(aux[:, 2 + n % 2, 0:P], later_key[:, :], ident[:, :], start=False, stop=True)\
                  .then_inc(m_e, 1)
                if n >= 2:
                    pe.wait_ge(m_p, n - 1)
                pe.matmul(aux[:, n % 2, 0:w], m_qk[:, 4 + h, j * P:(j + 1) * P], m_qk[:, h, j * P:T], start=True,
                          stop=True).then_inc(m_s, 1)
                if n >= 2:
                    weigh(n - 2)
            weigh(MH * TB - 2)
            weigh(MH * TB - 1)
            pe.wait_ge(inv_ready, inverse_of("m"))
            for h in range(MH + 1):
                if h < MH:
                    if h >= 2:
                        pe.wait_ge(m_normed, h - 1)
                    spread_tokens(aux[:, h % 2, :], 12 + TB * h)
                if h:
                    pe.wait_ge(m_normed, h)
                    if h >= 3:
                        pe.wait_ge(gn_centered, h - 2)
                    pe.matmul(aux[:, 2 + (h - 1) % 2, :], ones[:, :], m_h[:, h - 1, :], start=True, stop=True)\
                      .then_inc(gn_mean, 1)
            for h in range(MH):
                pe.wait_ge(gn_square, h + 1)
                token_sums(lin[:, 3, TB * h:TB * (h + 1)], tmp[:, h % 2, :]).then_inc(gn_var, 1)
            pe.wait_ge(inv_ready, inverse_of("gn"))
            for h in range(MH):
                if h >= 2:
                    pe.wait_ge(gn_done, h - 1)
                spread_tokens(aux[:, h % 2, :], 44 + TB * h)

            pe.wait_ge(gn_done, MH)
            pe.wait_ge(r_act, 2)
            for q in range(8):
                rws = slice(64 * (q % 2), 64 * (q % 2) + 64)
                if q >= 4:
                    pe.wait_ge(r_sig, q - 3)
                pe.matmul(aux[:, q % 4, :], up_w[rws, q // 2 * P:(q // 2 + 1) * P], lora[rws, 0, :], start=True,
                          stop=True).then_inc(r_pre, 1)
            pe.wait_ge(r_sig, 8)
            for p in range(4):
                pe.wait_ge(kk_square, p + 1)
                token_sums(aux[:, 1, 8 * p:8 * p + 8], tmp[:, p % 2, :], 2).then_inc(kk_sum, 1)
            for half in range(2):
                for pl in range(2):
                    p = 2 * half + pl
                    pe.wait_ge(pairs_ready, pairs_of(f"kk {half}", pl))
                    if p == 2:
                        pe.wait_ge(mix_ready, 6)
                    if pl:
                        pe.wait_ge(packed, p)
                    spread_pair(aux[:, 0, :], tmp[:, 0, :])
                    pe.wait_ge(bonus_in, p + 1)
                    pe.matmul(aux[:, 1, :], halves[:, :], tmp[:, 1, :], start=True, stop=True).then_inc(bonus_sum, 1)
                for pl in range(2):
                    pe.wait_ge(bonus_done, 2 * half + 2)
                    for b in range(2):
                        for c in range(4):
                            last = pe.transpose(aux[:, 2 * pl + b, c * P:(c + 1) * P],
                                                BK[:, pl, 4 * b + c, :, :].rearrange("p a b -> p (a b)"), ident[:, :])
                        last.then_inc(bt_turned, 1)
                for pl in range(2):
                    if pl:
                        pe.wait_ge(g_masked, 4 * (2 * half + 1))
                    for hh in range(2):
                        rws = slice(64 * hh, 64 * hh + 64)
                        for b in range(2):
                            for c in range(4):
                                last = pe.matmul(lin[:, 2 * hh + b, c * P:(c + 1) * P],
                                                 BK[rws, pl, 4 * b + c, :, :].rearrange("p a b -> p (a b)"),
                                                 RK[rws, pl, 4 * b + c, :, :].rearrange("p a b -> p (a b)"),
                                                 start=True, stop=True)
                            last.then_inc(g_built, 1)
                bank = (aux, lin)
                pe.wait_ge(bt_done, 4 * (half + 1))

                def units(pl, first, lhs, rhs):
                    for u in range(16):
                        last = pe.matmul(bank[pl][half64, first + u // 8, u % 8 * CH:(u % 8 + 1) * CH], lhs(u), rhs(u),
                                         start=True, stop=True)
                    return last

                for pl in range(2):
                    pe.wait_ge(xt_first, 2 * half + pl + 1)
                    units(pl, 2, lambda u: XT[pl][:, u, :], lambda u: ident[half64, 0:CH]).then_inc(x_first, 1)
                for m in range(5):
                    for pl in range(2):
                        n = (5 * half + m) * 2 + pl
                        if m == 0:
                            pe.wait_ge(x_copied, 2 * half + pl + 1)
                        else:
                            pe.wait_ge(iv_xd, (4 * half + m - 1) * 2 + pl + 1)
                            pe.wait_ge(iv_xtd, n - 1)
                        units(pl, 0, lambda u: G[half64, pl, u // NC, u % NC, CH:2 * CH], lambda u: X[pl][:, u, :])\
                            .then_inc(iv_y, 1)
                    for pl in range(2):
                        n = (5 * half + m) * 2 + pl
                        pe.wait_ge(iv_t, n + 1)
                        if m < 4:
                            units(pl, 2, lambda u: XT[pl][:, u, :], lambda u: T1(half, pl)[:, u, :]).then_inc(iv_x, 1)
                        units(pl, 0, lambda u: T1(half, pl)[:, u, :], lambda u: XT[pl][:, u, :]).then_inc(iv_xt, 1)
                pe.wait_ge(iv_xtd, 10 * (half + 1))
                for pl in range(2):
                    for b in range(2):
                        for c in range(4):
                            at = (8 + 2 * half + pl) * T + (4 * b + c) * CH - CH
                            last = pe.transpose(aux[:, 2 * pl + b, c * P:(c + 1) * P], mix[:, at:at + P], ident[:, :])
                        last.then_inc(uv_turned, 1)
                pe.wait_ge(uv_zero, half + 1)
                pe.wait_ge(uv_done, 4 * (half + 1))
                for c in range(NC):
                    n = NC * half + c
                    s_now = state[:, c % 2, :, :]
                    if c:
                        pe.wait_ge(s_new, (NC + 1) * half + c + 1)
                    else:
                        pe.wait_ge(s_new, (NC + 1) * half + 1)
                    for g in range(4):
                        pl, hh = g // 2, g % 2
                        to = aux[half64, 0, g * CH:(g + 1) * CH]
                        pe.matmul(to, RK[:, pl, c, 1, :], s_now[:, g, :], start=True, stop=False)
                        last = pe.matmul(to, G[:, pl, hh, c, CH:2 * CH], UV[:, c, g, :], start=False, stop=True)
                    last.then_inc(w_sum, 1)
                    pe.wait_ge(w_taken, n + 1)
                    for g in range(4):
                        pl, hh = g // 2, g % 2
                        last = pe.matmul(aux[half64, 1, g * CH:(g + 1) * CH], G[half64, pl, hh, c, CH:2 * CH],
                                         w_sb(half)[:, g, :], start=True, stop=True)
                    last.then_inc(u_sum, 1)
                    pe.wait_ge(u_taken, n + 1)
                    for g in range(4):
                        last = pe.matmul(aux[:, 2, g * CH:(g + 1) * CH], BKt[:, g // 2, c, :], UV[:, c, g, :],
                                         start=True, stop=True)
                    last.then_inc(s_sum, 1)
                    for g in range(4):
                        pl, hh = g // 2, g % 2
                        to = lin[64 * hh:64 * hh + 64, pl, c * CH:(c + 1) * CH]
                        pe.matmul(to, s_now[:, g, :], RK[:, pl, c, 0, :], start=True, stop=False)
                        last = pe.matmul(to, UV[:, c, g, :], G[:, pl, hh, c, 0:CH], start=False, stop=True)
                    last.then_inc(y_sum, 1)
                pe.wait_ge(s_new, (NC + 1) * (half + 1))
                for pl in range(2):
                    p = 2 * half + pl
                    pe.wait_ge(y_copied, p + 1)
                    if pl:
                        pe.wait_ge(y_centered, p)
                    pe.matmul(aux[:, 0, :], halves[:, :], y_sb[:, pl, :], start=True, stop=True).then_inc(y_mean, 1)
                for pl in range(2):
                    p = 2 * half + pl
                    pe.wait_ge(y_square, p + 1)
                    token_sums(aux[:, 1, 8 * pl:8 * pl + 8], tmp[:, pl, :], 2).then_inc(y_var, 1)
                    pe.matmul(aux[:, 2 + pl, :], up_g[:, 0, p * P:(p + 1) * P], lora[:, 1, :], start=True, stop=False)
                    pe.matmul(aux[:, 2 + pl, :], up_g[:, 1, p * P:(p + 1) * P], lora[:, 2, :], start=False, stop=True)\
                      .then_inc(y_gate, 1)
                pe.wait_ge(y_root, half + 1)
                for pl in range(2):
                    pe.wait_ge(pairs_ready, pairs_of(f"y {half}", pl))
                    spread_pair(aux[:, pl, :], tmp[:, pl, :])
            pe.wait_ge(mix_ready, KT)
            if not stop:
                pe_mem(pe)
            pe_linear(mix_out_l, act_hi, act_lo)

        def pool_masks(pool, step):
            every_tile_taken(pool, ffn_out_l)
            step(pool.memset(up_g[:, 1, :], 0.0))
            pool.memset(eps_col[:, 1:2], GN_EPS)
            for r in (0, 64):
                rws = slice(r, r + 64)
                pool.tensor_copy(g_mask[rws, 0:CH], upto[rws, r:r + CH])
                step(pool.tensor_copy(g_mask[rws, CH:2 * CH], before[rws, r:r + CH]))
            for m in range(6):
                b = 1 << m
                lev = level[:, m, :]
                step(pool.memset(lev, 0.0))
                v = lev.rearrange("p (g w) -> p g w", w=2 * b)
                cols = v[:, :, b:2 * b] if m == 0 else v[:, :, 0:b]
                step(pool.memset(cols, 1.0))
                first = 0 if m == 0 else b
                n = CH // (2 * b)
                step(pool.affine_select(out=cols, in_=cols, compare_op=ALU.is_ge, fill=0.0, base=-first,
                                        pattern=[[-2 * b, n], [0, b]], channel_multiplier=1))
                ins = pool.affine_select(out=cols, in_=cols, compare_op=ALU.is_ge, fill=0.0, base=first + b - 1,
                                         pattern=[[2 * b, n], [0, b]], channel_multiplier=-1)
                step(ins)
            pool.nop().then_inc(masks_ready, 1)

        def T1(half, pl):
            return part((7680, 9728)[pl] + 1024 * half, 16, CH, rows=half64)

        def w_sb(half):
            return part(7680 + 1024 * half, 4, CH, rows=half64)

        def dve_mix(dve, step):
            dve_norm(2, "norm_mix_2", step)
            for q in range(8):
                slab_ready(dve, m_qk_l, q // 4, q // 2 % 2)
                tile_taken(dve, m_qk_l, q // 4, q // 2 % 2, q % 2)
                for j in range(4):
                    tap = tab[:, 2, 8 * j + q:8 * j + q + 1]
                    if j == 0:
                        step(dve.tensor_scalar(m_qk[:, q, :], pad[:, q % 2, 0:T], tap, col("m_conv_b_2", q), ALU.mult,
                                               ALU.add))
                    else:
                        ins = dve.scalar_tensor_tensor(m_qk[:, q, :], pad[:, q % 2, j:j + T], tap, m_qk[:, q, :],
                                                       ALU.mult, ALU.add)
                        if j < 3:
                            step(ins)
                ins.then_inc(m_conv, 1)
            for q in range(15):
                layer, i, s, t = (rkv_l, q // 4, q // 2 % 2, q % 2) if q < 12 else (lora_l, 0, (q - 12) // 2,
                                                                                   (q - 12 + 1) // 2)
                slab_ready(dve, layer, i, s)
                tile_taken(dve, layer, i, s, t)
                to = rkv[:, q, :] if q < 12 else lora[:, q - 12, :]
                mu = col("r_mu_2", q) if q < 14 else col("r_mu_tail", 0)
                step(dve.tensor_tensor(tmp[:, q % 2, :], pad[:, q % 2, 2:2 + T], pad[:, q % 2, 3:3 + T], ALU.subtract))
                dve.scalar_tensor_tensor(to, tmp[:, q % 2, :], mu, pad[:, q % 2, 3:3 + T], ALU.mult, ALU.add)\
                   .then_inc(r_shift, 1)
            dve.wait_ge(f_logits, 2)
            dve.tensor_tensor(mg[:, 0, :, :], aux[:, 1, 0:32].rearrange("p (b h) -> p b h", h=8),
                              f_bias[:, 1:2, :].broadcast_to([P, TB, 8]), ALU.add).then_inc(f_biased, 1)
            dve.wait_ge(f_ln, 2)
            dve.scalar_tensor_tensor(mg[:, 3, :, :], mg[:, 0, :, :], 0.0, mg[:, 1, :, :], ALU.min, ALU.subtract)\
               .then_inc(f_ready, 1)
            dve.wait_ge(f_sum, 2)
            b_sum = aux[:, 0, 0:32].rearrange("p (b h) -> p b h", h=8)[:, :, MH:2 * MH]
            dve.tensor_tensor(mg[:, 4, :, 0:MH], mg[:, 0, :, 0:MH], b_sum, ALU.subtract).then_inc(u_ready, 1)
            dve.tensor_copy(mg[:, 4, :, MH:2 * MH], b_sum).then_inc(u_ready, 1)
            dve.wait_ge(u_turned, 1)
            step(dve.tensor_copy(rows[:, 0, :], aux[0:MH, 2, :]))
            step(dve.tensor_tensor_scan(rows[:, 1, :], rows[:, 0, :], rows[:, 0, :], -3.0e38, ALU.max, ALU.max))
            step(dve.scalar_tensor_tensor(rows[:, 0, :], aux[0:MH, 3, :], -1.0, rows[:, 1, :], ALU.mult, ALU.subtract))
            dve.tensor_scalar(rows[:, 1, :], rows[:, 1, :], -1.0, None, ALU.mult).then_inc(rows_ready, 1)
            for n in range(MH * TB):
                h, w = n // TB, T - n % TB * P
                dve.wait_ge(m_s, n + 1)
                dve.wait_ge(m_exp, n + 1)
                if n >= 4:
                    dve.wait_ge(m_pv, TB * h)
                dve.scalar_tensor_tensor(ptT[:, n % 4, 0:w], aux[:, n % 2, 0:w], float(P) ** -0.5,
                                         decay_e[:, n % 2, 0:w], ALU.mult, ALU.mult).then_inc(m_p, 1)
            dve.wait_ge(m_den, 1)
            step(dve.tensor_tensor(root[:, 12:28].rearrange("p (h b) -> p h b", h=MH),
                                   root[:, 12:28].rearrange("p (h b) -> p h b", h=MH),
                                   root[:, 28:44].rearrange("p (b h) -> p h b", h=MH), ALU.max))
            dve.reciprocal(inv[:, 12:28], root[:, 12:28]).then_inc(inv_ready, 1)
            dve.wait_ge(m_head, MH)
            for h in range(MH + 1):
                if h < MH:
                    dve.wait_ge(wide_ready, spread_of("m", h))
                    dve.tensor_tensor(m_h[:, h, :], aux[:, h % 2, :], m_h[:, h, :], ALU.mult).then_inc(m_normed, 1)
                if h:
                    dve.wait_ge(gn_mean, h)
                    dve.scalar_tensor_tensor(m_h[:, h - 1, :], aux[:, 2 + (h - 1) % 2, :], -1.0 / P, m_h[:, h - 1, :],
                                             ALU.mult, ALU.add).then_inc(gn_centered, 1)
            dve.wait_ge(gn_centered, MH)
            for h in range(MH):
                ins = dve.scalar_tensor_tensor(m_o[:, h, :], m_h[:, h, :], col("m_norm_g_2", h), m_o[:, h, :], ALU.mult,
                                               ALU.mult)
            step(ins)
            dve.wait_ge(gn_root, 1)
            dve.reciprocal(inv[:, 44:60], root[:, 44:60]).then_inc(inv_ready, 1)
            for h in range(MH):
                dve.wait_ge(wide_ready, spread_of("gn", h))
                step(dve.tensor_tensor(act_hi[:, h, :], aux[:, h % 2, :], m_o[:, h, :], ALU.mult))
                step(dve.tensor_tensor(m_o[:, h, :], aux[:, h % 2, :], m_o[:, h, :], ALU.mult))
                dve.nop().then_inc(gn_done, 1)
                dve.tensor_tensor(act_lo[:, h, :], m_o[:, h, :], act_hi[:, h, :].bitcast(F32), ALU.subtract)\
                   .then_inc(mix_ready, 1)

            dve.wait_ge(r_sig, 8)
            dve.wait_ge(masks_ready, 1)
            dve.wait_ge(kk_sum, 4)
            dve.tensor_scalar(root[:, 12:44], aux[:, 1, 0:32], 1e-24, None, ALU.max).then_inc(kk_floor, 1)
            dve.wait_ge(kk_root, 1)
            dve.reciprocal(inv[:, 12:44], root[:, 12:44]).then_inc(inv_ready, 1)
            for half in range(2):
                step(dve.memset(end_decay, 0.0))
                for pl in range(2):
                    p = 2 * half + pl
                    r, k, v = rkv[:, p, :], rkv[:, 4 + p, :], rkv[:, 8 + p, :]
                    chunks = lambda ap: ap.rearrange("p (c n) -> p c n", n=CH)
                    if p:
                        dve.wait_ge(z_exp, 3 * p)
                    for c in range(NC):
                        cs = slice(c * CH, (c + 1) * CH)
                        ins = dve.tensor_tensor_scan(work[:, 0, cs], ones[:, 0:CH], sw[:, p, cs], 0.0, ALU.mult, ALU.add)
                    step(ins)
                    dve.tensor_tensor(work[:, 1, :], work[:, 0, :], sw[:, p, :], ALU.subtract).then_inc(z_cum, 1)
                    dve.wait_ge(wide_ready, spread_of(f"kk {half}", pl))
                    step(dve.scalar_tensor_tensor(work[:, 4, :], k, col("r_kk_2", p), aux[:, 0, :], ALU.mult, ALU.mult))
                    step(dve.tensor_scalar(work[:, 5, :], rate[:, p, :], -1.0, col("r_ka_2", p), ALU.add, ALU.mult))
                    step(dve.scalar_tensor_tensor(k, work[:, 5, :], 1.0, k, ALU.add, ALU.mult))
                    dve.scalar_tensor_tensor(tmp[:, 1, :], r, col("r_rk_2", p), k, ALU.mult, ALU.mult)\
                       .then_inc(bonus_in, 1)
                    step(dve.tensor_tensor(work[:, 5, :], work[:, 4, :], rate[:, p, :], ALU.mult))
                    dve.wait_ge(z_exp, 3 * p + 3)
                    dve.tensor_tensor(RK[:, pl, :, 0, :], chunks(r), chunks(work[:, 2, :]), ALU.mult)
                    dve.tensor_tensor(RK[:, pl, :, 1, :], chunks(work[:, 4, :]), chunks(work[:, 1, :]), ALU.mult)
                    dve.tensor_tensor(BK[:, pl, :, 0, :], chunks(work[:, 5, :]), chunks(work[:, 3, :]), ALU.mult)
                    dve.tensor_tensor(BK[:, pl, :, 1, :], chunks(k), chunks(work[:, 3, :]), ALU.mult)
                    for hh in range(2):
                        rws = slice(64 * hh, 64 * hh + 64)
                        ins = dve.tensor_copy(end_decay[rws, :, 2 * pl + hh], chunks(work[rws, 2, :])[:, :, CH - 1])
                    ins.then_inc(packed, 1)
                    dve.wait_ge(packed, p + 1)
                    dve.wait_ge(bonus_sum, p + 1)
                    dve.tensor_tensor(r, aux[:, 1, :], v, ALU.mult).then_inc(bonus_done, 1)
                for pl in range(2):
                    for hh in range(2):
                        for b in range(2):
                            dve.wait_ge(g_built, 4 * (2 * half + pl) + 2 * hh + b + 1)
                            dve.tensor_tensor(G[:, pl, hh, 4 * b:4 * b + 4, :],
                                              lin[:, 2 * hh + b, :].rearrange("p (c n) -> p c n", n=P),
                                              g_mask.unsqueeze(1).broadcast_to([P, 4, P]), ALU.mult)\
                               .then_inc(g_masked, 1)
                dve.wait_ge(g_masked, 8 * (half + 1))
                wide = lambda ap: ap.unsqueeze(1).broadcast_to([CH, 16, CH])
                for pl in range(2):
                    lbt = G[half64, pl, :, :, CH:2 * CH].rearrange("p a c n -> p (a c) n")
                    step(dve.tensor_tensor(XT[pl], lbt, wide(level[:, 0, :]), ALU.mult))
                    dve.tensor_tensor(XT[pl], wide(ident[half64, 0:CH]), XT[pl], ALU.subtract).then_inc(xt_first, 1)
                bank = (aux, lin)
                banks = lambda pl, a: bank[pl][half64, a:a + 2, :].rearrange("p a (u n) -> p (a u) n", n=CH)
                for m in range(5):
                    for pl in range(2):
                        n = (5 * half + m) * 2 + pl
                        dve.wait_ge(iv_y, n + 1)
                        dve.tensor_tensor(T1(half, pl), banks(pl, 0), wide(level[:, m + 1, :]), ALU.mult)\
                           .then_inc(iv_t, 1)
                    for pl in range(2):
                        n = (5 * half + m) * 2 + pl
                        if m < 4:
                            dve.wait_ge(iv_x, (4 * half + m) * 2 + pl + 1)
                            dve.tensor_tensor(X[pl], X[pl], banks(pl, 2), ALU.subtract).then_inc(iv_xd, 1)
                        dve.wait_ge(iv_xt, n + 1)
                        if m < 4:
                            dve.tensor_tensor(XT[pl], XT[pl], banks(pl, 0), ALU.subtract).then_inc(iv_xtd, 1)
                        else:
                            lbt = G[half64, pl, :, :, CH:2 * CH].rearrange("p a c n -> p (a c) n")
                            dve.tensor_tensor(lbt, banks(pl, 0), XT[pl], ALU.subtract).then_inc(iv_xtd, 1)
                dve.wait_ge(iv_xtd, 10 * (half + 1))
                dve.memset(UV[0:64, :, :, :], 0.0).then_inc(uv_zero, 1)
                dve.memset(state[:, 0, :, :], 0.0).then_inc(s_new, 1)
                for c in range(NC):
                    n = NC * half + c
                    dve.wait_ge(w_sum, n + 1)
                    dve.tensor_copy(w_sb(half), aux[half64, 0, 0:256].rearrange("p (g n) -> p g n", n=CH))\
                       .then_inc(w_taken, 1)
                    dve.wait_ge(s_sum, n + 1)
                    if c:
                        dve.wait_ge(y_sum, n)
                    nxt = state[:, (c + 1) % 2, :, :]
                    step(dve.tensor_tensor(nxt, state[:, c % 2, :, :],
                                           aux[:, 2, 0:256].rearrange("p (g n) -> p g n", n=CH), ALU.add))
                    dve.tensor_tensor(nxt, nxt, end_decay[:, c, :].unsqueeze(2).broadcast_to([P, 4, CH]), ALU.mult)\
                       .then_inc(s_new, 1)
                    dve.wait_ge(s_new, (NC + 1) * half + c + 2)
                for pl in range(2):
                    p = 2 * half + pl
                    dve.wait_ge(y_mean, p + 1)
                    dve.scalar_tensor_tensor(y_sb[:, pl, :], aux[:, 0, :], -1.0 / CH, y_sb[:, pl, :], ALU.mult, ALU.add)\
                       .then_inc(y_centered, 1)
                dve.wait_ge(y_root, half + 1)
                dve.reciprocal(inv[:, 44:60], root[:, 44:60]).then_inc(inv_ready, 1)
                for pl in range(2):
                    p = 2 * half + pl
                    y = y_sb[:, pl, :]
                    dve.wait_ge(wide_ready, spread_of(f"y {half}", pl))
                    step(dve.scalar_tensor_tensor(y, y, col("r_gn_g_2", p), aux[:, pl, :], ALU.mult, ALU.mult))
                    step(dve.scalar_tensor_tensor(y, y, col("r_gn_b_2", p), rkv[:, p, :], ALU.add, ALU.add))
                    dve.wait_ge(y_gate, p + 1)
                    step(dve.tensor_tensor(act_hi[:, 4 + p, :], aux[:, 2 + pl, :], y, ALU.mult))
                    step(dve.tensor_tensor(y, aux[:, 2 + pl, :], y, ALU.mult))
                    dve.tensor_tensor(act_lo[:, 4 + p, :], y, act_hi[:, 4 + p, :].bitcast(F32), ALU.subtract)\
                       .then_inc(mix_ready, 1)

        (mem_in, mem_turned, mem_done, mem_added, mem_summed, mem_root, mem_ready) = (sem(n) for n in (
            "mem_in", "mem_turned", "mem_done", "mem_added", "mem_summed", "mem_root", "mem_ready"))
        f_conv, f_silu, y_ready, y_turned, rows_act, rows_dve = (sem(n) for n in (
            "f_conv", "f_silu", "y_ready", "y_turned", "rows_act", "rows_dve"))
        XSTEPS = XH * TB
        XB = HEADS * TB

        def act_mem_load(act):
            act.wait_ge(mix_ready, KT)
            act.dma_start(mem_rows[:, :, :], d["mem_2"].rearrange("o (b p) c -> p (o b) c", p=P)).then_inc(mem_in, 16)

        def act_rest(act, step):
            act_norm_square(3, mix_out_l)

            def take_kv(i, s):
                slab_ready(act, xkv_l, i, s)
                for t in range(2):
                    act.activation(kv_x[:, 4 * i + 2 * s + t, :], lin[:, 2 * s + t, 0:M_TOK], ACT.Copy)\
                       .then_inc(bank_free[s], 1)

            def take_q(i, s):
                slab_ready(act, xq_l, i, s)
                for t in range(2):
                    act.activation(q_x[:, 4 * i + 2 * s + t, :], lin[:, 2 * s + t, :], ACT.Copy)\
                       .then_inc(bank_free[s], 1)

            act_linear(xkv_l, take_kv, unroll=True)
            act_norm_root(3)
            act_norm_high(3)
            act_linear(xq_l, take_q, unroll=True)
            for g in range(4):
                act.wait_ge(v_turned, 2 * TB + g + 1)
                act.activation(v_xtok[:, g // 2, g % 2 * 512:(g % 2 + 1) * 512], aux[:, g, :], ACT.Copy)\
                   .then_inc(v_done, 1)

            def turned(n):
                h, i = n // TB, n % TB
                act.wait_ge(p_turned, XB + n + 1)
                if h >= 2:
                    act.wait_ge(o_ready, HEADS + 2 * (h - 1))
                act.activation(x_pT[:, h % 2, :, i * P:(i + 1) * P],
                               aux[:, 2 + n % 2, 0:2 * P].rearrange("p (m q) -> p m q", m=2), ACT.Copy)\
                   .then_inc(p_copied, 1)

            for n in range(XSTEPS):
                act.wait_ge(s_max, XB + n + 1)
                if n >= 4:
                    act.wait_ge(p_turned, XB + n - 3)
                step(act.activation(x_s[:, n % 4, :], aux[:, n % 2, 0:M_TOK], ACT.Exp, bias=x_stat[:, 1, n % 4:n % 4 + 1],
                                    scale=XHD ** -0.5, accum_out=x_stat[:, 2, n % 4:n % 4 + 1]))
                act.nop().then_inc(s_exp, 1)
                if n >= LAG:
                    turned(n - LAG)
            for n in range(XSTEPS - LAG, XSTEPS):
                turned(n)
            act_linear(xo_l)
            act_norm(4, xo_l)
            step(act.activation(gpad[:, :, 0:2], ident[:, 0:4].rearrange("p (a b) -> p a b", a=2), ACT.Copy, scale=0.0))

            def take_up(i, s):
                if s == 0:
                    slab_ready(act, up_l, i, 0)
                    for t in range(2):
                        tile_taken(act, up_l, i - 1, 1, t)
                        act.activation(gpad[:, t, 2:2 + T], lin[:, t, :], ACT.Copy).then_inc(bank_free[0], 1)
                else:
                    for t in range(2):
                        act.wait_ge(f_conv, 2 * i + t + 1)
                        act.activation(gconv[:, t, :], gconv[:, t, :], ACT.Silu).then_inc(f_silu, 1)

            act_linear(up_l, take_up)
            act_linear(down_l)
            act_norm_square(5, down_l)
            act_norm_root(5)
            for n in range(0, 8, 2):
                act.wait_ge(y_turned, n + 1)
                act.activation(out_rows[:, n % 4, n // 4 * 512:(n // 4 + 1) * 512], (lin, aux)[n // 4][:, n % 4, :],
                               ACT.Copy).then_inc(rows_act, 1)

        def pe_mem(pe):
            pe.wait_ge(mem_in, 16)
            for k in range(0, KT, 2):
                if k >= 4:
                    pe.wait_ge(mem_done, k // 2 - 1)
                for j in range(4):
                    last = pe.transpose(aux[:, k // 2 % 2, j * P:(j + 1) * P],
                                        mem_rows[:, j % 2, (k + j // 2) * P:(k + j // 2 + 1) * P], ident[:, :])
                last.then_inc(mem_turned, 1)
            pe.wait_ge(mem_added, KT)
            token_sums(aux[:, 2, :], rms_inv[:, 0:M_TOK]).then_inc(mem_summed, 1)
            pe.wait_ge(inv_ready, inverse_of("mem"))
            spread_tokens(aux[:, 3, :], 8, blocks=2)

        def pe_rest(pe):
            pe.wait_ge(mem_ready, KT)
            pe_linear(xkv_l, mem_hi, mem_lo)
            pe_norm(3)
            pe_linear(xq_l, act_hi, act_lo, (act_ready, 3 * KT))
            every_tile_taken(pe, xkv_l)
            for g in range(4):
                for j in range(4):
                    last = pe.transpose(aux[:, g, j * P:(j + 1) * P],
                                        kv_x[:, 8 + g % 2 * 4 + j, g // 2 * P:(g // 2 + 1) * P], ident[:, :])
                last.then_inc(v_turned, 1)
            every_tile_taken(pe, xq_l)

            def turn(n):
                h, i = n // TB, n % TB
                pe.wait_ge(s_diag, XB + n + 1)
                if n >= 2:
                    pe.wait_ge(p_copied, XB + n - 1)
                for m in range(2):
                    last = pe.matmul(aux[:, 2 + n % 2, m * P:(m + 1) * P], x_s[:, n % 4, m * P:(m + 1) * P],
                                     x_diag[:, n % 2, :], start=True, stop=True)
                last.then_inc(p_turned, 1)

            def x_values(h):
                pe.wait_ge(p_copied, XB + TB * (h + 1))
                if h >= 2:
                    pe.wait_ge(o_done, HEADS + 2 * (h - 1))
                for dt in range(2):
                    at = h * XHD + dt * P
                    for m in range(2):
                        last = pe.matmul(lin[:, 2 * (h % 2) + dt, :], v_xtok[:, m, at:at + P], x_pT[:, h % 2, m, :],
                                         start=(m == 0), stop=(m == 1))
                    last.then_inc(o_ready, 1)

            def x_scores(n):
                h, i = n // TB, n % TB
                if n >= 2:
                    pe.wait_ge(s_exp, XB + n - 1)
                else:
                    pe.wait_ge(v_done, 2 * TB + n + 1)
                for dt in range(2):
                    last = pe.matmul(aux[:, n % 2, 0:M_TOK], q_x[:, 2 * h + dt, i * P:(i + 1) * P], kv_x[:, 2 * h + dt, :],
                                     start=(dt == 0), stop=(dt == 1))
                last.then_inc(s_ready, 1)

            for n in range(XSTEPS + LAG + 1):
                if n < XSTEPS:
                    x_scores(n)
                if n == LAG:
                    pe.wait_ge(v_done, 2 * TB + 4)
                if LAG <= n < XSTEPS + LAG:
                    turn(n - LAG)
                if n > LAG and (n - LAG) % TB == 0:
                    x_values((n - LAG) // TB - 1)
            pe.wait_ge(o_done, HEADS + KT)
            pe_linear(xo_l, act_hi, act_lo)
            pe_norm(4)
            pe_linear(up_l, act_hi, act_lo, (act_ready, 4 * KT))
            pe_linear(down_l, hid2_hi, hid2_lo, (hid_ready, FT))
            pe_norm(5)
            every_tile_taken(pe, down_l)
            for n in range(8):
                k0, b = 4 * (n // 4), n % 4
                pe.wait_ge(y_ready, k0 + 4)
                for j in range(4):
                    last = pe.transpose((lin, aux)[n // 4][:, b, j * P:(j + 1) * P], y_fin[:, k0 + j, b * P:(b + 1) * P],
                                        ident[:, :])
                last.then_inc(y_turned, 1)

        def dve_mem(dve, step):
            for g in range(KT // 2):
                dve.wait_ge(mem_turned, g + 1)
                dve.tensor_copy(memT[:, 2 * g:2 * g + 2, :], aux[:, g % 2, :].rearrange("p (k m) -> p k m", k=2))\
                   .then_inc(mem_done, 1)
                dve.wait_ge(mem_done, g + 1)
                for k in (2 * g, 2 * g + 1):
                    if k == 0:
                        dve.tensor_tensor(rms_inv[:, 0:M_TOK], memT[:, k, :], memT[:, k, :], ALU.mult)\
                           .then_inc(mem_added, 1)
                    else:
                        step(dve.tensor_tensor(tmp[:, 0, 0:M_TOK], memT[:, k, :], memT[:, k, :], ALU.mult))
                        dve.tensor_tensor(rms_inv[:, 0:M_TOK], rms_inv[:, 0:M_TOK], tmp[:, 0, 0:M_TOK], ALU.add)\
                           .then_inc(mem_added, 1)
                    dve.wait_ge(mem_added, k + 1)
            dve.wait_ge(mem_root, 1)
            dve.reciprocal(inv[:, 8:10], root[:, 8:10]).then_inc(inv_ready, 1)
            dve.wait_ge(wide_ready, spread_of("mem"))
            for k in range(KT):
                step(dve.scalar_tensor_tensor(memT[:, k, :], memT[:, k, :], col("norm_mem_2", k), aux[:, 3, 0:M_TOK],
                                              ALU.mult, ALU.mult))
                step(dve.tensor_copy(mem_hi[:, k, :], memT[:, k, :]))
                dve.tensor_tensor(mem_lo[:, k, :], memT[:, k, :], mem_hi[:, k, :].bitcast(F32), ALU.subtract)\
                   .then_inc(mem_ready, 1)

        def dve_rest(dve, step):
            dve_norm(3, "norm_x_2", step)

            def divide(n):
                dve.wait_ge(s_exp, XB + n + 1)
                if n >= 2:
                    dve.wait_ge(p_turned, XB + n - 1)
                step(dve.reciprocal(x_stat[:, 0, n % 4:n % 4 + 1], x_stat[:, 2, n % 4:n % 4 + 1]))
                dve.tensor_scalar(x_diag[:, n % 2, :], ident[:, :], x_stat[:, 0, n % 4:n % 4 + 1], None, ALU.mult)\
                   .then_inc(s_diag, 1)

            def head_out(h):
                for dt in range(2):
                    k, bank = 2 * h + dt, lin[:, 2 * (h % 2) + dt, :]
                    dve.wait_ge(o_ready, HEADS + k + 1)
                    step(dve.tensor_copy(act_hi[:, k, :], bank))
                    dve.tensor_tensor(act_lo[:, k, :], bank, act_hi[:, k, :].bitcast(F32), ALU.subtract)\
                       .then_inc(o_done, 1)

            for n in range(XSTEPS):
                dve.wait_ge(s_ready, XB + n + 1)
                step(dve.tensor_reduce(x_stat[:, 0, n % 4:n % 4 + 1], aux[:, n % 2, 0:M_TOK], AX.X, ALU.max))
                dve.tensor_scalar(x_stat[:, 1, n % 4:n % 4 + 1], x_stat[:, 0, n % 4:n % 4 + 1], -XHD ** -0.5, None,
                                  ALU.mult).then_inc(s_max, 1)
                if n >= 2:
                    divide(n - 2)
                if n % TB == 1 and n // TB >= 2:
                    head_out(n // TB - 2)
            divide(XSTEPS - 2)
            divide(XSTEPS - 1)
            head_out(XH - 2)
            head_out(XH - 1)
            add_to_residual(xo_l)
            dve_norm(4, "norm_ffn_2", step)
            with dve.Fori(0, up_l.bodies) as i:
                step.enter(i, 6)
                for t in range(2):
                    tile_taken(dve, up_l, i, 0, t)
                    tap = lambda j: tab[:, 2, bass.ds(2 * i + (32 + FT * j + t), 1)]
                    step(dve.tensor_scalar(gconv[:, t, :], gpad[:, t, 0:T], tap(0), tap(3), ALU.mult, ALU.add))
                    step(dve.scalar_tensor_tensor(gconv[:, t, :], gpad[:, t, 1:1 + T], tap(1), gconv[:, t, :], ALU.mult,
                                                  ALU.add))
                    dve.scalar_tensor_tensor(gconv[:, t, :], gpad[:, t, 2:2 + T], tap(2), gconv[:, t, :], ALU.mult,
                                             ALU.add).then_inc(f_conv, 1)
                for t in range(2):
                    slab_ready(dve, up_l, i, 1)
                    dve.wait_ge(f_silu, 2 * i + t + 1)
                    at = 2 * i + t
                    step(dve.tensor_tensor(hid2_hi[:, bass.ds(at, 1), :], lin[:, 2 + t:3 + t, :], gconv[:, t:t + 1, :],
                                           ALU.mult))
                    dve.tensor_tensor(gconv[:, t, :], lin[:, 2 + t, :], gconv[:, t, :], ALU.mult).then_inc(bank_free[1], 1)
                    tile_taken(dve, up_l, i, 1, t)
                    dve.tensor_tensor(hid2_lo[:, bass.ds(at, 1), :], gconv[:, t:t + 1, :],
                                      hid2_hi[:, bass.ds(at, 1), :].bitcast(F32), ALU.subtract).then_inc(hid_ready, 1)
                    dve.wait_ge(hid_ready, FT + at + 1)
            step.leave(up_l.bodies)
            add_to_residual(down_l)
            dve_norm(5, "norm_final_2", step, to=y_fin)
            for n in range(1, 8, 2):
                dve.wait_ge(y_turned, n + 1)
                dve.tensor_copy(out_rows[:, n % 4, n // 4 * 512:(n // 4 + 1) * 512], (lin, aux)[n // 4][:, n % 4, :])\
                   .then_inc(rows_dve, 1)

        block = ctx.enter_context(nc.Block())

        @block.sync
        def _(sp):
            for t in range(2):
                sp.dma_start(x_rows[:, 2 * t:2 * t + 2, :],
                             d["x"].rearrange("o (b p) c -> p (o b) c", p=P)[:, 2 * t:2 * t + 2, :]).then_inc(x_in, 16)
            for layer in layers:
                stream(sp, layer)
            if stop:
                every_tile_taken(sp, layers[-1])
                sp.dma_start(out, xT[:, :, :]).then_inc(stored, 16)
                sp.wait_ge(stored, 16)
                return
            for n in range(8):
                sp.wait_ge((rows_act, rows_dve)[n % 2], n // 2 + 1)
                c = slice(n // 4 * 512, (n // 4 + 1) * 512)
                sp.dma_start(out.rearrange("o (b p) c -> p (o b) c", p=P)[:, n % 4, c], out_rows[:, n % 4, c])\
                   .then_inc(stored, 16)
            sp.wait_ge(stored, 16 * 8)

        @block.gpsimd
        def _(pool):
            step = Steps(pool, pool_step)
            pool.memset(raw_rows[:, :, :], 0.0).then_inc(rows_zero, 1)
            pool.memset(ident[:, :], 0.0)
            pool.memset(ones[:, :], 1.0)
            pool.memset(upto[:, :], 1.0)
            pool.memset(before[:, :], 1.0)
            pool.memset(later_key[:, :], 0.0)
            pool.memset(eps_col[:, 0:2], EPS)
            step(pool.memset(halves[:, :], 0.0))
            pool.sem_inc(w_low, RING)
            pool.memset(halves[0:64, 0:64], 1.0)
            step(pool.memset(halves[64:128, 64:128], 1.0))
            pool.affine_select(out=ident[:, :], in_=ident[:, :], compare_op=ALU.not_equal, fill=1.0, base=0,
                               pattern=[[-1, P]], channel_multiplier=1)
            pool.affine_select(out=upto[:, :], in_=upto[:, :], compare_op=ALU.is_ge, fill=0.0, base=0,
                               pattern=[[1, P]], channel_multiplier=-1)
            pool.affine_select(out=before[:, :], in_=before[:, :], compare_op=ALU.is_ge, fill=0.0, base=-1,
                               pattern=[[1, P]], channel_multiplier=-1)
            pool.affine_select(out=later_key[:, :], in_=later_key[:, :], compare_op=ALU.is_ge, fill=MASKED, base=0,
                               pattern=[[-1, P]], channel_multiplier=1).then_inc(consts, 1)
            for layer in layers[:9]:
                pool_linear(layer)
            if stop != "ffn":
                pool_masks(pool, step)
                for layer in layers[9:]:
                    pool_linear(layer)


        @block.scalar
        def _(act):
            step = Steps(act, act_step)
            act.wait_ge(rows_zero, 1)
            for name, (t, r, n) in place.items():
                if name == "r_mu_tail":
                    act.dma_start(raw_rows[r:r + 1, t, :], d["r_mu_2"][:, R_COLS - P:R_COLS]).then_inc(rows_in, 16)
                    continue
                src = d[name]
                if name in ("g_q", "g_k"):
                    for half in (0, 64):
                        act.dma_start(raw_rows[r:r + 1, t, half:half + 64], src).then_inc(rows_in, 16)
                    continue
                size = 1
                for m in src.shape:
                    size *= m
                flat = src.rearrange({1: "a -> a", 2: "a b -> (a b)", 3: "a b c -> (a b c)"}[len(src.shape)])
                full = n
                act.dma_start(raw_rows[r:r + full, t, :], flat[0:full * P].rearrange("(r c) -> r c", c=P))\
                   .then_inc(rows_in, 16)
            act.dma_start(f_bias[:, 0, :], d["b_forget"].broadcast_to([P, 8])).then_inc(small_in, 16)
            act.dma_start(f_bias[:, 1, :], d["m_gate_b_2"].broadcast_to([P, 8])).then_inc(small_in, 16)
            act.sem_inc(w_used, RING)
            act.sem_inc(bank_free[0], 2)
            act.sem_inc(bank_free[1], 2)
            act.wait_ge(tab_turned, 3)
            act.activation(tab[:, :, :], aux[:, 2, 0:3 * P], ACT.Copy).then_inc(tab_ready, 1)
            round_unit(layers[0], 0, 0)
            round_unit(layers[0], 0, 1)
            act_norm(0, None)

            def take_glu(i, s):
                if s == 1:
                    for t in range(2):
                        slab_ready(act, glu_l, i, s)
                        if i:
                            tile_taken(act, glu_l, i - 1, 0, t)
                        act.activation(tmp[:, t, :], lin[:, 2 + t, :], ACT.Sigmoid).then_inc(bank_free[1], 1)

            def take_qkv(i, s):
                slab_ready(act, qkv_l, i, s)
                for t in range(2):
                    act.activation(qkv[:, 4 * i + 2 * s + t, :], lin[:, 2 * (s % 2) + t, :], ACT.Copy)\
                       .then_inc(bank_free[s % 2], 1)

            def take_gate(i, s):
                slab_ready(act, gate_l, i, s)
                for t in range(2):
                    act.activation(sig[:, 4 * i + 2 * s + t, :], lin[:, 2 * (s % 2) + t, :], ACT.Sigmoid)\
                       .then_inc(bank_free[s % 2], 1)

            act_linear(glu_l, take_glu, unroll=True)
            act_linear(qkv_l, take_qkv, unroll=True)
            for t in range(8):
                act.activation(sig[:, t, :], qkv[:, t, :], ACT.Square).then_inc(qk_square, 1)
            act_linear(forget_l, take_eight(forget_l), unroll=True)
            act.wait_ge(qk_summed, 8)
            act.activation(root[:, 12:76], aux[:, 0, 0:64], ACT.Sqrt, scale=1.0 / HD, bias=eps_col[:, 0:1])\
               .then_inc(qk_root, 1)
            act_linear(gate_l, take_gate, unroll=True)

            act.wait_ge(f_biased, 1)
            step(act.activation(lf[:, 1, :, :], lf[:, 0, :, :], ACT.Abs))
            step(act.activation(lf[:, 2, :, :], lf[:, 1, :, :], ACT.Exp, scale=-1.0))
            act.activation(lf[:, 1, :, :], lf[:, 2, :, :], ACT.Ln, bias=ones[:, 0:1]).then_inc(f_ln, 1)
            for t in range(4):
                act.wait_ge(ln_centered, t + 1)
                act.activation(glu[:, t, 0:T], conv[:, t, :], ACT.Square).then_inc(ln_square, 1)

            def take_v(b):
                act.wait_ge(v_turned, b + 1)
                act.activation(v_tok[:, b, :], aux[:, 2 + b % 2, :], ACT.Copy).then_inc(v_done, 1)
            take_v(0)
            take_v(1)
            act.wait_ge(ln_var, 1)
            act.activation(root[:, 4:4 + TB], aux[:, 1, 0:TB], ACT.Sqrt, scale=1.0 / CONV_CH, bias=eps_col[:, 0:1])\
               .then_inc(ln_root, 1)
            take_v(2)
            take_v(3)
            for t in range(4):
                act.wait_ge(ln_scaled, t + 1)
                act.activation(conv[:, t, :], conv[:, t, :], ACT.Silu, bias=col("b_conv_ln", t)).then_inc(ln_silu, 1)
            act_linear(conv_out_l)

            act.wait_ge(inv_ready, inverse_of("qk"))
            for t in range(8):
                if t >= 2:
                    act.wait_ge(wide_ready, spread_of("qk", t - 2))
                repeat_pair(tmp[:, t % 2, :], 12 + 8 * t)

            def turned(n):
                h, i = n // TB, n % TB
                act.wait_ge(p_turned, n + 1)
                if h:
                    act.wait_ge(o_ready, h)
                act.activation(glu[:, 0:i + 1, i * P:(i + 1) * P],
                               aux[:, 2 + n % 2, 0:(i + 1) * P].rearrange("p (j q) -> p j q", q=P), ACT.Copy)\
                   .then_inc(p_copied, 1)

            def head_high(h):
                act.wait_ge(o_ready, h + 1)
                r = slice(64 * (h % 2), 64 * (h % 2) + 64)
                act.activation(br_hi[r, h // 2, :], lin[r, 2 + h % 2, :], ACT.Copy).then_inc(o_high, 1)

            for n in range(HEADS * TB):
                h, i = n // TB, n % TB
                if i == 0:
                    act.wait_ge(cb_ready, h + 1)
                    if h >= 2:
                        act.wait_ge(s_taken, TB * (h - 1))
                    act.activation(conv[:, 2 + h % 2, :], lin[:, h % 2, :], ACT.Copy).then_inc(cb_copied, 1)
                act.wait_ge(s_max, n + 1)
                step(act.activation(score(n)[:, 0:(i + 1) * P], score(n)[:, 0:(i + 1) * P], ACT.Exp,
                                    bias=stat[:, 1, n % 4:n % 4 + 1], accum_out=stat[:, 2, n % 4:n % 4 + 1]))
                act.nop().then_inc(s_exp, 1)
                if n >= LAG:
                    turned(n - LAG)
                if n >= 2 * TB and n % TB == 0:
                    head_high(n // TB - 2)
            for n in range(HEADS * TB - LAG, HEADS * TB):
                turned(n)
                if n == HEADS * TB - 2:
                    head_high(HEADS - 2)
            head_high(HEADS - 1)
            act_linear(attn_out_l)
            act_linear(out_l)
            act_norm(1, out_l)

            def take_ff(i, s):
                if s == 0:
                    slab_ready(act, ffn_in_l, i, s)
                    for t in range(2):
                        tile_taken(act, ffn_in_l, i - 1, 1, t)
                        act.activation(ffn_tmp[:, t, :], lin[:, t, :], ACT.Silu).then_inc(bank_free[0], 1)
            act_linear(ffn_in_l, take_ff)
            act_linear(ffn_out_l)
            if stop != "ffn":
                act_mix(act, step)
            if not stop:
                act_rest(act, step)

        @block.tensor
        def _(pe):
            pe.wait_ge(consts, 1)
            pe.wait_ge(rows_in, 16 * (len(place) + 2))
            for t in range(3):
                pe.transpose(aux[:, 2, t * P:(t + 1) * P], raw_rows[:, t, :], ident[:, :]).then_inc(tab_turned, 1)
            pe.wait_ge(x_in, 32)
            for k in range(KT):
                if k >= 2:
                    pe.wait_ge(x_done, k - 1)
                for b in range(TB):
                    last = pe.transpose(aux[:, k % 2, b * P:(b + 1) * P], x_rows[:, b, k * P:(k + 1) * P], ident[:, :])
                last.then_inc(x_turned, 1)
            pe.wait_ge(x_done, KT)
            pe_norm(0)
            pe_linear(glu_l, act_hi, act_lo, (act_ready, 0))
            pe_linear(qkv_l, act_hi, act_lo)
            pe_linear(forget_l, act_hi, act_lo)
            for t in range(8):
                pe.wait_ge(qk_square, t + 1)
                token_sums(aux[:, 0, 8 * t:8 * t + 8], sig[:, t, :], 2).then_inc(qk_summed, 1)
            turn_eight(1)
            pe_linear(gate_l, act_hi, act_lo)

            pe.wait_ge(qk_root, 1)
            pe.wait_ge(conv_step, 4 * CONV_W)
            for t in range(4):
                last = pe.matmul(aux[:, 0, :], ones[:, :], conv[:, t, :], start=(t == 0), stop=(t == 3))
            last.then_inc(ln_mean, 1)

            def turn_v(b):
                if b >= 2:
                    pe.wait_ge(v_done, b - 1)
                for t in range(4):
                    last = pe.transpose(aux[:, 2 + b % 2, t * P:(t + 1) * P], qkv[:, 8 + t, b * P:(b + 1) * P],
                                        ident[:, :])
                last.then_inc(v_turned, 1)
            turn_v(0)
            turn_v(1)
            pe.wait_ge(ln_square, 4)
            pe.wait_ge(f_biased, 1)
            for b in range(TB):
                for t in range(4):
                    last = pe.matmul(aux[:, 1, b:b + 1], glu[:, t, b * P:(b + 1) * P], ones[:, 0:1], start=(t == 0),
                                     stop=(t == 3))
            last.then_inc(ln_var, 1)
            turn_v(2)
            turn_v(3)
            pe.wait_ge(inv_ready, inverse_of("ln"))
            spread_tokens(aux[:, 1, :], 4)
            pe_linear(conv_out_l, br_hi, br_lo, (br_ready, 0))

            pe.wait_ge(f_ready, 1)
            for b in range(TB):
                for a in range(b + 1):
                    last = pe.matmul(aux[:, 1, 8 * b:8 * b + 8], upto[:, :] if a == b else ones[:, :], lf[:, 3, a, :],
                                     start=(a == 0), stop=(a == b))
            last.then_inc(f_sum, 1)
            pe.wait_ge(c_ready, 1)
            for b in range(TB):
                last = pe.transpose(aux[0:HEADS, 0, b * P:(b + 1) * P], csum[:, b, :], ident[:, :])
            last.then_inc(c_turned, 1)
            pe.wait_ge(v_done, TB)
            for t in range(8):
                if t >= 2:
                    pe.wait_ge(qk_done, t - 1)
                pe.wait_ge(pairs_ready, pairs_of("qk", t))
                spread_pair(aux[:, 2 + t % 2, :], tmp[:, t % 2, :])
            pe.wait_ge(qk_done, 8)
            every_tile_taken(pe, conv_out_l)

            def scores(n):
                h, i = n // TB, n % TB
                r = slice(64 * (h % 2), 64 * (h % 2) + 64)
                if n >= 2:
                    pe.wait_ge(s_taken, n - 1)
                pe.matmul(aux[:, n % 2, 0:(i + 1) * P], qkv[r, h // 2, i * P:(i + 1) * P],
                          qkv[r, 4 + h // 2, 0:(i + 1) * P], start=True, stop=False)
                pe.matmul(aux[:, n % 2, i * P:(i + 1) * P], ident[:, :], later_key[:, :], start=False, stop=True)\
                  .then_inc(s_ready, 1)

            def key_bias(h):
                if h >= 2:
                    pe.wait_ge(cb_copied, h - 1)
                pe.matmul(lin[:, h % 2, :], ident[0:HEADS, h:h + 1].broadcast_to([HEADS, P]), neg_c[:, :], start=True,
                          stop=True).then_inc(cb_ready, 1)

            def turn(n):
                h, i = n // TB, n % TB
                pe.wait_ge(s_diag, n + 1)
                if n >= 2:
                    pe.wait_ge(p_copied, n - 1)
                for j in range(i + 1):
                    last = pe.matmul(aux[:, 2 + n % 2, j * P:(j + 1) * P], score(n)[:, j * P:(j + 1) * P],
                                     diag[:, n % 2, :], start=True, stop=True)
                last.then_inc(p_turned, 1)

            def values(h):
                pe.wait_ge(p_copied, TB * (h + 1))
                if h >= 2:
                    pe.wait_ge(o_done, h - 1)
                for j in range(TB):
                    last = pe.matmul(lin[64 * (h % 2):64 * (h % 2) + 64, 2 + h % 2, j * P:T],
                                     v_tok[:, j, h * HD:(h + 1) * HD], glu[:, j, j * P:T],
                                     start=(j == 0), stop=(j == TB - 1))
                last.then_inc(o_ready, 1)

            pe.wait_ge(c_rows, 1)
            key_bias(0)
            for n in range(HEADS * TB + LAG + 1):
                if n < HEADS * TB:
                    scores(n)
                if n % TB == 1 and n // TB + 1 < HEADS:
                    key_bias(n // TB + 1)
                if LAG <= n < HEADS * TB + LAG:
                    turn(n - LAG)
                if n > LAG and (n - LAG) % TB == 0:
                    values((n - LAG) // TB - 1)
            pe.wait_ge(o_done, HEADS)
            pe_linear(attn_out_l, br_hi, br_lo)
            pe_linear(out_l, act_hi, act_lo, (m_ready, 0))
            pe_norm(1)
            pe_linear(ffn_in_l, act_hi, act_lo, (act_ready, KT))
            pe_linear(ffn_out_l, hid_hi, hid_lo, (hid_ready, 0))
            if stop != "ffn":
                pe_mix(pe)
            if not stop:
                pe_rest(pe)

        @block.vector
        def _(dve):
            step = Steps(dve, dve_step)
            for k in range(KT):
                dve.wait_ge(x_turned, k + 1)
                dve.tensor_copy(xT[:, k, :], aux[:, k % 2, :]).then_inc(x_done, 1)
            dve.wait_ge(tab_ready, 1)
            dve_norm(0, "g_mix", step)
            step(dve.tensor_scalar(q_gain, col("g_q", 0), HD ** -0.5, None, ALU.mult))
            step(dve.memset(glu[:, :, 0:PAD], 0.0))
            for i in range(2):
                for t in range(2):
                    slab_ready(dve, glu_l, i, 0)
                    tile_taken(dve, glu_l, i, 1, t)
                    dve.tensor_tensor(glu[:, 2 * i + t, PAD:PAD + T], lin[:, t, :], tmp[:, t, :], ALU.mult)\
                       .then_inc(bank_free[0], 1)
            tile_taken(dve, glu_l, 1, 0, 1)
            for j in range(CONV_W):
                for t in range(4):
                    tap = tab[:, 1, 4 * j + t:4 * j + t + 1]
                    if j == 0:
                        dve.tensor_scalar(conv[:, t, :], glu[:, t, 0:T], tap, col("b_dw", t), ALU.mult, ALU.add)\
                           .then_inc(conv_step, 1)
                    else:
                        dve.wait_ge(conv_step, 4 * (j - 1) + t + 1)
                        dve.scalar_tensor_tensor(conv[:, t, :], glu[:, t, j:j + T], tap, conv[:, t, :], ALU.mult,
                                                 ALU.add).then_inc(conv_step, 1)
            dve.wait_ge(qk_root, 1)
            dve.reciprocal(inv[:, 12:76], root[:, 12:76]).then_inc(inv_ready, 1)
            dve.wait_ge(f_logits, 1)
            dve.wait_ge(small_in, 32)
            dve.tensor_tensor(lf[:, 0, :, :], aux[:, 1, 0:32].rearrange("p (b h) -> p b h", h=8),
                                   f_bias[:, 0:1, :].broadcast_to([P, TB, 8]), ALU.add).then_inc(f_biased, 1)
            dve.wait_ge(ln_mean, 1)
            for t in range(4):
                dve.scalar_tensor_tensor(conv[:, t, :], aux[:, 0, :], -1.0 / CONV_CH, conv[:, t, :], ALU.mult, ALU.add)\
                   .then_inc(ln_centered, 1)
            dve.wait_ge(f_ln, 1)
            dve.scalar_tensor_tensor(lf[:, 3, :, :], lf[:, 0, :, :], 0.0, lf[:, 1, :, :], ALU.min, ALU.subtract)\
               .then_inc(f_ready, 1)
            dve.wait_ge(ln_root, 1)
            dve.reciprocal(inv[:, 4:4 + TB], root[:, 4:4 + TB]).then_inc(inv_ready, 1)
            dve.wait_ge(wide_ready, spread_of("ln"))
            for t in range(4):
                dve.scalar_tensor_tensor(conv[:, t, :], conv[:, t, :], col("g_conv_ln", t), aux[:, 1, :], ALU.mult,
                                         ALU.mult).then_inc(ln_scaled, 1)
            for t in range(4):
                dve.wait_ge(ln_silu, t + 1)
                step(dve.tensor_copy(br_hi[:, t, :], conv[:, t, :]))
                dve.tensor_tensor(br_lo[:, t, :], conv[:, t, :], br_hi[:, t, :].bitcast(F32), ALU.subtract)\
                   .then_inc(br_ready, 1)
            for s in range(4):
                slab_ready(dve, conv_out_l, 0, s)
                for t in range(2):
                    g = sig[:, 2 * s + t, :]
                    dve.tensor_tensor(g, lin[:, 2 * (s % 2) + t, :], g, ALU.mult).then_inc(bank_free[s % 2], 1)

            dve.wait_ge(f_sum, 1)
            dve.tensor_copy(csum[:, :, :], aux[:, 1, 0:32].rearrange("p (b h) -> p b h", h=8)).then_inc(c_ready, 1)
            dve.wait_ge(c_turned, 1)
            dve.tensor_scalar(neg_c[:, :], aux[0:HEADS, 0, :], -1.0, None, ALU.mult).then_inc(c_rows, 1)
            for t in range(8):
                dve.wait_ge(wide_ready, spread_of("qk", t))
                dve.scalar_tensor_tensor(qkv[:, t, :], qkv[:, t, :], q_gain if t < 4 else col("g_k", 0),
                                         aux[:, 2 + t % 2, :], ALU.mult, ALU.mult).then_inc(qk_done, 1)

            def divide(n):
                dve.wait_ge(s_exp, n + 1)
                if n >= 2:
                    dve.wait_ge(p_turned, n - 1)
                step(dve.reciprocal(stat[:, 0, n % 4:n % 4 + 1], stat[:, 2, n % 4:n % 4 + 1]))
                dve.tensor_scalar(diag[:, n % 2, :], ident[:, :], stat[:, 0, n % 4:n % 4 + 1], None, ALU.mult)\
                   .then_inc(s_diag, 1)

            def head_out(h):
                r = slice(64 * (h % 2), 64 * (h % 2) + 64)
                dve.wait_ge(o_high, h + 1)
                dve.tensor_tensor(br_lo[r, h // 2, :], lin[r, 2 + h % 2, :], br_hi[r, h // 2, :].bitcast(F32),
                                  ALU.subtract).then_inc(o_done, 1)

            for n in range(HEADS * TB):
                h, i = n // TB, n % TB
                m = (i + 1) * P
                dve.wait_ge(s_ready, n + 1)
                dve.wait_ge(cb_copied, h + 1)
                if n >= 4:
                    dve.wait_ge(p_turned, n - 3)
                dve.scalar_tensor_tensor(score(n)[:, 0:m], aux[:, n % 2, 0:m], csum[:, i, h:h + 1],
                                         conv[:, 2 + h % 2, 0:m], ALU.add, ALU.add).then_inc(s_taken, 1)
                dve.wait_ge(s_taken, n + 1)
                step(dve.tensor_reduce(stat[:, 0, n % 4:n % 4 + 1], score(n)[:, 0:m], AX.X, ALU.max))
                dve.tensor_scalar(stat[:, 1, n % 4:n % 4 + 1], stat[:, 0, n % 4:n % 4 + 1], -1.0, None, ALU.mult)\
                   .then_inc(s_max, 1)
                if n >= 2:
                    divide(n - 2)
                if i == 1 and h >= 2:
                    head_out(h - 2)
            divide(HEADS * TB - 2)
            divide(HEADS * TB - 1)
            head_out(HEADS - 2)
            head_out(HEADS - 1)

            for s in range(4):
                slab_ready(dve, attn_out_l, 0, s)
                for t in range(2):
                    k = 2 * s + t
                    dve.tensor_tensor(tmp[:, t, :], lin[:, 2 * (s % 2) + t, :], sig[:, KT + k, :], ALU.mult)\
                       .then_inc(bank_free[s % 2], 1)
                    tile_taken(dve, attn_out_l, 0, s, t)
                    step(dve.tensor_tensor(act_hi[:, k, :], tmp[:, t, :], sig[:, k, :], ALU.add))
                    step(dve.tensor_tensor(tmp[:, t, :], tmp[:, t, :], sig[:, k, :], ALU.add))
                    dve.tensor_tensor(act_lo[:, k, :], tmp[:, t, :], act_hi[:, k, :].bitcast(F32), ALU.subtract)\
                       .then_inc(m_ready, 1)
                    dve.wait_ge(m_ready, k + 1)

            add_to_residual(out_l)
            dve_norm(1, "g_ffn", step)
            with dve.Fori(0, ffn_in_l.bodies) as i:
                step.enter(i, 2)
                for t in range(2):
                    slab_ready(dve, ffn_in_l, i, 1)
                    tile_taken(dve, ffn_in_l, i, 0, t)
                    at = 2 * i + t
                    step(dve.tensor_tensor(hid_hi[:, bass.ds(at, 1), :], lin[:, 2 + t:3 + t, :], ffn_tmp[:, t:t + 1, :],
                                           ALU.mult))
                    dve.tensor_tensor(ffn_tmp[:, 2 + t, :], lin[:, 2 + t, :], ffn_tmp[:, t, :], ALU.mult)\
                       .then_inc(bank_free[1], 1)
                    tile_taken(dve, ffn_in_l, i, 1, t)
                    dve.tensor_tensor(hid_lo[:, bass.ds(at, 1), :], ffn_tmp[:, 2 + t:3 + t, :],
                                      hid_hi[:, bass.ds(at, 1), :].bitcast(F32), ALU.subtract).then_inc(hid_ready, 1)
                    dve.wait_ge(hid_ready, at + 1)
            step.leave(ffn_in_l.bodies)
            add_to_residual(ffn_out_l)
            if stop != "ffn":
                dve_mix(dve, step)
                if not stop:
                    dve_mem(dve, step)
                add_to_residual(mix_out_l)
            if not stop:
                dve_rest(dve, step)


def kernel(**inputs):
    import numpy as np
    import concourse.bacc as bacc
    from concourse.bass_utils import run_bass_kernel_spmd

    nc = bacc.Bacc("TRN2", target_bir_lowering=False, num_devices=1)
    arrays, d = {}, {}
    for name, value in inputs.items():
        a = np.ascontiguousarray(value)
        arrays[f"in_{name}_dram"] = a
        d[name] = nc.dram_tensor(f"in_{name}_dram", a.shape, mybir.dt.from_np(a.dtype), kind="ExternalInput").ap()
    out = nc.dram_tensor("out_0_dram", (1, T, D), F32, kind="ExternalOutput").ap()
    build(nc, d, out)
    return run_bass_kernel_spmd(nc, [arrays], core_ids=[0]).results[0]["out_0_dram"]
```

```python
from contextlib import ExitStack
import math

import concourse.bass as bass
from concourse import mybir

F32 = mybir.dt.float32
F32R = mybir.dt.float32r
BF16 = mybir.dt.bfloat16
ALU = mybir.AluOpType
ACT = mybir.ActivationFunctionType
AX = mybir.AxisListType

P = 128
D = 1024
T = 512
KT = D // P
TB = T // P
EPS = 1e-6
CONV_CH, CONV_W = 512, 31
HEADS, HD = 8, 64
FF = 2816
FT = FF // P
RING = 4
UK, UN = 4, 256
PAD = CONV_W - 1
LAG = 3
MASKED = -1.0e30

MH = 4
M_COLS = 4 * 512 + 2 * MH
R_COLS = 3 * 512 + 64 + 64 + 160
DECAY = math.exp(-0.5)
GN_EPS = 64e-5
CH = 64
NC = T // CH
M_TOK = 256
XH, XHD = 4, 256

TABLE_A = [("g_mix", 8), ("b_dw", 4), ("g_conv_ln", 4), ("b_conv_ln", 4), ("g_ffn", 8), ("norm_mix_2", 8),
           ("m_conv_b_2", 8), ("m_norm_g_2", 4), ("r_mu_2", 14), ("r_mu_tail", 1), ("r_w0_2", 4), ("r_a0_2", 4), ("r_kk_2", 4),
           ("r_ka_2", 4), ("r_rk_2", 4), ("r_gn_g_2", 4), ("r_gn_b_2", 4), ("norm_x_2", 8), ("norm_mem_2", 8),
           ("norm_ffn_2", 8), ("norm_final_2", 8), ("g_q", 1), ("g_k", 1)]
TABLE_B = [("w_dw", 124)]
TABLE_C = [("m_conv_w_2", 32), ("f_conv_w_2", 66), ("f_conv_b_2", 22)]

INVERSES = ["norm 0", "qk", "ln", "norm 1", "norm 2", "m", "gn", "kk", "y 0", "y 1", "mem", "norm 3", "norm 4", "norm 5"]
SPREADS = [("norm 0", 1), ("ln", 1), ("qk", 8), ("norm 1", 1), ("norm 2", 1), ("m", MH), ("gn", MH), ("kk 0", 2), ("kk 1", 2),
           ("y 0", 2), ("y 1", 2), ("mem", 1), ("norm 3", 1), ("norm 4", 1), ("norm 5", 1)]


def inverse_of(name):
    return INVERSES.index(name) + 1


def spread_of(name, k=0):
    at = [n for n, _ in SPREADS].index(name)
    return sum(n for _, n in SPREADS[:at]) + k + 1


def pairs_of(name, k=0):
    of_pairs = [(n, c) for n, c in SPREADS if n.split()[0] in ("qk", "kk", "y")]
    at = [n for n, _ in of_pairs].index(name)
    return sum(c for _, c in of_pairs[:at]) + k + 1


class Steps:

    def __init__(self, eng, sem):
        self.eng, self.sem, self.n = eng, sem, 0

    def __call__(self, ins):
        ins.then_inc(self.sem, 1)
        self.n = self.n + 1
        self.eng.wait_ge(self.sem, self.n)

    def enter(self, i, per):
        self.start, self.per = self.n, per
        self.n = i * per + self.start

    def leave(self, times):
        self.n = self.start + times * self.per


def build(nc, d, out):
    ctx = ExitStack()
    with ctx:
        def sb(name, shape, dt=F32, where=ctx):
            return where.enter_context(nc.sbuf_tensor(name, shape, dt))

        def sem(name):
            return ctx.enter_context(nc.semaphore(name))

        w_raw = sb("w_raw", [P, RING, UK, UN])
        w_hi = sb("w_hi", [P, RING, UK, UN], F32R)
        w_lo = sb("w_lo", [P, RING, UK, UN], F32R)
        xT = sb("xT", [P, KT, T])
        ident = sb("ident", [P, P])
        ones = sb("ones", [P, P])
        halves = sb("halves", [P, P])
        upto = sb("upto", [P, P])
        before = sb("before", [P, P])
        later_key = sb("later_key", [P, P], BF16)
        ident_b = sb("ident_b", [P, P], BF16)
        tab = sb("tab", [P, 3, P])
        rms_inv = sb("rms_inv", [P, T])
        eps_col = sb("eps_col", [P, 3])
        q_gain = eps_col[:, 2:3]
        root = sb("root", [P, 108])
        inv = sb("inv", [P, 108])
        f_bias = sb("f_bias", [P, 2, 8])

        with ExitStack() as ph:
            raw_rows = sb("raw_rows", [P, 3, P], where=ph)
            x_rows = sb("x_rows", [P, TB, D], where=ph)
        act_hi = sb("act_hi", [P, KT, T], F32R)
        act_lo = sb("act_lo", [P, KT, T], F32R)
        tmp = sb("tmp", [P, 2, T])
        with ExitStack() as ph:
            glu = sb("glu", [P, 4, T + PAD], where=ph)
            conv = sb("conv", [P, 4, T], where=ph)
            qkv = sb("qkv", [P, 12, T], where=ph)
            v_tok = sb("v_tok", [P, TB, 512], where=ph)
            sig = sb("sig", [P, 16, T], where=ph)
            br_hi = sb("br_hi", [P, 4, T], F32R, where=ph)
            br_lo = sb("br_lo", [P, 4, T], F32R, where=ph)
            lf = sb("lf", [P, 4, TB, 8], where=ph)
            csum = sb("csum", [P, TB, 8], where=ph)
            neg_c = sb("neg_c", [P, T], where=ph)
            stat = sb("stat", [P, 3, 4], where=ph)

        diag = rms_inv[:, 0:2 * P].rearrange("p (a b) -> p a b", a=2)

        def score(n):
            return (conv, tmp)[n % 4 // 2][:, n % 2, :]
        with ExitStack() as ph:
            hid_hi = sb("hid_hi", [P, FT, T], F32R, where=ph)
            hid_lo = sb("hid_lo", [P, FT, T], F32R, where=ph)
            ffn_tmp = sb("ffn_tmp", [P, 4, T], where=ph)
        with ExitStack() as ph:
            mix = sb("mix", [P, 25632], where=ph)
            end_decays = sb("end_decays", [P, 2, NC, 4], where=ph)

        def part(at, *dims, rows=slice(0, P)):
            size = math.prod(dims)
            names = "abcde"[:len(dims)]
            flat = mix[rows, at:at + size]
            if len(dims) == 1:
                return flat
            return flat.rearrange(f"p ({' '.join(names)}) -> p {' '.join(names)}", **dict(zip(names, dims)))

        rkv = part(0, 12, T)
        lora = part(6144, 3, T)
        sw = part(7680, 4, T)
        rate = part(9728, 4, T)
        ptT = part(7680, 4, T)
        decay_e = part(9728, 2, T)
        rows_whole = part(10752, 2, T)
        rows = part(10752, 2, T, rows=slice(0, MH))
        m_qk = part(11776, 8, T)
        m_v = part(15872, 4, T)
        m_h = part(15872, 4, T)
        m_vtok = part(17920, TB, 512)
        m_o = part(19968, 4, T)
        pad = part(22016, 2, T + 4)
        up_w = part(23048, 512)
        mg = part(23560, 5, TB, 8)
        def RK(half, pl):
            return part((11776 + 1024 * pl, (7680, 9728)[pl])[half], NC, 2, CH)
        BKt = part(13824, 2, NC, P)
        BK = part(15872, 2, NC, 2, CH)
        UV = part(17920, NC, 4, CH)
        G = part(19968, 2, 2, NC, P)
        half64 = slice(0, CH)
        mem_rows = part(15872, 2, D)
        memT = part(13824, KT, M_TOK)
        X = [part(15872 + 1024 * p, 16, CH) for p in range(2)]
        XT = [part(17920 + 1024 * p, 16, CH) for p in range(2)]
        y_sb = part(11776, 2, T)
        g_mask = part(24096, P)
        level = part(24224, 6, CH, rows=half64)
        up_g = part(24608, 2, 512)
        state = part(6144, 2, 4, CH)

        with ExitStack() as ph:
            q_x = sb("q_x", [P, KT, T], where=ph)
            mem_hi = sb("mem_hi", [P, KT, M_TOK], F32R, where=ph)
            mem_lo = sb("mem_lo", [P, KT, M_TOK], F32R, where=ph)
            kv_x = sb("kv_x", [P, 16, M_TOK], where=ph)
            v_xtok = sb("v_xtok", [P, 2, D], where=ph)
            x_s = sb("x_s", [P, 4, M_TOK], where=ph)
            x_pT = sb("x_pT", [P, 2, 2, T], where=ph)
            x_stat = sb("x_stat", [P, 3, 4], where=ph)
            x_diag = sb("x_diag", [P, 2, P], where=ph)
        with ExitStack() as ph:
            hid2_hi = sb("hid2_hi", [P, FT, T], F32R, where=ph)
            hid2_lo = sb("hid2_lo", [P, FT, T], F32R, where=ph)
            gpad = sb("gpad", [P, 2, T + 2], where=ph)
            gconv = sb("gconv", [P, 2, T], where=ph)
        with ExitStack() as ph:
            out_rows = sb("out_rows", [P, TB, D], where=ph)
            y_fin = sb("y_fin", [P, KT, T], where=ph)

        lin = ctx.enter_context(nc.psum_tensor("lin", [P, 4, T], F32))
        aux = ctx.enter_context(nc.psum_tensor("aux", [P, 4, T], F32))

        class Layer:
            units, slabs = 0, 0

            def __init__(self, weight, kt, bodies, column, slabs=2, skip=(), uk=UK, made=None):
                self.skip = skip
                made = made or slabs
                self.w = weight.rearrange("o (k p) n -> p (o k) n", p=P)
                self.bodies, self.column, self.slabs = bodies, column, slabs
                self.parts = [(k, min(uk, kt - k)) for k in range(0, kt, uk)]
                self.kt, self.per = kt, made * len(self.parts)
                self.u0, self.s0 = Layer.units, Layer.slabs
                Layer.units += bodies * self.per
                Layer.slabs += bodies * slabs
                assert self.per % RING == 0

            def unit(self, k):
                return (k // len(self.parts), *self.parts[k % len(self.parts)])

        Layer.slabs = 0
        whole = lambda i, s: i * 2 * UN + s * UN
        glu_l = Layer(d["w_in"], KT, 2, lambda i, s: i * UN + s * CONV_CH)
        qkv_l = Layer(d["w_in"], KT, 3, lambda i, s: 2 * CONV_CH + whole(i, s))
        eight = dict(skip=[(0, 1), (1, 0), (1, 1)], uk=2, made=1)
        forget_l = Layer(d["w_in"], KT, 1, lambda i, s: 2 * CONV_CH + 3 * HEADS * HD, **eight)
        gate_l = Layer(d["w_in"], KT, 4, lambda i, s: 2 * CONV_CH + 3 * HEADS * HD + HEADS + whole(i, s))
        conv_out_l = Layer(d["w_conv_out"], 4, 1, lambda i, s: s * UN, slabs=4)
        attn_out_l = Layer(d["w_attn_out"], 4, 1, lambda i, s: s * UN, slabs=4)
        out_l = Layer(d["w_out"], KT, 2, whole)
        ffn_in_l = Layer(d["w_ffn_in"], KT, 11, lambda i, s: i * UN + s * FF)
        ffn_out_l = Layer(d["w_ffn_out"], FT, 2, whole)
        layers = [glu_l, qkv_l, forget_l, gate_l, conv_out_l, attn_out_l, out_l, ffn_in_l, ffn_out_l]
        m_qk_l = Layer(d["w_in_2"], KT, 2, whole)
        m_vo_l = Layer(d["w_in_2"], KT, 2, lambda i, s: 1024 + whole(i, s))
        rkv_l = Layer(d["w_in_2"], KT, 3, lambda i, s: M_COLS + whole(i, s))
        lora_l = Layer(d["w_in_2"], KT, 1, lambda i, s: M_COLS + 3 * 512 + 32 * s, skip=[(1, 0)])
        m_gate_l = Layer(d["w_in_2"], KT, 1, lambda i, s: 4 * 512, **eight)
        mix_out_l = Layer(d["w_out_2"], KT, 2, whole)
        layers += [m_qk_l, m_vo_l, rkv_l, lora_l, m_gate_l, mix_out_l]
        xkv_l = Layer(d["x_wkv_2"], KT, 4, whole)
        xq_l = Layer(d["x_wq_2"], KT, 2, whole)
        xo_l = Layer(d["x_wo_2"], KT, 2, whole)
        up_l = Layer(d["f_up_2"], KT, 11, lambda i, s: i * UN + s * FF)
        down_l = Layer(d["f_down_2"], FT, 2, whole)
        layers += [xkv_l, xq_l, xo_l, up_l, down_l]

        w_arrived = [sem(f"w_arrived{s}") for s in range(RING)]
        w_high = sem("w_high")
        w_low = sem("w_low")
        w_used = sem("w_used")
        bank_free = [sem("bank_free0"), sem("bank_free1")]
        consts = sem("consts")
        rows_zero = sem("rows_zero")
        rows_in = sem("rows_in")
        x_in = sem("x_in")
        small_in = sem("small_in")
        tab_turned = sem("tab_turned")
        tab_ready = sem("tab_ready")
        x_turned = sem("x_turned")
        x_done = sem("x_done")
        n_square, n_added, n_summed, n_root, n_scaled, n_high, act_ready = (
            sem(n) for n in ("n_square", "n_added", "n_summed", "n_root", "n_scaled", "n_high", "act_ready"))
        inv_ready, wide_ready, pairs_ready = sem("inv_ready"), sem("wide_ready"), sem("pairs_ready")
        dve_step, act_step, pool_step = (sem(n) for n in ("dve_step", "act_step", "pool_step"))

        conv_step = sem("conv_step")
        f_rows, f_logits, f_biased, f_ln, f_ready, f_sum, c_ready = (
            sem(n) for n in ("f_rows", "f_logits", "f_biased", "f_ln", "f_ready", "f_sum", "c_ready"))
        ln_mean, ln_centered, ln_square, ln_var, ln_root, ln_scaled, ln_silu, br_ready = (
            sem(n) for n in ("ln_mean", "ln_centered", "ln_square", "ln_var", "ln_root", "ln_scaled", "ln_silu",
                             "br_ready"))
        qk_square, qk_summed, qk_root, qk_done = (sem(n) for n in ("qk_square", "qk_summed", "qk_root", "qk_done"))
        v_turned, v_done = sem("v_turned"), sem("v_done")
        c_turned, c_rows, cb_ready, cb_copied = sem("c_turned"), sem("c_rows"), sem("cb_ready"), sem("cb_copied")
        s_ready, s_taken, s_max, s_exp, s_diag, p_turned, p_copied, o_ready, o_high, o_done = (
            sem(n) for n in ("s_ready", "s_taken", "s_max", "s_exp", "s_diag", "p_turned", "p_copied", "o_ready",
                             "o_high", "o_done"))
        m_ready, hid_ready = sem("m_ready"), sem("hid_ready")
        stored = sem("stored")
        lower_zero, keys_zero, neg_c_zero = sem("lower_zero"), sem("keys_zero"), sem("neg_c_zero")

        place, row = {}, 0
        for t, table in enumerate((TABLE_A, TABLE_B, TABLE_C)):
            row = 0
            for name, n in table:
                place[name] = (t, row, n)
                row += n
            assert row <= P

        def col(name, j):
            t, r, _ = place[name]
            return tab[:, t, r + j:r + j + 1]

        def stream(eng, layer):
            with eng.Fori(0, layer.bodies) as i:
                at = [eng.snap(layer.column(i, s)) for s in range(layer.slabs)]
                for k in range(layer.per):
                    s, r, n = layer.unit(k)
                    eng.wait_ge(w_low, i * layer.per + (layer.u0 + k + 1))
                    eng.dma_start(w_raw[:, k % RING, 0:n, :], layer.w[:, r:r + n, bass.ds(at[s], UN)])\
                       .then_inc(w_arrived[k % RING], 16)

        def round_unit(layer, i, k):
            if k >= layer.per:
                follow = layers.index(layer) + 1
                last = layer.bodies - 1
                if type(i) is int and i == last:
                    if follow == len(layers):
                        return
                    layer, i, k = layers[follow], 0, k - layer.per
                else:
                    i, k = i + 1, k - layer.per
            n = layer.unit(k)[2]
            s = k % RING
            nc.scalar.wait_ge(w_arrived[s], i * (16 * (layer.per // RING)) + 16 * (layer.u0 // RING + k // RING + 1))
            nc.scalar.wait_ge(w_used, i * layer.per + (layer.u0 + k + 1))
            nc.scalar.activation(w_hi[:, s, 0:n, :], w_raw[:, s, 0:n, :], ACT.Copy).then_inc(w_high, 1)

        AHEAD = 2

        def act_linear(layer, take=None, unroll=False):
            def body(i):
                for k in range(layer.per):
                    round_unit(layer, i, k + AHEAD)
                    if (k + 1) % len(layer.parts) == 0 and take:
                        take(i, k // len(layer.parts))
            if unroll:
                for i in range(layer.bodies - 1):
                    body(i)
            elif layer.bodies > 1:
                with nc.scalar.Fori(0, layer.bodies - 1) as i:
                    body(i)
            body(layer.bodies - 1)

        def slab_ready(eng, layer, i, s):
            eng.wait_ge(w_used, i * layer.per + (RING + layer.u0 + (s + 1) * len(layer.parts)))

        def tile_taken(eng, layer, i, s, t):
            eng.wait_ge(bank_free[s % 2], i * layer.slabs + (layer.s0 + 2 * (s // 2) + 3 + t))

        def every_tile_taken(eng, layer):
            for s in (layer.slabs - 2, layer.slabs - 1):
                tile_taken(eng, layer, layer.bodies - 1, s, 1)

        def pool_linear(layer):
            with nc.gpsimd.Fori(0, layer.bodies) as i:
                for k in range(layer.per):
                    n, s = layer.unit(k)[2], k % RING
                    nc.gpsimd.wait_ge(w_high, i * layer.per + (layer.u0 + k + 1))
                    nc.gpsimd.tensor_tensor(w_lo[:, s, 0:n, :], w_raw[:, s, 0:n, :], w_hi[:, s, 0:n, :].bitcast(F32),
                                            ALU.subtract).then_inc(w_low, 1)

        def pe_linear(layer, hi, lo, ready=None, bodies=None):
            def body(i, first):
                for k in range(layer.per):
                    s, r, n = layer.unit(k)
                    if r == 0:
                        nc.tensor.wait_ge(bank_free[s % 2], i * layer.slabs + (layer.s0 + 2 * (s // 2) + 2))
                    nc.tensor.wait_ge(w_low, i * layer.per + (RING + layer.u0 + k + 1))
                    tiles = [t for t in range(2) if (s, t) not in layer.skip]
                    if first and s == 0:
                        order = [(j, t) for j in range(n) for t in tiles]
                    else:
                        order = [(j, t) for t in tiles for j in range(n)]
                    for j, t in order:
                        if first and s == 0 and t == 0:
                            nc.tensor.wait_ge(ready[0], ready[1] + r + j + 1)
                        bank = lin[:, 2 * (s % 2) + t, 0:hi.shape[2]]
                        c = slice(t * P, t * P + P)
                        high, low = w_hi[:, k % RING, j, c], w_lo[:, k % RING, j, c]
                        nc.tensor.matmul(bank, high, hi[:, r + j, :], start=(r + j == 0), stop=False)
                        nc.tensor.matmul(bank, high, lo[:, r + j, :], start=False, stop=False)
                        last = nc.tensor.matmul(bank, low, hi[:, r + j, :], start=False,
                                                stop=(r + j == layer.kt - 1))
                    last.then_inc(w_used, 1)
            if ready:
                body(0, True)
            low, high = bodies or (int(bool(ready)), layer.bodies)
            if high == low + 1:
                body(low, False)
            elif high > low:
                with nc.tensor.Fori(low, high) as i:
                    body(i, False)

        def take_eight(layer):
            def take(i, s):
                slab_ready(nc.scalar, layer, 0, 0)
                nc.scalar.activation(rms_inv[0:8, :], lin[0:8, 0, :], ACT.Copy).then_inc(f_rows, 1)
                nc.scalar.wait_ge(f_rows, 1 if layer is forget_l else 2)
                nc.scalar.sem_inc(bank_free[0], 2)
                nc.scalar.sem_inc(bank_free[1], 2)
            return take

        def turn_eight(n):
            nc.tensor.wait_ge(f_rows, n)
            for b in range(TB):
                last = nc.tensor.transpose(aux[:, 1, 8 * b:8 * b + 8], rms_inv[0:8, b * P:(b + 1) * P], ident[0:8, 0:8])
            last.then_inc(f_logits, 1)

        def norm_add(m, k):
            nc.vector.wait_ge(n_square, KT * m + k + 1)
            if k == 0:
                nc.vector.tensor_copy(rms_inv[:, :], tmp[:, 0, :]).then_inc(n_added, 1)
            else:
                nc.vector.wait_ge(n_added, KT * m + k)
                nc.vector.tensor_tensor(rms_inv[:, :], rms_inv[:, :], tmp[:, k % 2, :], ALU.add).then_inc(n_added, 1)

        def add_to_residual(layer, m=None):
            for i in range(2):
                for s in range(2):
                    if m is not None and (i, s) == (1, 0):
                        for k in range(4):
                            norm_add(m, k)
                    slab_ready(nc.vector, layer, i, s)
                    for t in range(2):
                        x = xT[:, 4 * i + 2 * s + t, :]
                        nc.vector.tensor_tensor(x, lin[:, 2 * s + t, :], x, ALU.add)\
                          .then_inc(bank_free[s], 1)
                    if m is not None and i == 1:
                        norm_add(m, 4 + 2 * s)
                        norm_add(m, 5 + 2 * s)

        def act_norm_square(m, after, tiles=range(KT)):
            for k in tiles:
                if after is None:
                    nc.scalar.wait_ge(x_done, k + 1)
                else:
                    tile_taken(nc.scalar, after, k // 4, k // 2 % 2, k % 2)
                if k >= 2:
                    nc.scalar.wait_ge(n_added, KT * m + k - 1)
                nc.scalar.activation(tmp[:, k % 2, :], xT[:, k, :], ACT.Square).then_inc(n_square, 1)

        def act_norm_root(m):
            nc.scalar.wait_ge(n_summed, m + 1)
            nc.scalar.activation(root[:, 0:TB], aux[:, 0, 0:TB], ACT.Sqrt, scale=1.0 / D, bias=eps_col[:, 0:1])\
              .then_inc(n_root, 1)

        def act_norm_high(m):
            for k in range(KT):
                nc.scalar.wait_ge(n_scaled, KT * m + k + 1)
                nc.scalar.activation(act_hi[:, k, :], tmp[:, k % 2, :], ACT.Copy).then_inc(n_high, 1)

        def act_linear_square(layer, m):
            def take(i, s):
                if i == 1:
                    act_norm_square(m, layer, (2 * s, 2 * s + 1))
            act_linear(layer, take, unroll=True)
            act_norm_square(m, layer, range(4, KT))

        def act_norm_rest(m):
            act_norm_root(m)
            act_norm_high(m)

        def token_sums(to, squares, groups=1):
            for b in range(squares.shape[1] // P):
                last = nc.tensor.matmul(to[:, groups * b:groups * (b + 1)], squares[:, b * P:(b + 1) * P],
                                        ones[:, 0:1] if groups == 1 else halves[:, 0:P:CH], start=True, stop=True)
            return last

        def spread_tokens(to, at, blocks=TB):
            for b in range(blocks):
                last = nc.tensor.matmul(to[:, b * P:(b + 1) * P], inv[:, at + b:at + b + 1].broadcast_to([P, P]),
                                        ident[:, :], start=True, stop=True)
            last.then_inc(wide_ready, 1)

        def repeat_pair(to, at):
            nc.scalar.activation(to.rearrange("p (b g c) -> p b g c", b=TB, g=2),
                                 inv[:, at:at + 2 * TB].rearrange("p (b g) -> p b g", g=2).unsqueeze(3)
                                 .broadcast_to([P, TB, 2, CH]), ACT.Copy).then_inc(pairs_ready, 1)

        def spread_pair(to, repeated):
            for b in range(TB):
                last = nc.tensor.matmul(to[:, b * P:(b + 1) * P], repeated[:, b * P:(b + 1) * P], ident[:, :], start=True,
                                        stop=True)
            last.then_inc(wide_ready, 1)

        def pe_norm(m):
            nc.tensor.wait_ge(n_added, KT * (m + 1))
            token_sums(aux[:, 0, :], rms_inv).then_inc(n_summed, 1)
            nc.tensor.wait_ge(inv_ready, inverse_of(f"norm {m}"))
            spread_tokens(aux[:, 1, :], 0)

        def dve_norm(m, gain, step, to=None):
            v = nc.vector
            if m in (0, 3):
                for k in range(KT):
                    norm_add(m, k)
            v.wait_ge(n_root, m + 1)
            v.reciprocal(inv[:, 0:TB], root[:, 0:TB]).then_inc(inv_ready, 1)
            v.wait_ge(wide_ready, spread_of(f"norm {m}"))
            if m == 0:
                v.wait_ge(tab_ready, 1)

            if to is not None:
                for k in range(KT):
                    v.scalar_tensor_tensor(to[:, k, :], xT[:, k, :], col(gain, k), aux[:, 1, :], ALU.mult, ALU.mult)\
                     .then_inc(y_ready, 1)
                return

            def low(k):
                v.wait_ge(n_high, KT * m + k + 1)
                v.tensor_tensor(act_lo[:, k, :], tmp[:, k % 2, :], act_hi[:, k, :].bitcast(F32), ALU.subtract)\
                 .then_inc(act_ready, 1)
            for k in range(KT):
                if k >= 2:
                    low(k - 2)
                    v.wait_ge(act_ready, KT * m + k - 1)
                v.scalar_tensor_tensor(tmp[:, k % 2, :], xT[:, k, :], col(gain, k), aux[:, 1, :], ALU.mult, ALU.mult)\
                 .then_inc(n_scaled, 1)
            low(KT - 2)
            low(KT - 1)

        (m_conv, m_silu, r_shift, u_ready, u_turned, rows_ready, em_turned, m_e, m_s, m_exp, m_p, m_pv, m_den,
         m_head, m_normed) = (sem(n) for n in (
            "m_conv", "m_silu", "r_shift", "u_ready",
            "u_turned", "rows_ready", "em_turned", "m_e", "m_s", "m_exp", "m_p", "m_pv", "m_den",
            "m_head", "m_normed"))
        (gn_mean, gn_centered, gn_square, gn_var, gn_root, gn_done) = (sem(n) for n in (
            "gn_mean", "gn_centered", "gn_square", "gn_var", "gn_root", "gn_done"))
        (two_in, masks_ready, r_act, r_pre, r_sig, kk_square, kk_sum, kk_floor, kk_root, z_cum, z_exp, packed, bonus_in,
         bonus_sum, bonus_done) = (sem(n) for n in (
            "two_in", "masks_ready", "r_act", "r_pre", "r_sig", "kk_square", "kk_sum", "kk_floor", "kk_root", "z_cum",
            "z_exp", "packed", "bonus_in", "bonus_sum", "bonus_done"))
        (bt_turned, bt_done, g_built, g_masked, xt_first, x_first, x_copied, iv_y, iv_t, iv_x, iv_xd, iv_xt, iv_xtd, uv_zero,
         uv_turned, uv_done) = (sem(n) for n in (
            "bt_turned", "bt_done", "g_built", "g_masked", "xt_first", "x_first", "x_copied", "iv_y", "iv_t", "iv_x",
            "iv_xd", "iv_xt", "iv_xtd", "uv_zero", "uv_turned", "uv_done"))
        (w_sum, w_taken, u_sum, u_taken, s_sum, s_new, y_sum, y_copied, y_mean, y_centered, y_square, y_var, y_root,
         y_gate, mix_ready) = (sem(n) for n in (
            "w_sum", "w_taken", "u_sum", "u_taken", "s_sum", "s_new", "y_sum", "y_copied", "y_mean", "y_centered",
            "y_square", "y_var", "y_root", "y_gate", "mix_ready"))

        def act_mix(act, step):
            act.dma_start(up_w[0:64, :], d["r_w_up_2"][0]).then_inc(two_in, 16)
            act.dma_start(up_w[64:128, :], d["r_a_up_2"][0]).then_inc(two_in, 16)
            act.dma_start(up_g[:, 0, :], d["r_g_up_2"][0, 0:P, :]).then_inc(two_in, 16)
            act.wait_ge(masks_ready, 1)
            act.dma_start(up_g[96:128, 1, :], d["r_g_up_2"][0, P:160, :]).then_inc(two_in, 16)
            act_norm_root(2)
            act_norm_high(2)
            act.wait_ge(two_in, 64)
            step(act.activation(pad[:, :, 0:3], ident[:, 0:6].rearrange("p (a b) -> p a b", a=2), ACT.Copy, scale=0.0))

            def silu(q):
                act.wait_ge(m_conv, q + 1)
                act.activation(m_qk[:, q, :], m_qk[:, q, :], ACT.Silu).then_inc(m_silu, 1)

            def take_qk(i, s):
                slab_ready(act, m_qk_l, i, s)
                for t in range(2):
                    q = 4 * i + 2 * s + t
                    if q >= 2:
                        act.wait_ge(m_conv, q - 1)
                    act.activation(pad[:, t, 3:3 + T], lin[:, 2 * s + t, :], ACT.Copy).then_inc(bank_free[s], 1)
                    if q >= 2:
                        silu(q - 2)

            def take_vo(i, s):
                slab_ready(act, m_vo_l, i, s)
                for t in range(2):
                    q = 2 * s + t
                    if i == 0:
                        act.activation(m_v[:, q, :], lin[:, q, :], ACT.Copy).then_inc(bank_free[s], 1)
                    else:
                        act.activation(m_o[:, q, :], lin[:, q, :], ACT.Sigmoid).then_inc(bank_free[s], 1)

            def take_shift(layer, i, s, t, q):
                if q >= 2:
                    act.wait_ge(r_shift, q - 1)
                act.activation(pad[:, q % 2, 3:3 + T], lin[:, 2 * s + t, :], ACT.Copy).then_inc(bank_free[s], 1)

            def take_rkv(i, s):
                slab_ready(act, rkv_l, i, s)
                for t in range(2):
                    take_shift(rkv_l, i, s, t, 4 * i + 2 * s + t)

            def take_lora(i, s):
                slab_ready(act, lora_l, i, s)
                if s == 1:
                    act.sem_inc(bank_free[1], 1)
                for t in range(s, 2):
                    take_shift(lora_l, i, s, t, 12 + s + t)

            act_linear(m_qk_l, take_qk, unroll=True)
            silu(6)
            silu(7)
            act_linear(m_vo_l, take_vo, unroll=True)
            act_linear(rkv_l, take_rkv, unroll=True)
            act_linear(lora_l, take_lora, unroll=True)
            act_linear(m_gate_l, take_eight(m_gate_l), unroll=True)

            act.wait_ge(f_biased, 2)
            step(act.activation(mg[:, 1, :, :], mg[:, 0, :, :], ACT.Abs))
            step(act.activation(mg[:, 2, :, :], mg[:, 1, :, :], ACT.Exp, scale=-1.0))
            act.activation(mg[:, 1, :, :], mg[:, 2, :, :], ACT.Ln, bias=ones[:, 0:1]).then_inc(f_ln, 1)
            for b in range(TB):
                act.wait_ge(v_turned, TB + b + 1)
                act.activation(m_vtok[:, b, :], aux[:, 2 + b % 2, :], ACT.Copy).then_inc(v_done, 1)
            act.wait_ge(r_shift, 15)
            for p in range(4):
                if p >= 2:
                    act.wait_ge(kk_sum, p - 1)
                act.activation(tmp[:, p % 2, :], rkv[:, 4 + p, :], ACT.Square, scale=col("r_kk_2", p))\
                   .then_inc(kk_square, 1)
            act.wait_ge(em_turned, 1)
            step(act.activation(root[:, 28:44], lin[:, 3, 0:16], ACT.Exp))

            def copy_head(h):
                act.wait_ge(m_pv, TB * h + TB)
                act.activation(m_h[:, h, :], lin[:, 2 * (h % 2), :], ACT.Copy).then_inc(m_head, 1)

            for n in range(MH * TB):
                h, j = n // TB, n % TB
                w = T - j * P
                act.wait_ge(m_e, n + 1)
                if n >= 2:
                    act.wait_ge(m_p, n - 1)
                act.activation(decay_e[:, n % 2, 0:w], aux[:, 2 + n % 2, 0:w], ACT.Exp,
                               bias=mg[:, 4, j, h:h + 1]).then_inc(m_exp, 1)
                if h and j == 2:
                    copy_head(h - 1)
            copy_head(MH - 1)
            act.activation(root[:, 12:28], lin[:, 1, 0:16], ACT.Abs).then_inc(m_den, 1)
            for h in range(MH):
                act.wait_ge(gn_centered, h + 1)
                if h >= 2:
                    act.wait_ge(gn_var, h - 1)
                act.activation(tmp[:, h % 2, :], m_h[:, h, :], ACT.Square).then_inc(gn_square, 1)
            act.wait_ge(gn_var, MH)
            act.activation(root[:, 44:60], lin[:, 3, 0:16], ACT.Sqrt, scale=1.0 / P, bias=eps_col[:, 0:1])\
               .then_inc(gn_root, 1)
            act.wait_ge(kk_floor, 1)
            act.activation(root[:, 76:108], root[:, 76:108], ACT.Sqrt).then_inc(kk_root, 1)

            act.wait_ge(gn_var, MH)
            act.activation(tmp[64:128, 0, :], lora[0:64, 0, :], ACT.Copy, scale=0.0)
            act.activation(tmp[0:64, 1, :], lora[0:64, 0, :], ACT.Copy, scale=0.0)
            act.activation(tmp[64:128, 1, :], lora[64:128, 0, :], ACT.Copy)
            act.activation(tmp[0:64, 0, :], lora[0:64, 0, :], ACT.Tanh).then_inc(r_act, 1)
            act.activation(lora[:, 1:3, :], lora[:, 1:3, :], ACT.Sigmoid).then_inc(r_act, 1)
            for q in range(8):
                act.wait_ge(r_pre, q + 1)
                act.activation((sw, rate)[q % 2][:, q // 2, :], aux[:, q % 4, :], ACT.Sigmoid,
                               bias=col(("r_w0_2", "r_a0_2")[q % 2], q // 2)).then_inc(r_sig, 1)
            def prepare_act(p):
                if p == 0:
                    act.wait_ge(inv_ready, inverse_of("kk"))
                else:
                    act.wait_ge(wide_ready, spread_of(f"kk {(p - 1) // 2}", (p - 1) % 2))
                if p == 0:
                    act.wait_ge(r_pre, 8)
                repeat_pair(tmp[:, 0, :], 76 + 8 * p)
                if p:
                    act.wait_ge(packed, p)
                act.wait_ge(z_cum, p + 1)
                step(act.activation(rms_inv[:, :], sw[:, p, :], ACT.Exp, scale=DECAY))
                act.activation(sw[:, p, :], sw[:, p, :], ACT.Exp, scale=-DECAY).then_inc(z_exp, 1)

            prepare_act(0)
            prepare_act(1)
            for half in range(2):
                for pl in range(2):
                    for b in range(2):
                        act.wait_ge(bt_turned, 4 * half + 2 * pl + b + 1)
                        act.activation(BKt[:, pl, 4 * b:4 * b + 4, :],
                                       aux[:, 2 * (pl % 2) + b, :].rearrange("p (c n) -> p c n", n=P), ACT.Copy)\
                           .then_inc(bt_done, 1)
                for pl in range(2):
                    act.wait_ge(x_first, 2 * half + pl + 1)
                    act.activation(X[pl][half64], (aux, lin)[pl][half64, 2:4, :].rearrange("p a (u n) -> p (a u) n", n=CH),
                                   ACT.Copy).then_inc(x_copied, 1)
                for pl in range(2):
                    for b in range(2):
                        n = 4 * half + 2 * pl + b
                        act.wait_ge(uv_turned, n + 1)
                        act.activation(UV[64:128, 4 * b:4 * b + 4, 2 * pl:2 * pl + 2, :],
                                       aux[64:128, 2 * pl + b, :].rearrange("p (c g n) -> p c g n", c=4, g=2), ACT.Copy)\
                           .then_inc(uv_done, 1)
                if half:
                    act.wait_ge(iv_xtd, 20)
                    act.dma_start(mem_rows, d["mem_2"].rearrange("o (b p) c -> p (o b) c", p=P)).then_inc(mem_in, 16)
                for c in range(NC):
                    n = NC * half + c
                    act.wait_ge(w_sum, n + 1)
                    act.activation(w_sb(half)[half64], aux[half64, 0, 0:256].rearrange("p (g n) -> p g n", n=CH), ACT.Copy)\
                       .then_inc(w_taken, 1)
                    act.wait_ge(u_sum, n + 1)
                    act.activation(UV[0:64, c, :, :], aux[0:64, 1, 0:256].rearrange("p (g n) -> p g n", n=CH), ACT.Copy)\
                       .then_inc(u_taken, 1)
                    if half == 0 and c in (1, 4):
                        prepare_act(2 + c // 4)
                for pl in range(2):
                    p = 2 * half + pl
                    act.wait_ge(y_sum, NC * (half + 1))
                    act.activation(y_sb[:, pl, :], lin[:, pl, :], ACT.Copy).then_inc(y_copied, 1)
                for pl in range(2):
                    p = 2 * half + pl
                    act.wait_ge(y_centered, p + 1)
                    act.activation(tmp[:, pl, :], y_sb[:, pl, :], ACT.Square).then_inc(y_square, 1)
                act.wait_ge(y_var, 2 * half + 2)
                act.activation(root[:, 44:60], aux[:, 1, 0:16], ACT.Sqrt, scale=1.0 / CH, bias=eps_col[:, 1:2])\
                   .then_inc(y_root, 1)
                act.wait_ge(inv_ready, inverse_of(f"y {half}"))
                for pl in range(2):
                    repeat_pair(tmp[:, pl, :], 44 + 8 * pl)
            for g in range(KT // 2):
                act.wait_ge(mem_turned, g + 1)
                act.activation(memT[:, 2 * g:2 * g + 2, :], lin[:, 2 + g % 2, :].rearrange("p (k m) -> p k m", k=2), ACT.Copy)\
                   .then_inc(mem_done, 1)
            act_linear(mix_out_l, unroll=True)
            act.wait_ge(mem_summed, 1)
            act.activation(root[:, 8:10], aux[:, 2, 0:2], ACT.Sqrt, scale=1.0 / D, bias=eps_col[:, 0:1])\
               .then_inc(mem_root, 1)

        def pe_mix(pe):
            pe_norm(2)
            pe_linear(m_qk_l, act_hi, act_lo, (act_ready, 2 * KT))
            pe_linear(m_vo_l, act_hi, act_lo)
            pe_linear(rkv_l, act_hi, act_lo)
            pe_linear(lora_l, act_hi, act_lo)
            pe_linear(m_gate_l, act_hi, act_lo)
            turn_eight(2)
            for b in range(TB):
                if b >= 2:
                    pe.wait_ge(v_done, TB + b - 1)
                for t in range(4):
                    last = pe.transpose(aux[:, 2 + b % 2, t * P:(t + 1) * P], m_v[:, t, b * P:(b + 1) * P], ident[:, :])
                last.then_inc(v_turned, 1)
            pe.wait_ge(f_ready, 2)
            for b in range(TB):
                for a in range(b + 1):
                    last = pe.matmul(aux[:, 0, 8 * b:8 * b + 8], upto[:, :] if a == b else ones[:, :], mg[:, 3, a, :],
                                     start=(a == 0), stop=(a == b))
            last.then_inc(f_sum, 1)
            pe.wait_ge(v_done, TB + TB)
            pe.wait_ge(u_ready, 2)
            for kind in range(2):
                for b in range(TB):
                    last = pe.transpose(aux[0:MH, 2 + kind, b * P:(b + 1) * P], mg[:, 4, b, MH * kind:MH * kind + MH],
                                        ident[:, :])
            last.then_inc(u_turned, 1)
            for p in range(4):
                pe.wait_ge(kk_square, p + 1)
                token_sums(aux[:, 1, 32 + 8 * p:40 + 8 * p], tmp[:, p % 2, :], 2).then_inc(kk_sum, 1)
            pe.wait_ge(kk_floor, 1)
            pe.wait_ge(rows_ready, 1)
            pe.wait_ge(m_silu, 8)
            every_tile_taken(pe, m_gate_l)
            for b in range(TB):
                last = pe.transpose(lin[:, 3, MH * b:MH * b + MH], rows[:, 0, b * P:(b + 1) * P], ident[0:MH, 0:MH])
            last.then_inc(em_turned, 1)

            def weigh(n):
                h, j = n // TB, n % TB
                pe.wait_ge(m_p, n + 1)
                if j == 0 and h >= 2:
                    pe.wait_ge(m_head, h - 1)
                to = lin[:, 2 * (h % 2), j * P:T]
                last = pe.matmul(to, m_vtok[:, j, h * P:(h + 1) * P], ptT[:, n % 4, 0:T - j * P], start=(j == 0),
                                 stop=(j == TB - 1))
                if j == TB - 1:
                    for b in range(TB):
                        for a in range(b + 1):
                            last = pe.matmul(lin[:, 1, TB * h + b:TB * h + b + 1], ptT[:, a, (b - a) * P:(b - a + 1) * P],
                                             ones[:, 0:1], start=(a == 0), stop=(a == b))
                last.then_inc(m_pv, 1)

            for n in range(MH * TB):
                h, j = n // TB, n % TB
                w = T - j * P
                if n >= 2:
                    pe.wait_ge(m_exp, n - 1)
                pe.matmul(aux[:, 2 + n % 2, 0:w], ident[:, h:h + 1].broadcast_to([P, P]), rows_whole[:, 1, T - w:T],
                          start=True, stop=False)
                pe.matmul(aux[:, 2 + n % 2, 0:P], later_key[:, :], ident_b[:, :], start=False, stop=True)\
                  .then_inc(m_e, 1)
                if n >= 2:
                    pe.wait_ge(m_p, n - 1)
                pe.matmul(aux[:, n % 2, 0:w], m_qk[:, 4 + h, j * P:(j + 1) * P], m_qk[:, h, j * P:T], start=True,
                          stop=True).then_inc(m_s, 1)
                if n >= 2:
                    weigh(n - 2)
            weigh(MH * TB - 2)
            weigh(MH * TB - 1)
            pe.wait_ge(inv_ready, inverse_of("m"))
            for h in range(MH + 1):
                if h < MH:
                    if h >= 2:
                        pe.wait_ge(m_normed, h - 1)
                    spread_tokens(aux[:, h % 2, :], 12 + TB * h)
                if h:
                    pe.wait_ge(m_normed, h)
                    if h >= 3:
                        pe.wait_ge(gn_centered, h - 2)
                    pe.matmul(aux[:, 2 + (h - 1) % 2, :], ones[:, :], m_h[:, h - 1, :], start=True, stop=True)\
                      .then_inc(gn_mean, 1)
            for h in range(MH):
                pe.wait_ge(gn_square, h + 1)
                token_sums(lin[:, 3, TB * h:TB * (h + 1)], tmp[:, h % 2, :]).then_inc(gn_var, 1)
            pe.wait_ge(inv_ready, inverse_of("gn"))
            for h in range(MH):
                if h >= 2:
                    pe.wait_ge(gn_done, h - 1)
                spread_tokens(aux[:, h % 2, :], 44 + TB * h)

            pe.wait_ge(gn_done, MH)
            pe.wait_ge(r_act, 2)
            for q in range(8):
                if q >= 4:
                    pe.wait_ge(r_sig, q - 3)
                pe.matmul(aux[:, q % 4, :], up_w[:, q // 2 * P:(q // 2 + 1) * P], tmp[:, q % 2, :], start=True,
                          stop=True).then_inc(r_pre, 1)
            pe.wait_ge(r_sig, 8)
            def spread_kk(p):
                pe.wait_ge(pairs_ready, pairs_of(f"kk {p // 2}", p % 2))
                if p:
                    pe.wait_ge(packed, p)
                spread_pair(aux[:, 3, :], tmp[:, 0, :])

            def sum_bonus(p):
                pe.wait_ge(bonus_in, p + 1)
                if p:
                    pe.wait_ge(bonus_done, p)
                pe.matmul(lin[:, 2, :], halves[:, :], RK(p // 2, p % 2)[:, :, 0, :], start=True, stop=True)\
                  .then_inc(bonus_sum, 1)

            for p in range(2):
                spread_kk(p)
                sum_bonus(p)
            for half in range(2):
                for pl in range(2):
                    pe.wait_ge(bonus_done, 2 * half + 2)
                    if half:
                        pe.wait_ge(mix_ready, 6)
                    for b in range(2):
                        for c in range(4):
                            last = pe.transpose(aux[:, 2 * pl + b, c * P:(c + 1) * P],
                                                BK[:, pl, 4 * b + c, :, :].rearrange("p a b -> p (a b)"), ident[:, :])
                        last.then_inc(bt_turned, 1)
                for pl in range(2):
                    if pl:
                        pe.wait_ge(g_masked, 4 * (2 * half + 1))
                    for b in range(2):
                        for c in range(4):
                            for hh in range(2):
                                rws = slice(64 * hh, 64 * hh + 64)
                                last = pe.matmul(lin[:, 2 * hh + b, c * P:(c + 1) * P],
                                                 BK[rws, pl, 4 * b + c, :, :].rearrange("p a b -> p (a b)"),
                                                 RK(half, pl)[rws, 4 * b + c, :, :].rearrange("p a b -> p (a b)"),
                                                 start=True, stop=True)
                                if c == 3:
                                    last.then_inc(g_built, 1)
                bank = (aux, lin)
                pe.wait_ge(bt_done, 4 * (half + 1))

                def units(pl, first, lhs, rhs):
                    for u in range(16):
                        last = pe.matmul(bank[pl][half64, first + u // 8, u % 8 * CH:(u % 8 + 1) * CH], lhs(u), rhs(u),
                                         start=True, stop=True)
                    return last

                for pl in range(2):
                    pe.wait_ge(xt_first, 2 * half + pl + 1)
                    pe.wait_ge(lower_zero, half + 1)
                    units(pl, 2, lambda u: XT[pl][:, u, :], lambda u: ident[:, 0:CH]).then_inc(x_first, 1)
                for m in range(5):
                    for pl in range(2):
                        n = (5 * half + m) * 2 + pl
                        if m == 0:
                            pe.wait_ge(x_copied, 2 * half + pl + 1)
                        else:
                            pe.wait_ge(iv_xd, (4 * half + m - 1) * 2 + pl + 1)
                            pe.wait_ge(iv_xtd, n - 1)
                        units(pl, 0, lambda u: G[:, pl, u // NC, u % NC, CH:2 * CH], lambda u: X[pl][:, u, :])\
                            .then_inc(iv_y, 1)
                    for pl in range(2):
                        n = (5 * half + m) * 2 + pl
                        pe.wait_ge(iv_t, n + 1)
                        if m < 4:
                            units(pl, 2, lambda u: XT[pl][:, u, :], lambda u: T1(half, pl)[:, u, :]).then_inc(iv_x, 1)
                        units(pl, 0, lambda u: T1(half, pl)[:, u, :], lambda u: XT[pl][:, u, :]).then_inc(iv_xt, 1)
                pe.wait_ge(iv_xtd, 10 * (half + 1))
                for pl in range(2):
                    for b in range(2):
                        for c in range(4):
                            at = (8 + 2 * half + pl) * T + (4 * b + c) * CH - CH
                            last = pe.transpose(aux[:, 2 * pl + b, c * P:(c + 1) * P], mix[:, at:at + P], ident[:, :])
                        last.then_inc(uv_turned, 1)
                pe.wait_ge(uv_zero, half + 1)
                pe.wait_ge(uv_done, 4 * (half + 1))
                for c in range(NC):
                    n = NC * half + c
                    s_now = state[:, c % 2, :, :]
                    if c:
                        pe.wait_ge(s_new, (NC + 1) * half + c + 1)
                    else:
                        pe.wait_ge(s_new, (NC + 1) * half + 1)
                    for g in range(4):
                        pl, hh = g // 2, g % 2
                        to = aux[half64, 0, g * CH:(g + 1) * CH]
                        pe.matmul(to, RK(half, pl)[:, c, 1, :], s_now[:, g, :], start=True, stop=False)
                        last = pe.matmul(to, G[:, pl, hh, c, CH:2 * CH], UV[:, c, g, :], start=False, stop=True)
                    last.then_inc(w_sum, 1)
                    pe.wait_ge(w_taken, n + 1)
                    for g in range(4):
                        pl, hh = g // 2, g % 2
                        last = pe.matmul(aux[half64, 1, g * CH:(g + 1) * CH], G[:, pl, hh, c, CH:2 * CH],
                                         w_sb(half)[:, g, :], start=True, stop=True)
                    last.then_inc(u_sum, 1)
                    pe.wait_ge(u_taken, n + 1)
                    for g in range(4):
                        last = pe.matmul(aux[:, 2, g * CH:(g + 1) * CH], BKt[:, g // 2, c, :], UV[:, c, g, :],
                                         start=True, stop=True)
                    last.then_inc(s_sum, 1)
                    for g in range(4):
                        pl, hh = g // 2, g % 2
                        to = lin[64 * hh:64 * hh + 64, pl, c * CH:(c + 1) * CH]
                        pe.matmul(to, s_now[:, g, :], RK(half, pl)[:, c, 0, :], start=True, stop=False)
                        last = pe.matmul(to, UV[:, c, g, :], G[:, pl, hh, c, 0:CH], start=False, stop=True)
                    last.then_inc(y_sum, 1)
                    if half == 0 and c in (1, 4):
                        spread_kk(2 + c // 4)
                    if half == 0 and c in (3, 6):
                        sum_bonus(2 + c // 6)
                pe.wait_ge(s_new, (NC + 1) * (half + 1))
                for pl in range(2):
                    p = 2 * half + pl
                    pe.wait_ge(y_copied, p + 1)
                    if pl:
                        pe.wait_ge(y_centered, p)
                    pe.matmul(aux[:, 0, :], halves[:, :], y_sb[:, pl, :], start=True, stop=True).then_inc(y_mean, 1)
                for pl in range(2):
                    p = 2 * half + pl
                    pe.wait_ge(y_square, p + 1)
                    token_sums(aux[:, 1, 8 * pl:8 * pl + 8], tmp[:, pl, :], 2).then_inc(y_var, 1)
                    pe.matmul(aux[:, 2 + pl, :], up_g[:, 0, p * P:(p + 1) * P], lora[:, 1, :], start=True, stop=False)
                    pe.matmul(aux[:, 2 + pl, :], up_g[:, 1, p * P:(p + 1) * P], lora[:, 2, :], start=False, stop=True)\
                      .then_inc(y_gate, 1)
                pe.wait_ge(y_root, half + 1)
                for pl in range(2):
                    pe.wait_ge(pairs_ready, pairs_of(f"y {half}", pl))
                    spread_pair(aux[:, pl, :], tmp[:, pl, :])
            pe.wait_ge(mem_in, 16)
            for g in range(KT // 2):
                if g >= 2:
                    pe.wait_ge(mem_done, g - 1)
                for j in range(4):
                    k = 2 * g + j // 2
                    last = pe.transpose(lin[:, 2 + g % 2, j * P:(j + 1) * P], mem_rows[:, j % 2, k * P:(k + 1) * P],
                                        ident[:, :])
                last.then_inc(mem_turned, 1)
            pe.wait_ge(mem_done, KT // 2)
            pe_linear(mix_out_l, act_hi, act_lo, (mix_ready, 0))

        def pool_masks(pool, step):
            every_tile_taken(pool, ffn_out_l)
            step(pool.memset(rows_whole[:, 1, :], 0.0))
            step(pool.memset(up_g[:, 1, :], 0.0))
            pool.memset(eps_col[:, 1:2], GN_EPS)
            for r in (0, 64):
                rws = slice(r, r + 64)
                pool.tensor_copy(g_mask[rws, 0:CH], upto[rws, r:r + CH])
                step(pool.tensor_copy(g_mask[rws, CH:2 * CH], before[rws, r:r + CH]))
            for m in range(6):
                b = 1 << m
                lev = level[:, m, :]
                step(pool.memset(lev, 0.0))
                v = lev.rearrange("p (g w) -> p g w", w=2 * b)
                cols = v[:, :, b:2 * b] if m == 0 else v[:, :, 0:b]
                step(pool.memset(cols, 1.0))
                first = 0 if m == 0 else b
                n = CH // (2 * b)
                step(pool.affine_select(out=cols, in_=cols, compare_op=ALU.is_ge, fill=0.0, base=-first,
                                        pattern=[[-2 * b, n], [0, b]], channel_multiplier=1))
                ins = pool.affine_select(out=cols, in_=cols, compare_op=ALU.is_ge, fill=0.0, base=first + b - 1,
                                         pattern=[[2 * b, n], [0, b]], channel_multiplier=-1)
                step(ins)
            pool.nop().then_inc(masks_ready, 1)

        def T1(half, pl):
            return part((7680, 9728)[pl] + 1024 * half, 16, CH)

        def w_sb(half):
            return tmp[:, 1, 0:4 * CH].rearrange("p (g n) -> p g n", n=CH)

        def dve_mix(dve, step):
            dve_norm(2, "norm_mix_2", step)
            for q in range(8):
                slab_ready(dve, m_qk_l, q // 4, q // 2 % 2)
                tile_taken(dve, m_qk_l, q // 4, q // 2 % 2, q % 2)
                for j in range(4):
                    tap = tab[:, 2, 8 * j + q:8 * j + q + 1]
                    if j == 0:
                        step(dve.tensor_scalar(m_qk[:, q, :], pad[:, q % 2, 0:T], tap, col("m_conv_b_2", q), ALU.mult,
                                               ALU.add))
                    else:
                        ins = dve.scalar_tensor_tensor(m_qk[:, q, :], pad[:, q % 2, j:j + T], tap, m_qk[:, q, :],
                                                       ALU.mult, ALU.add)
                        if j < 3:
                            step(ins)
                ins.then_inc(m_conv, 1)
            for q in range(15):
                layer, i, s, t = (rkv_l, q // 4, q // 2 % 2, q % 2) if q < 12 else (lora_l, 0, (q - 12) // 2,
                                                                                   (q - 12 + 1) // 2)
                slab_ready(dve, layer, i, s)
                tile_taken(dve, layer, i, s, t)
                to = rkv[:, q, :] if q < 12 else lora[:, q - 12, :]
                mu = col("r_mu_2", q) if q < 14 else col("r_mu_tail", 0)
                step(dve.tensor_tensor(tmp[:, q % 2, :], pad[:, q % 2, 2:2 + T], pad[:, q % 2, 3:3 + T], ALU.subtract))
                dve.scalar_tensor_tensor(to, tmp[:, q % 2, :], mu, pad[:, q % 2, 3:3 + T], ALU.mult, ALU.add)\
                   .then_inc(r_shift, 1)
            dve.wait_ge(f_logits, 2)
            dve.tensor_tensor(mg[:, 0, :, :], aux[:, 1, 0:32].rearrange("p (b h) -> p b h", h=8),
                              f_bias[:, 1:2, :].broadcast_to([P, TB, 8]), ALU.add).then_inc(f_biased, 1)
            dve.wait_ge(f_ln, 2)
            dve.scalar_tensor_tensor(mg[:, 3, :, :], mg[:, 0, :, :], 0.0, mg[:, 1, :, :], ALU.min, ALU.subtract)\
               .then_inc(f_ready, 1)
            dve.wait_ge(f_sum, 2)
            b_sum = aux[:, 0, 0:32].rearrange("p (b h) -> p b h", h=8)[:, :, MH:2 * MH]
            dve.tensor_tensor(mg[:, 4, :, 0:MH], mg[:, 0, :, 0:MH], b_sum, ALU.subtract).then_inc(u_ready, 1)
            dve.tensor_copy(mg[:, 4, :, MH:2 * MH], b_sum).then_inc(u_ready, 1)
            dve.wait_ge(u_turned, 1)
            dve.wait_ge(masks_ready, 1)
            step(dve.tensor_copy(rows[:, 0, :], aux[0:MH, 2, :]))
            step(dve.tensor_tensor_scan(rows[:, 1, :], rows[:, 0, :], rows[:, 0, :], -3.0e38, ALU.max, ALU.max))
            step(dve.scalar_tensor_tensor(rows[:, 0, :], aux[0:MH, 3, :], -1.0, rows[:, 1, :], ALU.mult, ALU.subtract))
            dve.tensor_scalar(rows[:, 1, :], rows[:, 1, :], -1.0, None, ALU.mult).then_inc(rows_ready, 1)
            dve.wait_ge(kk_sum, 4)
            dve.tensor_scalar(root[:, 76:108], aux[:, 1, 32:64], 1e-24, None, ALU.max).then_inc(kk_floor, 1)
            for n in range(MH * TB):
                h, w = n // TB, T - n % TB * P
                dve.wait_ge(m_s, n + 1)
                dve.wait_ge(m_exp, n + 1)
                if n >= 4:
                    dve.wait_ge(m_pv, TB * h)
                dve.scalar_tensor_tensor(ptT[:, n % 4, 0:w], aux[:, n % 2, 0:w], float(P) ** -0.5,
                                         decay_e[:, n % 2, 0:w], ALU.mult, ALU.mult).then_inc(m_p, 1)
            dve.wait_ge(m_den, 1)
            step(dve.tensor_tensor(root[:, 12:28].rearrange("p (h b) -> p h b", h=MH),
                                   root[:, 12:28].rearrange("p (h b) -> p h b", h=MH),
                                   root[:, 28:44].rearrange("p (b h) -> p h b", h=MH), ALU.max))
            dve.reciprocal(inv[:, 12:28], root[:, 12:28]).then_inc(inv_ready, 1)
            dve.wait_ge(m_head, MH)
            for h in range(MH + 1):
                if h < MH:
                    dve.wait_ge(wide_ready, spread_of("m", h))
                    dve.tensor_tensor(m_h[:, h, :], aux[:, h % 2, :], m_h[:, h, :], ALU.mult).then_inc(m_normed, 1)
                if h:
                    dve.wait_ge(gn_mean, h)
                    dve.scalar_tensor_tensor(m_h[:, h - 1, :], aux[:, 2 + (h - 1) % 2, :], -1.0 / P, m_h[:, h - 1, :],
                                             ALU.mult, ALU.add).then_inc(gn_centered, 1)
            dve.wait_ge(gn_centered, MH)
            for h in range(MH):
                ins = dve.scalar_tensor_tensor(m_o[:, h, :], m_h[:, h, :], col("m_norm_g_2", h), m_o[:, h, :], ALU.mult,
                                               ALU.mult)
            step(ins)
            dve.wait_ge(gn_root, 1)
            dve.reciprocal(inv[:, 44:60], root[:, 44:60]).then_inc(inv_ready, 1)
            for h in range(MH):
                dve.wait_ge(wide_ready, spread_of("gn", h))
                step(dve.tensor_tensor(act_hi[:, h, :], aux[:, h % 2, :], m_o[:, h, :], ALU.mult))
                step(dve.tensor_tensor(m_o[:, h, :], aux[:, h % 2, :], m_o[:, h, :], ALU.mult))
                dve.nop().then_inc(gn_done, 1)
                dve.tensor_tensor(act_lo[:, h, :], m_o[:, h, :], act_hi[:, h, :].bitcast(F32), ALU.subtract)\
                   .then_inc(mix_ready, 1)

            dve.wait_ge(r_sig, 8)
            dve.wait_ge(masks_ready, 1)
            dve.wait_ge(kk_root, 1)
            dve.reciprocal(inv[:, 76:108], root[:, 76:108]).then_inc(inv_ready, 1)
            step(dve.memset(end_decays[:, :, :, :], 0.0))
            chunks = lambda ap: ap.rearrange("p (c n) -> p c n", n=CH)

            def sum_decay(p):
                for c in range(NC):
                    cs = slice(c * CH, (c + 1) * CH)
                    ins = dve.tensor_tensor_scan(sw[:, p, cs], ones[:, 0:CH], sw[:, p, cs], 0.0, ALU.mult, ALU.add)
                ins.then_inc(z_cum, 1)

            def make_kk(p):
                half, pl = p // 2, p % 2
                r, k = rkv[:, p, :], rkv[:, 4 + p, :]
                kk, b, t = RK(half, pl)[:, :, 1, :], BK[:, pl, :, 0, :], BK[:, pl, :, 1, :]
                if half:
                    dve.wait_ge(y_sum, 1)
                step(dve.tensor_scalar(t, chunks(rate[:, p, :]), -1.0, col("r_ka_2", p), ALU.add, ALU.mult))
                dve.wait_ge(wide_ready, spread_of(f"kk {half}", pl))
                step(dve.scalar_tensor_tensor(kk, chunks(k), col("r_kk_2", p), chunks(aux[:, 3, :]), ALU.mult, ALU.mult))
                dve.tensor_tensor(b, kk, chunks(rate[:, p, :]), ALU.mult)
                step(dve.scalar_tensor_tensor(chunks(k), t, 1.0, chunks(k), ALU.add, ALU.mult))
                dve.scalar_tensor_tensor(RK(half, pl)[:, :, 0, :], chunks(r), col("r_rk_2", p), chunks(k), ALU.mult,
                                         ALU.mult).then_inc(bonus_in, 1)

            def pack(p):
                half, pl = p // 2, p % 2
                r, k, v = rkv[:, p, :], rkv[:, 4 + p, :], rkv[:, 8 + p, :]
                dve.wait_ge(z_exp, p + 1)
                dve.wait_ge(bonus_in, p + 1)
                fall, rise = chunks(sw[:, p, :]), chunks(rms_inv[:, :])
                dve.tensor_tensor(BK[:, pl, :, 0, :], BK[:, pl, :, 0, :], rise, ALU.mult)
                dve.tensor_tensor(BK[:, pl, :, 1, :], chunks(k), rise, ALU.mult)
                kk = RK(half, pl)[:, :, 1, 1:CH]
                dve.tensor_tensor(kk, kk, fall[:, :, 0:CH - 1], ALU.mult)
                for hh in range(2):
                    rws = slice(64 * hh, 64 * hh + 64)
                    dve.tensor_copy(end_decays[rws, half, :, 2 * pl + hh], fall[rws, :, CH - 1])
                dve.wait_ge(bonus_sum, p + 1)
                dve.tensor_tensor(RK(half, pl)[:, :, 0, :], chunks(r), fall, ALU.mult).then_inc(packed, 1)
                dve.wait_ge(packed, p + 1)
                dve.tensor_tensor(r, lin[:, 2, :], v, ALU.mult).then_inc(bonus_done, 1)

            for p in range(2):
                sum_decay(p)
                make_kk(p)
                pack(p)
            for half in range(2):
                end_decay = end_decays[:, half, :, :]
                for pl in range(2):
                    for b in range(2):
                        for hh in range(2):
                            dve.wait_ge(g_built, 4 * (2 * half + pl) + 2 * b + hh + 1)
                            dve.tensor_tensor(G[:, pl, hh, 4 * b:4 * b + 4, :],
                                              lin[:, 2 * hh + b, :].rearrange("p (c n) -> p c n", n=P),
                                              g_mask.unsqueeze(1).broadcast_to([P, 4, P]), ALU.mult)\
                               .then_inc(g_masked, 1)
                dve.wait_ge(g_masked, 8 * (half + 1))
                wide = lambda ap: ap.unsqueeze(1).broadcast_to([CH, 16, CH])
                for pl in range(2):
                    lbt = G[half64, pl, :, :, CH:2 * CH].rearrange("p a c n -> p (a c) n")
                    step(dve.tensor_tensor(XT[pl][half64], lbt, wide(level[:, 0, :]), ALU.mult))
                    dve.tensor_tensor(XT[pl][half64], wide(ident[half64, 0:CH]), XT[pl][half64], ALU.subtract).then_inc(xt_first, 1)
                bank = (aux, lin)
                banks = lambda pl, a: bank[pl][half64, a:a + 2, :].rearrange("p a (u n) -> p (a u) n", n=CH)
                for m in range(5):
                    for pl in range(2):
                        n = (5 * half + m) * 2 + pl
                        dve.wait_ge(iv_y, n + 1)
                        dve.tensor_tensor(T1(half, pl)[half64], banks(pl, 0), wide(level[:, m + 1, :]), ALU.mult)\
                           .then_inc(iv_t, 1)
                    for pl in range(2):
                        n = (5 * half + m) * 2 + pl
                        if m < 4:
                            dve.wait_ge(iv_x, (4 * half + m) * 2 + pl + 1)
                            dve.tensor_tensor(X[pl][half64], X[pl][half64], banks(pl, 2), ALU.subtract).then_inc(iv_xd, 1)
                        dve.wait_ge(iv_xt, n + 1)
                        if m < 4:
                            dve.tensor_tensor(XT[pl][half64], XT[pl][half64], banks(pl, 0), ALU.subtract).then_inc(iv_xtd, 1)
                        else:
                            lbt = G[half64, pl, :, :, CH:2 * CH].rearrange("p a c n -> p (a c) n")
                            dve.tensor_tensor(lbt, banks(pl, 0), XT[pl][half64], ALU.subtract).then_inc(iv_xtd, 1)
                dve.wait_ge(iv_xtd, 10 * (half + 1))
                dve.memset(w_sb(half)[64:128], 0.0)
                dve.memset(UV[0:64, :, :, :], 0.0).then_inc(uv_zero, 1)
                dve.memset(state[:, 0, :, :], 0.0).then_inc(s_new, 1)
                for c in range(NC):
                    n = NC * half + c
                    dve.wait_ge(s_sum, n + 1)
                    if c:
                        dve.wait_ge(y_sum, n)
                    nxt = state[:, (c + 1) % 2, :, :]
                    step(dve.tensor_tensor(nxt, state[:, c % 2, :, :],
                                           aux[:, 2, 0:256].rearrange("p (g n) -> p g n", n=CH), ALU.add))
                    dve.tensor_tensor(nxt, nxt, end_decay[:, c, :].unsqueeze(2).broadcast_to([P, 4, CH]), ALU.mult)\
                       .then_inc(s_new, 1)
                    dve.wait_ge(s_new, (NC + 1) * half + c + 2)
                    if half == 0 and c in (0, 3):
                        sum_decay(2 + c // 3)
                    if half == 0 and c in (2, 5):
                        make_kk(2 + c // 5)
                    if half == 0 and c in (3, 6):
                        pack(2 + c // 6)
                for pl in range(2):
                    p = 2 * half + pl
                    dve.wait_ge(y_mean, p + 1)
                    dve.scalar_tensor_tensor(y_sb[:, pl, :], aux[:, 0, :], -1.0 / CH, y_sb[:, pl, :], ALU.mult, ALU.add)\
                       .then_inc(y_centered, 1)
                dve.wait_ge(y_root, half + 1)
                dve.reciprocal(inv[:, 44:60], root[:, 44:60]).then_inc(inv_ready, 1)
                for pl in range(2):
                    p = 2 * half + pl
                    y = y_sb[:, pl, :]
                    dve.wait_ge(wide_ready, spread_of(f"y {half}", pl))
                    step(dve.scalar_tensor_tensor(y, y, col("r_gn_g_2", p), aux[:, pl, :], ALU.mult, ALU.mult))
                    step(dve.scalar_tensor_tensor(y, y, col("r_gn_b_2", p), rkv[:, p, :], ALU.add, ALU.add))
                    dve.wait_ge(y_gate, p + 1)
                    step(dve.tensor_tensor(act_hi[:, 4 + p, :], aux[:, 2 + pl, :], y, ALU.mult))
                    step(dve.tensor_tensor(y, aux[:, 2 + pl, :], y, ALU.mult))
                    dve.tensor_tensor(act_lo[:, 4 + p, :], y, act_hi[:, 4 + p, :].bitcast(F32), ALU.subtract)\
                       .then_inc(mix_ready, 1)

        (mem_in, mem_turned, mem_done, mem_added, mem_summed, mem_root, mem_ready) = (sem(n) for n in (
            "mem_in", "mem_turned", "mem_done", "mem_added", "mem_summed", "mem_root", "mem_ready"))
        f_conv, f_silu, y_ready, y_turned, rows_act, rows_dve = (sem(n) for n in (
            "f_conv", "f_silu", "y_ready", "y_turned", "rows_act", "rows_dve"))
        XSTEPS = XH * TB
        XB = HEADS * TB

        def act_rest(act, step):
            def take_kv(i, s):
                slab_ready(act, xkv_l, i, s)
                for t in range(2):
                    act.activation(kv_x[:, 4 * i + 2 * s + t, :], lin[:, 2 * s + t, 0:M_TOK], ACT.Copy)\
                       .then_inc(bank_free[s], 1)
                act_norm_square(3, mix_out_l, [2 * i + s])

            def take_q(i, s):
                slab_ready(act, xq_l, i, s)
                for t in range(2):
                    act.activation(q_x[:, 4 * i + 2 * s + t, :], lin[:, 2 * s + t, :], ACT.Copy)\
                       .then_inc(bank_free[s], 1)

            act_linear(xkv_l, take_kv, unroll=True)
            act_norm_root(3)
            act_norm_high(3)
            act_linear(xq_l, take_q, unroll=True)
            for g in range(4):
                act.wait_ge(v_turned, 2 * TB + g + 1)
                act.activation(v_xtok[:, g // 2, g % 2 * 512:(g % 2 + 1) * 512], aux[:, g, :], ACT.Copy)\
                   .then_inc(v_done, 1)

            def turned(n):
                h, i = n // TB, n % TB
                act.wait_ge(p_turned, XB + n + 1)
                if h >= 2:
                    act.wait_ge(o_ready, HEADS + 2 * (h - 1))
                act.activation(x_pT[:, h % 2, :, i * P:(i + 1) * P],
                               aux[:, 2 + n % 2, 0:2 * P].rearrange("p (m q) -> p m q", m=2), ACT.Copy)\
                   .then_inc(p_copied, 1)

            for n in range(XSTEPS):
                act.wait_ge(s_max, XB + n + 1)
                if n >= 4:
                    act.wait_ge(p_turned, XB + n - 3)
                step(act.activation(x_s[:, n % 4, :], aux[:, n % 2, 0:M_TOK], ACT.Exp, bias=x_stat[:, 1, n % 4:n % 4 + 1],
                                    scale=XHD ** -0.5, accum_out=x_stat[:, 2, n % 4:n % 4 + 1]))
                act.nop().then_inc(s_exp, 1)
                if n >= LAG:
                    turned(n - LAG)
            for n in range(XSTEPS - LAG, XSTEPS):
                turned(n)
            act_linear_square(xo_l, 4)
            act_norm_rest(4)
            step(act.activation(gpad[:, :, 0:2], ident[:, 0:4].rearrange("p (a b) -> p a b", a=2), ACT.Copy, scale=0.0))

            def take_up(i, s):
                if s == 0:
                    slab_ready(act, up_l, i, 0)
                    for t in range(2):
                        tile_taken(act, up_l, i - 1, 1, t)
                        act.activation(gpad[:, t, 2:2 + T], lin[:, t, :], ACT.Copy).then_inc(bank_free[0], 1)
                else:
                    for t in range(2):
                        act.wait_ge(f_conv, 2 * i + t + 1)
                        act.activation(gconv[:, t, :], gconv[:, t, :], ACT.Silu).then_inc(f_silu, 1)

            act_linear(up_l, take_up)
            act_linear_square(down_l, 5)
            act_norm_root(5)
            for n in range(0, 8, 2):
                act.wait_ge(y_turned, n + 1)
                act.activation(out_rows[:, n % 4, n // 4 * 512:(n // 4 + 1) * 512], (lin, aux)[n // 4][:, n % 4, :],
                               ACT.Copy).then_inc(rows_act, 1)

        def pe_rest(pe):
            pe.wait_ge(mem_added, KT)
            token_sums(aux[:, 2, :], rms_inv[:, 0:M_TOK]).then_inc(mem_summed, 1)
            pe.wait_ge(inv_ready, inverse_of("mem"))
            spread_tokens(aux[:, 3, :], 8, blocks=2)
            pe_linear(xkv_l, mem_hi, mem_lo, (mem_ready, 0))
            pe_norm(3)
            pe_linear(xq_l, act_hi, act_lo, (act_ready, 3 * KT))
            every_tile_taken(pe, xkv_l)
            for g in range(4):
                for j in range(4):
                    last = pe.transpose(aux[:, g, j * P:(j + 1) * P],
                                        kv_x[:, 8 + g % 2 * 4 + j, g // 2 * P:(g // 2 + 1) * P], ident[:, :])
                last.then_inc(v_turned, 1)
            every_tile_taken(pe, xq_l)

            def turn(n):
                h, i = n // TB, n % TB
                pe.wait_ge(s_diag, XB + n + 1)
                if n >= 2:
                    pe.wait_ge(p_copied, XB + n - 1)
                for m in range(2):
                    last = pe.matmul(aux[:, 2 + n % 2, m * P:(m + 1) * P], x_s[:, n % 4, m * P:(m + 1) * P],
                                     x_diag[:, n % 2, :], start=True, stop=True)
                last.then_inc(p_turned, 1)

            def x_values(h):
                pe.wait_ge(p_copied, XB + TB * (h + 1))
                if h >= 2:
                    pe.wait_ge(o_done, HEADS + 2 * (h - 1))
                for dt in range(2):
                    at = h * XHD + dt * P
                    for m in range(2):
                        last = pe.matmul(lin[:, 2 * (h % 2) + dt, :], v_xtok[:, m, at:at + P], x_pT[:, h % 2, m, :],
                                         start=(m == 0), stop=(m == 1))
                    last.then_inc(o_ready, 1)

            def x_scores(n):
                h, i = n // TB, n % TB
                if n >= 2:
                    pe.wait_ge(s_exp, XB + n - 1)
                else:
                    pe.wait_ge(v_done, 2 * TB + n + 1)
                for dt in range(2):
                    last = pe.matmul(aux[:, n % 2, 0:M_TOK], q_x[:, 2 * h + dt, i * P:(i + 1) * P], kv_x[:, 2 * h + dt, :],
                                     start=(dt == 0), stop=(dt == 1))
                last.then_inc(s_ready, 1)

            for n in range(XSTEPS + LAG + 1):
                if n < XSTEPS:
                    x_scores(n)
                if n == LAG:
                    pe.wait_ge(v_done, 2 * TB + 4)
                if LAG <= n < XSTEPS + LAG:
                    turn(n - LAG)
                if n > LAG and (n - LAG) % TB == 0:
                    x_values((n - LAG) // TB - 1)
            pe.wait_ge(o_done, HEADS + KT)
            pe_linear(xo_l, act_hi, act_lo)
            pe_norm(4)
            pe_linear(up_l, act_hi, act_lo, (act_ready, 4 * KT))
            pe_linear(down_l, hid2_hi, hid2_lo, (hid_ready, FT))
            pe_norm(5)
            every_tile_taken(pe, down_l)
            for n in range(8):
                k0, b = 4 * (n // 4), n % 4
                pe.wait_ge(y_ready, k0 + 4)
                for j in range(4):
                    last = pe.transpose((lin, aux)[n // 4][:, b, j * P:(j + 1) * P], y_fin[:, k0 + j, b * P:(b + 1) * P],
                                        ident[:, :])
                last.then_inc(y_turned, 1)

        def dve_mem_squares(dve, step):
            dve.wait_ge(mem_done, KT // 2)
            for k in range(KT):
                if k == 0:
                    dve.tensor_tensor(rms_inv[:, 0:M_TOK], memT[:, k, :], memT[:, k, :], ALU.mult).then_inc(mem_added, 1)
                else:
                    step(dve.tensor_tensor(tmp[:, 0, 0:M_TOK], memT[:, k, :], memT[:, k, :], ALU.mult))
                    dve.tensor_tensor(rms_inv[:, 0:M_TOK], rms_inv[:, 0:M_TOK], tmp[:, 0, 0:M_TOK], ALU.add)\
                       .then_inc(mem_added, 1)
                dve.wait_ge(mem_added, k + 1)

        def dve_mem_norm(dve, step):
            dve.wait_ge(mem_root, 1)
            dve.reciprocal(inv[:, 8:10], root[:, 8:10]).then_inc(inv_ready, 1)
            dve.wait_ge(wide_ready, spread_of("mem"))
            for k in range(KT):
                step(dve.scalar_tensor_tensor(memT[:, k, :], memT[:, k, :], col("norm_mem_2", k), aux[:, 3, 0:M_TOK],
                                              ALU.mult, ALU.mult))
                step(dve.tensor_copy(mem_hi[:, k, :], memT[:, k, :]))
                dve.tensor_tensor(mem_lo[:, k, :], memT[:, k, :], mem_hi[:, k, :].bitcast(F32), ALU.subtract)\
                   .then_inc(mem_ready, 1)

        def dve_rest(dve, step):
            dve_norm(3, "norm_x_2", step)

            def divide(n):
                dve.wait_ge(s_exp, XB + n + 1)
                if n >= 2:
                    dve.wait_ge(p_turned, XB + n - 1)
                step(dve.reciprocal(x_stat[:, 0, n % 4:n % 4 + 1], x_stat[:, 2, n % 4:n % 4 + 1]))
                dve.tensor_scalar(x_diag[:, n % 2, :], ident[:, :], x_stat[:, 0, n % 4:n % 4 + 1], None, ALU.mult)\
                   .then_inc(s_diag, 1)

            def head_out(h):
                for dt in range(2):
                    k, bank = 2 * h + dt, lin[:, 2 * (h % 2) + dt, :]
                    dve.wait_ge(o_ready, HEADS + k + 1)
                    step(dve.tensor_copy(act_hi[:, k, :], bank))
                    dve.tensor_tensor(act_lo[:, k, :], bank, act_hi[:, k, :].bitcast(F32), ALU.subtract)\
                       .then_inc(o_done, 1)

            for n in range(XSTEPS):
                dve.wait_ge(s_ready, XB + n + 1)
                step(dve.tensor_reduce(x_stat[:, 0, n % 4:n % 4 + 1], aux[:, n % 2, 0:M_TOK], AX.X, ALU.max))
                dve.tensor_scalar(x_stat[:, 1, n % 4:n % 4 + 1], x_stat[:, 0, n % 4:n % 4 + 1], -XHD ** -0.5, None,
                                  ALU.mult).then_inc(s_max, 1)
                if n >= 2:
                    divide(n - 2)
                if n % TB == 1 and n // TB >= 2:
                    head_out(n // TB - 2)
            divide(XSTEPS - 2)
            divide(XSTEPS - 1)
            head_out(XH - 2)
            head_out(XH - 1)
            add_to_residual(xo_l, 4)
            dve_norm(4, "norm_ffn_2", step)
            with dve.Fori(0, up_l.bodies) as i:
                step.enter(i, 6)
                for t in range(2):
                    tile_taken(dve, up_l, i, 0, t)
                    tap = lambda j: tab[:, 2, bass.ds(2 * i + (32 + FT * j + t), 1)]
                    step(dve.tensor_scalar(gconv[:, t, :], gpad[:, t, 0:T], tap(0), tap(3), ALU.mult, ALU.add))
                    step(dve.scalar_tensor_tensor(gconv[:, t, :], gpad[:, t, 1:1 + T], tap(1), gconv[:, t, :], ALU.mult,
                                                  ALU.add))
                    dve.scalar_tensor_tensor(gconv[:, t, :], gpad[:, t, 2:2 + T], tap(2), gconv[:, t, :], ALU.mult,
                                             ALU.add).then_inc(f_conv, 1)
                for t in range(2):
                    slab_ready(dve, up_l, i, 1)
                    dve.wait_ge(f_silu, 2 * i + t + 1)
                    at = 2 * i + t
                    step(dve.tensor_tensor(hid2_hi[:, bass.ds(at, 1), :], lin[:, 2 + t:3 + t, :], gconv[:, t:t + 1, :],
                                           ALU.mult))
                    dve.tensor_tensor(gconv[:, t, :], lin[:, 2 + t, :], gconv[:, t, :], ALU.mult).then_inc(bank_free[1], 1)
                    tile_taken(dve, up_l, i, 1, t)
                    dve.tensor_tensor(hid2_lo[:, bass.ds(at, 1), :], gconv[:, t:t + 1, :],
                                      hid2_hi[:, bass.ds(at, 1), :].bitcast(F32), ALU.subtract).then_inc(hid_ready, 1)
                    dve.wait_ge(hid_ready, FT + at + 1)
            step.leave(up_l.bodies)
            add_to_residual(down_l, 5)
            dve_norm(5, "norm_final_2", step, to=y_fin)
            for n in range(1, 8, 2):
                dve.wait_ge(y_turned, n + 1)
                dve.tensor_copy(out_rows[:, n % 4, n // 4 * 512:(n // 4 + 1) * 512], (lin, aux)[n // 4][:, n % 4, :])\
                   .then_inc(rows_dve, 1)

        def load_parameters(eng, part_of):
            eng.wait_ge(rows_zero, 1)
            for name, (t, row, n) in list(place.items())[part_of::2]:
                src = d[name] if name in d else None
                if name == "r_mu_tail":
                    eng.dma_start(raw_rows[row:row + 1, t, :], d["r_mu_2"][:, R_COLS - P:R_COLS]).then_inc(rows_in, 16)
                elif name in ("g_q", "g_k"):
                    for half in (0, 64):
                        eng.dma_start(raw_rows[row:row + 1, t, half:half + 64], src).then_inc(rows_in, 16)
                else:
                    flat = src.rearrange({1: "a -> a", 2: "a b -> (a b)", 3: "a b c -> (a b c)"}[len(src.shape)])
                    eng.dma_start(raw_rows[row:row + n, t, :], flat[0:n * P].rearrange("(r c) -> r c", c=P))\
                       .then_inc(rows_in, 16)

        block = ctx.enter_context(nc.Block())

        @block.sync
        def _(sp):
            for t in range(2):
                sp.dma_start(x_rows[:, 2 * t:2 * t + 2, :],
                             d["x"].rearrange("o (b p) c -> p (o b) c", p=P)[:, 2 * t:2 * t + 2, :]).then_inc(x_in, 16)
            load_parameters(sp, 1)
            for layer in layers:
                stream(sp, layer)
            for n in range(8):
                sp.wait_ge((rows_act, rows_dve)[n % 2], n // 2 + 1)
                c = slice(n // 4 * 512, (n // 4 + 1) * 512)
                sp.dma_start(out.rearrange("o (b p) c -> p (o b) c", p=P)[:, n % 4, c], out_rows[:, n % 4, c])\
                   .then_inc(stored, 16)
            sp.wait_ge(stored, 16 * 8)

        @block.gpsimd
        def _(pool):
            step = Steps(pool, pool_step)
            pool.memset(raw_rows[:, :, :], 0.0).then_inc(rows_zero, 1)
            pool.memset(ident[:, :], 0.0)
            pool.memset(ones[:, :], 1.0)
            pool.memset(upto[:, :], 1.0)
            pool.memset(before[:, :], 1.0)
            pool.memset(later_key[:, :], 0.0)
            pool.memset(ident_b[:, :], 0.0)
            pool.memset(eps_col[:, 0:2], EPS)
            step(pool.memset(halves[:, :], 0.0))
            pool.sem_inc(w_low, RING)
            pool.memset(halves[0:64, 0:64], 1.0)
            step(pool.memset(halves[64:128, 64:128], 1.0))
            pool.affine_select(out=ident[:, :], in_=ident[:, :], compare_op=ALU.not_equal, fill=1.0, base=0,
                               pattern=[[-1, P]], channel_multiplier=1)
            pool.affine_select(out=ident_b[:, :], in_=ident_b[:, :], compare_op=ALU.not_equal, fill=1.0, base=0,
                               pattern=[[-1, P]], channel_multiplier=1)
            pool.affine_select(out=upto[:, :], in_=upto[:, :], compare_op=ALU.is_ge, fill=0.0, base=0,
                               pattern=[[1, P]], channel_multiplier=-1)
            pool.affine_select(out=before[:, :], in_=before[:, :], compare_op=ALU.is_ge, fill=0.0, base=-1,
                               pattern=[[1, P]], channel_multiplier=-1)
            pool.affine_select(out=later_key[:, :], in_=later_key[:, :], compare_op=ALU.is_ge, fill=MASKED, base=0,
                               pattern=[[-1, P]], channel_multiplier=1).then_inc(consts, 1)
            for layer in layers[:9]:
                if layer is conv_out_l:
                    step(pool.memset(neg_c[:, :], 0.0))
                    pool.nop().then_inc(neg_c_zero, 1)
                if layer is attn_out_l:
                    pool.wait_ge(v_turned, TB)
                    step(pool.memset(qkv[0:64, 8:12, :], 0.0))
                    pool.wait_ge(qk_done, 8)
                    step(pool.memset(qkv[64:P, 4:8, :], 0.0))
                    pool.nop().then_inc(keys_zero, 1)
                pool_linear(layer)
            pool_masks(pool, step)
            for layer in layers[9:]:
                if layer is mix_out_l:
                    for half in range(2):
                        pool.wait_ge(g_built, 8 * (half + 1))
                        step(pool.memset(part(17920, 2048, rows=slice(64, P)), 0.0))
                        step(pool.memset(part(15872, 2048, rows=slice(64, P)), 0.0))
                        pool.nop().then_inc(lower_zero, 1)
                pool_linear(layer)


        @block.scalar
        def _(act):
            step = Steps(act, act_step)
            load_parameters(act, 0)
            act.dma_start(f_bias[:, 0, :], d["b_forget"].broadcast_to([P, 8])).then_inc(small_in, 16)
            act.dma_start(f_bias[:, 1, :], d["m_gate_b_2"].broadcast_to([P, 8])).then_inc(small_in, 16)
            act.sem_inc(w_used, RING)
            act.sem_inc(bank_free[0], 2)
            act.sem_inc(bank_free[1], 2)
            act_norm_square(0, None)
            round_unit(layers[0], 0, 0)
            round_unit(layers[0], 0, 1)
            act.wait_ge(tab_turned, 3)
            act.activation(tab[:, :, :], aux[:, 2, 0:3 * P], ACT.Copy).then_inc(tab_ready, 1)
            act_norm_rest(0)

            def take_glu(i, s):
                if s == 1:
                    for t in range(2):
                        slab_ready(act, glu_l, i, s)
                        if i:
                            tile_taken(act, glu_l, i - 1, 0, t)
                        act.activation(tmp[:, t, :], lin[:, 2 + t, :], ACT.Sigmoid).then_inc(bank_free[1], 1)

            def take_qkv(i, s):
                slab_ready(act, qkv_l, i, s)
                for t in range(2):
                    act.activation(qkv[:, 4 * i + 2 * s + t, :], lin[:, 2 * (s % 2) + t, :], ACT.Copy)\
                       .then_inc(bank_free[s % 2], 1)
                for t in (4 * i + 2 * s - 4, 4 * i + 2 * s - 3):
                    if t >= 0:
                        act.wait_ge(bank_free[(t // 2) % 2], qkv_l.s0 + 2 + 2 * (t // 4) + 1 + t % 2)
                        act.activation(sig[:, t, :], qkv[:, t, :], ACT.Square).then_inc(qk_square, 1)

            def take_gate(i, s):
                slab_ready(act, gate_l, i, s)
                for t in range(2):
                    act.activation(sig[:, 4 * i + 2 * s + t, :], lin[:, 2 * (s % 2) + t, :], ACT.Sigmoid)\
                       .then_inc(bank_free[s % 2], 1)
                if (i, s) == (1, 0):
                    for t in range(4):
                        act.wait_ge(ln_centered, t + 1)
                        act.activation(glu[:, t, 0:T], conv[:, t, :], ACT.Square).then_inc(ln_square, 1)
                if (i, s) == (0, 0):
                    take_v(0)
                    take_v(1)
                if (i, s) == (2, 0):
                    act.wait_ge(qk_summed, 8)
                    act.activation(root[:, 12:76], aux[:, 1, 32:96], ACT.Sqrt, scale=1.0 / HD, bias=eps_col[:, 0:1])\
                       .then_inc(qk_root, 1)
                    act.wait_ge(ln_var, 1)
                    act.activation(root[:, 4:4 + TB], aux[:, 1, 96:96 + TB], ACT.Sqrt, scale=1.0 / CONV_CH,
                                   bias=eps_col[:, 0:1]).then_inc(ln_root, 1)
                if (i, s) == (2, 1):
                    take_v(2)
                    take_v(3)

            def take_v(b):
                act.wait_ge(v_turned, b + 1)
                act.activation(v_tok[:, b, :], aux[:, 2 + b % 2, :], ACT.Copy).then_inc(v_done, 1)

            act_linear(glu_l, take_glu, unroll=True)
            act_linear(qkv_l, take_qkv, unroll=True)
            act_linear(forget_l, take_eight(forget_l), unroll=True)
            act_linear(gate_l, take_gate, unroll=True)

            for t in range(4):
                act.wait_ge(ln_scaled, t + 1)
                act.activation(conv[:, t, :], conv[:, t, :], ACT.Silu, bias=col("b_conv_ln", t)).then_inc(ln_silu, 1)
            act.wait_ge(f_biased, 1)
            step(act.activation(lf[:, 1, :, :], lf[:, 0, :, :], ACT.Abs))
            step(act.activation(lf[:, 2, :, :], lf[:, 1, :, :], ACT.Exp, scale=-1.0))
            act.activation(lf[:, 1, :, :], lf[:, 2, :, :], ACT.Ln, bias=ones[:, 0:1]).then_inc(f_ln, 1)
            act_linear(conv_out_l)

            act.wait_ge(inv_ready, inverse_of("qk"))
            for t in range(8):
                if t >= 2:
                    act.wait_ge(wide_ready, spread_of("qk", t - 2))
                repeat_pair(tmp[:, t % 2, :], 12 + 8 * t)

            def turned(n):
                h, i = n // TB, n % TB
                act.wait_ge(p_turned, n + 1)
                if h:
                    act.wait_ge(o_ready, h)
                act.activation(glu[:, 0:i + 1, i * P:(i + 1) * P],
                               aux[:, 2 + n % 2, 0:(i + 1) * P].rearrange("p (j q) -> p j q", q=P), ACT.Copy)\
                   .then_inc(p_copied, 1)

            def head_high(h):
                act.wait_ge(o_ready, h + 1)
                r = slice(64 * (h % 2), 64 * (h % 2) + 64)
                act.activation(br_hi[r, h // 2, :], lin[r, 2 + h % 2, :], ACT.Copy).then_inc(o_high, 1)

            for n in range(HEADS * TB):
                h, i = n // TB, n % TB
                if i == 0:
                    act.wait_ge(cb_ready, h + 1)
                    if h >= 2:
                        act.wait_ge(s_taken, TB * (h - 1))
                    act.activation(conv[:, 2 + h % 2, :], lin[:, h % 2, :], ACT.Copy).then_inc(cb_copied, 1)
                act.wait_ge(s_max, n + 1)
                step(act.activation(score(n)[:, 0:(i + 1) * P], score(n)[:, 0:(i + 1) * P], ACT.Exp,
                                    bias=stat[:, 1, n % 4:n % 4 + 1], accum_out=stat[:, 2, n % 4:n % 4 + 1]))
                act.nop().then_inc(s_exp, 1)
                if n >= LAG:
                    turned(n - LAG)
                if n >= 2 * TB and n % TB == 0:
                    head_high(n // TB - 2)
            for n in range(HEADS * TB - LAG, HEADS * TB):
                turned(n)
                if n == HEADS * TB - 2:
                    head_high(HEADS - 2)
            head_high(HEADS - 1)
            act_linear(attn_out_l)
            act_linear_square(out_l, 1)
            act_norm_rest(1)

            def take_ff(i, s):
                if s == 0:
                    slab_ready(act, ffn_in_l, i, s)
                    for t in range(2):
                        tile_taken(act, ffn_in_l, i - 1, 1, t)
                        act.activation(ffn_tmp[:, t, :], lin[:, t, :], ACT.Silu).then_inc(bank_free[0], 1)
            act_linear(ffn_in_l, take_ff)
            act_linear_square(ffn_out_l, 2)
            act_mix(act, step)
            act_rest(act, step)

        @block.tensor
        def _(pe):
            pe.wait_ge(consts, 1)
            pe.wait_ge(x_in, 32)
            for k in range(KT):
                if k >= 2:
                    pe.wait_ge(x_done, k - 1)
                for b in range(TB):
                    last = pe.transpose(aux[:, k % 2, b * P:(b + 1) * P], x_rows[:, b, k * P:(k + 1) * P], ident[:, :])
                last.then_inc(x_turned, 1)
            pe.wait_ge(rows_in, 16 * (len(place) + 2))
            for t in range(3):
                pe.transpose(aux[:, 2, t * P:(t + 1) * P], raw_rows[:, t, :], ident[:, :]).then_inc(tab_turned, 1)
            pe.wait_ge(x_done, KT)
            pe_norm(0)
            pe_linear(glu_l, act_hi, act_lo, (act_ready, 0))
            pe_linear(qkv_l, act_hi, act_lo)
            pe_linear(forget_l, act_hi, act_lo)
            for t in range(8):
                pe.wait_ge(qk_square, t + 1)
                token_sums(aux[:, 1, 32 + 8 * t:40 + 8 * t], sig[:, t, :], 2).then_inc(qk_summed, 1)
            turn_eight(1)

            def turn_v(b):
                if b >= 2:
                    pe.wait_ge(v_done, b - 1)
                for t in range(4):
                    last = pe.transpose(aux[:, 2 + b % 2, t * P:(t + 1) * P], qkv[:, 8 + t, b * P:(b + 1) * P],
                                        ident[:, :])
                last.then_inc(v_turned, 1)

            turn_v(0)
            turn_v(1)
            pe_linear(gate_l, act_hi, act_lo, bodies=(0, 1))
            pe.wait_ge(conv_step, 4 * CONV_W)
            for t in range(4):
                last = pe.matmul(aux[:, 0, :], ones[:, :], conv[:, t, :], start=(t == 0), stop=(t == 3))
            last.then_inc(ln_mean, 1)
            pe_linear(gate_l, act_hi, act_lo, bodies=(1, 2))
            pe.wait_ge(ln_square, 4)
            pe.wait_ge(f_biased, 1)
            for b in range(TB):
                for t in range(4):
                    last = pe.matmul(aux[:, 1, 96 + b:97 + b], glu[:, t, b * P:(b + 1) * P], ones[:, 0:1], start=(t == 0),
                                     stop=(t == 3))
            last.then_inc(ln_var, 1)
            turn_v(2)
            turn_v(3)
            pe_linear(gate_l, act_hi, act_lo, bodies=(2, 3))
            pe.wait_ge(inv_ready, inverse_of("ln"))
            spread_tokens(aux[:, 0, :], 4)
            pe_linear(gate_l, act_hi, act_lo, bodies=(3, 4))
            pe_linear(conv_out_l, br_hi, br_lo, (br_ready, 0))

            pe.wait_ge(f_ready, 1)
            for b in range(TB):
                for a in range(b + 1):
                    last = pe.matmul(aux[:, 1, 8 * b:8 * b + 8], upto[:, :] if a == b else ones[:, :], lf[:, 3, a, :],
                                     start=(a == 0), stop=(a == b))
            last.then_inc(f_sum, 1)
            pe.wait_ge(c_ready, 1)
            for b in range(TB):
                last = pe.transpose(aux[0:HEADS, 0, b * P:(b + 1) * P], csum[:, b, :], ident[:, :])
            last.then_inc(c_turned, 1)
            pe.wait_ge(v_done, TB)
            for t in range(8):
                if t >= 2:
                    pe.wait_ge(qk_done, t - 1)
                pe.wait_ge(pairs_ready, pairs_of("qk", t))
                spread_pair(aux[:, 2 + t % 2, :], tmp[:, t % 2, :])
            pe.wait_ge(qk_done, 8)
            every_tile_taken(pe, conv_out_l)

            def scores(n):
                h, i = n // TB, n % TB
                if n >= 2:
                    pe.wait_ge(s_taken, n - 1)
                pe.matmul(aux[:, n % 2, 0:(i + 1) * P], qkv[:, h // 2, i * P:(i + 1) * P],
                          qkv[:, 4 + 4 * (h % 2) + h // 2, 0:(i + 1) * P], start=True, stop=False)
                pe.matmul(aux[:, n % 2, i * P:(i + 1) * P], ident_b[:, :], later_key[:, :], start=False, stop=True)\
                  .then_inc(s_ready, 1)

            def key_bias(h):
                if h >= 2:
                    pe.wait_ge(cb_copied, h - 1)
                pe.matmul(lin[:, h % 2, :], ident[:, h:h + 1].broadcast_to([P, P]), neg_c[:, :], start=True,
                          stop=True).then_inc(cb_ready, 1)

            def turn(n):
                h, i = n // TB, n % TB
                pe.wait_ge(s_diag, n + 1)
                if n >= 2:
                    pe.wait_ge(p_copied, n - 1)
                for j in range(i + 1):
                    last = pe.matmul(aux[:, 2 + n % 2, j * P:(j + 1) * P], score(n)[:, j * P:(j + 1) * P],
                                     diag[:, n % 2, :], start=True, stop=True)
                last.then_inc(p_turned, 1)

            def values(h):
                pe.wait_ge(p_copied, TB * (h + 1))
                if h >= 2:
                    pe.wait_ge(o_done, h - 1)
                for j in range(TB):
                    last = pe.matmul(lin[64 * (h % 2):64 * (h % 2) + 64, 2 + h % 2, j * P:T],
                                     v_tok[:, j, h * HD:(h + 1) * HD], glu[:, j, j * P:T],
                                     start=(j == 0), stop=(j == TB - 1))
                last.then_inc(o_ready, 1)

            pe.wait_ge(c_rows, 1)
            key_bias(0)
            pe.wait_ge(keys_zero, 1)
            for n in range(HEADS * TB + LAG + 1):
                if n < HEADS * TB:
                    scores(n)
                if n % TB == 1 and n // TB + 1 < HEADS:
                    key_bias(n // TB + 1)
                if LAG <= n < HEADS * TB + LAG:
                    turn(n - LAG)
                if n > LAG and (n - LAG) % TB == 0:
                    values((n - LAG) // TB - 1)
            pe.wait_ge(o_done, HEADS)
            pe_linear(attn_out_l, br_hi, br_lo)
            pe_linear(out_l, act_hi, act_lo, (m_ready, 0))
            pe_norm(1)
            pe_linear(ffn_in_l, act_hi, act_lo, (act_ready, KT))
            pe_linear(ffn_out_l, hid_hi, hid_lo, (hid_ready, 0))
            pe_mix(pe)
            pe_rest(pe)

        @block.vector
        def _(dve):
            step = Steps(dve, dve_step)
            for k in range(KT):
                dve.wait_ge(x_turned, k + 1)
                dve.tensor_copy(xT[:, k, :], aux[:, k % 2, :]).then_inc(x_done, 1)
            dve_norm(0, "g_mix", step)
            step(dve.tensor_scalar(q_gain, col("g_q", 0), HD ** -0.5, None, ALU.mult))
            step(dve.memset(glu[:, :, 0:PAD], 0.0))
            for i in range(2):
                for t in range(2):
                    slab_ready(dve, glu_l, i, 0)
                    tile_taken(dve, glu_l, i, 1, t)
                    dve.tensor_tensor(glu[:, 2 * i + t, PAD:PAD + T], lin[:, t, :], tmp[:, t, :], ALU.mult)\
                       .then_inc(bank_free[0], 1)
            tile_taken(dve, glu_l, 1, 0, 1)
            for j in range(CONV_W):
                for t in range(4):
                    tap = tab[:, 1, 4 * j + t:4 * j + t + 1]
                    if j == 0:
                        dve.tensor_scalar(conv[:, t, :], glu[:, t, 0:T], tap, col("b_dw", t), ALU.mult, ALU.add)\
                           .then_inc(conv_step, 1)
                    else:
                        dve.wait_ge(conv_step, 4 * (j - 1) + t + 1)
                        dve.scalar_tensor_tensor(conv[:, t, :], glu[:, t, j:j + T], tap, conv[:, t, :], ALU.mult,
                                                 ALU.add).then_inc(conv_step, 1)
            dve.wait_ge(f_logits, 1)
            dve.wait_ge(small_in, 32)
            dve.tensor_tensor(lf[:, 0, :, :], aux[:, 1, 0:32].rearrange("p (b h) -> p b h", h=8),
                                   f_bias[:, 0:1, :].broadcast_to([P, TB, 8]), ALU.add).then_inc(f_biased, 1)
            dve.wait_ge(ln_mean, 1)
            for t in range(4):
                dve.scalar_tensor_tensor(conv[:, t, :], aux[:, 0, :], -1.0 / CONV_CH, conv[:, t, :], ALU.mult, ALU.add)\
                   .then_inc(ln_centered, 1)
            dve.wait_ge(qk_root, 1)
            dve.reciprocal(inv[:, 12:76], root[:, 12:76]).then_inc(inv_ready, 1)
            dve.wait_ge(ln_root, 1)
            dve.reciprocal(inv[:, 4:4 + TB], root[:, 4:4 + TB]).then_inc(inv_ready, 1)
            dve.wait_ge(wide_ready, spread_of("ln"))
            for t in range(4):
                dve.scalar_tensor_tensor(conv[:, t, :], conv[:, t, :], col("g_conv_ln", t), aux[:, 0, :], ALU.mult,
                                         ALU.mult).then_inc(ln_scaled, 1)
            for t in range(4):
                dve.wait_ge(ln_silu, t + 1)
                step(dve.tensor_copy(br_hi[:, t, :], conv[:, t, :]))
                dve.tensor_tensor(br_lo[:, t, :], conv[:, t, :], br_hi[:, t, :].bitcast(F32), ALU.subtract)\
                   .then_inc(br_ready, 1)
            dve.wait_ge(f_ln, 1)
            dve.scalar_tensor_tensor(lf[:, 3, :, :], lf[:, 0, :, :], 0.0, lf[:, 1, :, :], ALU.min, ALU.subtract)\
               .then_inc(f_ready, 1)
            for s in range(4):
                slab_ready(dve, conv_out_l, 0, s)
                for t in range(2):
                    g = sig[:, 2 * s + t, :]
                    dve.tensor_tensor(g, lin[:, 2 * (s % 2) + t, :], g, ALU.mult).then_inc(bank_free[s % 2], 1)

            dve.wait_ge(f_sum, 1)
            dve.tensor_copy(csum[:, :, :], aux[:, 1, 0:32].rearrange("p (b h) -> p b h", h=8)).then_inc(c_ready, 1)
            dve.wait_ge(c_turned, 1)
            dve.wait_ge(neg_c_zero, 1)
            dve.tensor_scalar(neg_c[0:HEADS, :], aux[0:HEADS, 0, :], -1.0, None, ALU.mult).then_inc(c_rows, 1)
            for t in range(8):
                dve.wait_ge(wide_ready, spread_of("qk", t))
                if t < 4:
                    dve.scalar_tensor_tensor(qkv[:, t, :], qkv[:, t, :], q_gain, aux[:, 2 + t % 2, :], ALU.mult, ALU.mult)\
                       .then_inc(qk_done, 1)
                else:
                    gain, wide = col("g_k", 0), aux[:, 2 + t % 2, :]
                    for rws, to in ((slice(64, P), t + 4), (slice(0, 64), t)):
                        ins = dve.scalar_tensor_tensor(qkv[rws, to, :], qkv[rws, t, :], gain[rws], wide[rws], ALU.mult,
                                                       ALU.mult)
                    ins.then_inc(qk_done, 1)

            def divide(n):
                dve.wait_ge(s_exp, n + 1)
                if n >= 2:
                    dve.wait_ge(p_turned, n - 1)
                step(dve.reciprocal(stat[:, 0, n % 4:n % 4 + 1], stat[:, 2, n % 4:n % 4 + 1]))
                dve.tensor_scalar(diag[:, n % 2, :], ident[:, :], stat[:, 0, n % 4:n % 4 + 1], None, ALU.mult)\
                   .then_inc(s_diag, 1)

            def head_out(h):
                r = slice(64 * (h % 2), 64 * (h % 2) + 64)
                dve.wait_ge(o_high, h + 1)
                dve.tensor_tensor(br_lo[r, h // 2, :], lin[r, 2 + h % 2, :], br_hi[r, h // 2, :].bitcast(F32),
                                  ALU.subtract).then_inc(o_done, 1)

            for n in range(HEADS * TB):
                h, i = n // TB, n % TB
                m = (i + 1) * P
                dve.wait_ge(s_ready, n + 1)
                dve.wait_ge(cb_copied, h + 1)
                if n >= 4:
                    dve.wait_ge(p_turned, n - 3)
                dve.scalar_tensor_tensor(score(n)[:, 0:m], aux[:, n % 2, 0:m], csum[:, i, h:h + 1],
                                         conv[:, 2 + h % 2, 0:m], ALU.add, ALU.add).then_inc(s_taken, 1)
                dve.wait_ge(s_taken, n + 1)
                step(dve.tensor_reduce(stat[:, 0, n % 4:n % 4 + 1], score(n)[:, 0:m], AX.X, ALU.max))
                dve.tensor_scalar(stat[:, 1, n % 4:n % 4 + 1], stat[:, 0, n % 4:n % 4 + 1], -1.0, None, ALU.mult)\
                   .then_inc(s_max, 1)
                if n >= 2:
                    divide(n - 2)
                if i == 1 and h >= 2:
                    head_out(h - 2)
            divide(HEADS * TB - 2)
            divide(HEADS * TB - 1)
            head_out(HEADS - 2)
            head_out(HEADS - 1)

            for s in range(4):
                slab_ready(dve, attn_out_l, 0, s)
                for t in range(2):
                    k = 2 * s + t
                    dve.tensor_tensor(tmp[:, t, :], lin[:, 2 * (s % 2) + t, :], sig[:, KT + k, :], ALU.mult)\
                       .then_inc(bank_free[s % 2], 1)
                    tile_taken(dve, attn_out_l, 0, s, t)
                    step(dve.tensor_tensor(act_hi[:, k, :], tmp[:, t, :], sig[:, k, :], ALU.add))
                    step(dve.tensor_tensor(tmp[:, t, :], tmp[:, t, :], sig[:, k, :], ALU.add))
                    dve.tensor_tensor(act_lo[:, k, :], tmp[:, t, :], act_hi[:, k, :].bitcast(F32), ALU.subtract)\
                       .then_inc(m_ready, 1)
                    dve.wait_ge(m_ready, k + 1)

            add_to_residual(out_l, 1)
            dve_norm(1, "g_ffn", step)
            with dve.Fori(0, ffn_in_l.bodies) as i:
                step.enter(i, 2)
                for t in range(2):
                    slab_ready(dve, ffn_in_l, i, 1)
                    tile_taken(dve, ffn_in_l, i, 0, t)
                    at = 2 * i + t
                    step(dve.tensor_tensor(hid_hi[:, bass.ds(at, 1), :], lin[:, 2 + t:3 + t, :], ffn_tmp[:, t:t + 1, :],
                                           ALU.mult))
                    dve.tensor_tensor(ffn_tmp[:, 2 + t, :], lin[:, 2 + t, :], ffn_tmp[:, t, :], ALU.mult)\
                       .then_inc(bank_free[1], 1)
                    tile_taken(dve, ffn_in_l, i, 1, t)
                    dve.tensor_tensor(hid_lo[:, bass.ds(at, 1), :], ffn_tmp[:, 2 + t:3 + t, :],
                                      hid_hi[:, bass.ds(at, 1), :].bitcast(F32), ALU.subtract).then_inc(hid_ready, 1)
                    dve.wait_ge(hid_ready, at + 1)
            step.leave(ffn_in_l.bodies)
            add_to_residual(ffn_out_l, 2)
            dve_mix(dve, step)
            dve_mem_squares(dve, step)
            add_to_residual(mix_out_l)
            dve_mem_norm(dve, step)
            dve_rest(dve, step)


def kernel(**inputs):
    import numpy as np
    import concourse.bacc as bacc
    from concourse.bass_utils import run_bass_kernel_spmd

    nc = bacc.Bacc("TRN2", target_bir_lowering=False, num_devices=1)
    arrays, d = {}, {}
    for name, value in inputs.items():
        a = np.ascontiguousarray(value)
        arrays[f"in_{name}_dram"] = a
        d[name] = nc.dram_tensor(f"in_{name}_dram", a.shape, mybir.dt.from_np(a.dtype), kind="ExternalInput").ap()
    out = nc.dram_tensor("out_0_dram", (1, T, D), F32, kind="ExternalOutput").ap()
    build(nc, d, out)
    return run_bass_kernel_spmd(nc, [arrays], core_ids=[0]).results[0]["out_0_dram"]
```
